# Optimizing a Trainium2 kernel written in Bass

```python
import jax, jax.numpy as jnp
from jax import lax
import numpy as np

D_MODEL = 1024
BATCH = 1
SEQ = 512
DEPTH = 1
DEC_BATCH = 1
DEC_SEQ = 512
PAST_LEN = 128

GRID_W = 64
MIX_W = D_MODEL
NA_HEADS = 8
NA_HEAD_DIM = 64
NA_WIN_ROWS = 8
NA_WIN_COLS = 16
NA_QBLOCK_COLS = 16
GDN_HEADS = 4
GDN_DK = 128
GDN_DV = 128
GDN_CONV = 5
GDN_CHUNK = 64
D_FF = 2816
FFN_CONV = 3
LN_EPS = 1e-5
RMS_EPS = 1e-6
DEEPNORM_ALPHA = (2 * DEPTH) ** 0.25
DEEPNORM_BETA = (8 * DEPTH) ** -0.25

NA_WIDTH = NA_HEADS * NA_HEAD_DIM
GDN_QK_WIDTH = GDN_HEADS * GDN_DK
GDN_V_WIDTH = GDN_HEADS * GDN_DV
GDN_CONV_CH = 2 * GDN_QK_WIDTH + GDN_V_WIDTH
IN_SPLITS = (NA_WIDTH, NA_WIDTH, NA_WIDTH, GDN_QK_WIDTH, GDN_QK_WIDTH, GDN_V_WIDTH, GDN_V_WIDTH,
             GDN_HEADS, GDN_HEADS, GDN_HEADS, GDN_HEADS)
IN_COLS = sum(IN_SPLITS)

kernel_name = 'hymba_natten_gdn_encoder'

def _layer_norm(x, g, b):
    xf = x.astype(jnp.float32)
    mu = jnp.mean(xf, -1, keepdims=True)
    var = jnp.mean(jnp.square(xf - mu), -1, keepdims=True)
    y = (xf - mu) * lax.rsqrt(var + LN_EPS) * g.astype(jnp.float32) + b.astype(jnp.float32)
    return y.astype(x.dtype)

def _l2norm(t):
    return t * lax.rsqrt(jnp.sum(t * t, -1, keepdims=True) + RMS_EPS)

def _dwconv_centred(x, w):
    k = w.shape[0]
    pad = k // 2
    s = x.shape[1]
    xp = jnp.pad(x, ((0, 0), (pad, pad), (0, 0)))
    y = xp[:, 0:s] * w[0]
    for j in range(1, k):
        y = y + xp[:, j:j + s] * w[j]
    return y

def _na_col_tables():
    ncb = GRID_W // NA_QBLOCK_COLS
    span = NA_QBLOCK_COLS + NA_WIN_COLS
    kc0 = np.clip(np.arange(ncb) * NA_QBLOCK_COLS - NA_WIN_COLS // 2, 0, GRID_W - span)
    kcols = kc0[:, None] + np.arange(span)
    qcols = np.arange(GRID_W).reshape(ncb, NA_QBLOCK_COLS)
    start = np.clip(qcols - NA_WIN_COLS // 2, 0, GRID_W - NA_WIN_COLS)
    kc = kcols[:, None, :]
    colmask = (kc >= start[..., None]) & (kc < start[..., None] + NA_WIN_COLS)
    dc_idx = np.clip(kc - qcols[..., None] + NA_WIN_COLS - 1, 0, 2 * NA_WIN_COLS - 2)
    return kcols, colmask, dc_idx

def _neighbourhood_attention(q, k, v, rpb):
    b, h, rows, w, hd = q.shape
    wr = min(NA_WIN_ROWS, rows)
    kcols, colmask, dc_idx = _na_col_tables()
    ncb, span = kcols.shape
    bias_c = rpb[:, :, dc_idx].astype(jnp.float32)
    colmask_b = jnp.asarray(colmask)[:, :, None, :]

    def row(r):
        rs = jnp.clip(r - wr // 2, 0, rows - wr)
        qr = lax.dynamic_index_in_dim(q, r, axis=2, keepdims=False).reshape(b, h, ncb, NA_QBLOCK_COLS, hd)
        kr = lax.dynamic_slice_in_dim(k, rs, wr, axis=2)[:, :, :, kcols]
        vr = lax.dynamic_slice_in_dim(v, rs, wr, axis=2)[:, :, :, kcols]
        s = jnp.einsum('bhnqd,bhrnkd->bhnqrk', qr, kr).astype(jnp.float32)
        dr_idx = rs + jnp.arange(wr) - r + (NA_WIN_ROWS - 1)
        bias = jnp.take(bias_c, dr_idx, axis=1).transpose(0, 2, 3, 1, 4)
        s = jnp.where(colmask_b, s + bias, -1e30)
        p = jax.nn.softmax(s.reshape(b, h, ncb, NA_QBLOCK_COLS, wr * span), axis=-1)
        p = p.reshape(s.shape).astype(v.dtype)
        o = jnp.einsum('bhnqrk,bhrnkd->bhnqd', p, vr)
        return o.reshape(b, h, w, hd)

    out = lax.map(row, jnp.arange(rows))
    return out.transpose(1, 0, 3, 2, 4).reshape(b, rows * w, h * hd)

def _gated_delta_chunked(q, k, v, beta, g):
    b, s, h, dk = q.shape
    dv = v.shape[-1]
    c = GDN_CHUNK
    n = s // c
    chunks = lambda t: t.reshape(b, n, c, h, -1).transpose(0, 3, 1, 2, 4)
    q, k, v = chunks(q), chunks(k), chunks(v)
    beta = beta.reshape(b, n, c, h).transpose(0, 3, 1, 2)
    g = g.reshape(b, n, c, h).transpose(0, 3, 1, 2)
    gc = jnp.cumsum(g, axis=-1)
    tril = jnp.asarray(np.tril(np.ones((c, c), dtype=bool)))
    strict = jnp.asarray(np.tril(np.ones((c, c), dtype=bool), -1))
    decay = jnp.exp(jnp.where(tril, gc[..., :, None] - gc[..., None, :], -jnp.inf))
    kb = k * beta[..., None]
    lower = jnp.where(strict, jnp.einsum('bhnid,bhnjd->bhnij', kb, k) * decay, 0.0)
    a = lower + jnp.eye(c, dtype=jnp.float32)
    rhs = jnp.concatenate([v * beta[..., None], kb * jnp.exp(gc)[..., None]], axis=-1)
    sol = lax.linalg.triangular_solve(a, rhs, left_side=True, lower=True, unit_diagonal=True)
    u, wk = sol[..., :dv], sol[..., dv:]
    attn = jnp.einsum('bhnid,bhnjd->bhnij', q, k) * decay
    q_dec = q * jnp.exp(gc)[..., None]
    k_dec = k * jnp.exp(gc[..., -1:] - gc)[..., None]
    chunk_decay = jnp.exp(gc[..., -1])
    xs = tuple(jnp.moveaxis(t, 2, 0) for t in (u, wk, attn, q_dec, k_dec, chunk_decay))

    def step(state, inp):
        u_i, w_i, attn_i, qd_i, kd_i, cd_i = inp
        v_new = u_i - jnp.einsum('bhcd,bhde->bhce', w_i, state)
        o = jnp.einsum('bhcd,bhde->bhce', qd_i, state) + jnp.einsum('bhij,bhje->bhie', attn_i, v_new)
        state = state * cd_i[..., None, None] + jnp.einsum('bhcd,bhce->bhde', kd_i, v_new)
        return state, o

    state0 = jnp.zeros((b, h, dk, dv), jnp.float32)
    _, o = lax.scan(step, state0, xs)
    return o.transpose(1, 0, 3, 2, 4).reshape(b, s, h, dv)

def _layer(x, w_in, na_rpb, gdn_conv_w, gdn_a_log, gdn_dt_bias, gdn_norm_w, w_out,
           ln1_g, ln1_b, ffn_w_up, ffn_conv_w, ffn_conv_b, ffn_w_down, ln2_g, ln2_b):
    b, s, _ = x.shape
    rows = s // GRID_W
    f32 = jnp.float32
    proj = x @ w_in
    na_q, na_k, na_v, g_q, g_k, g_v, g_z, bf, bb, af, ab = jnp.split(
        proj, np.cumsum(IN_SPLITS)[:-1].tolist(), axis=-1)
    grid = lambda t: t.reshape(b, rows, GRID_W, NA_HEADS, NA_HEAD_DIM).transpose(0, 3, 1, 2, 4)
    na_out = _neighbourhood_attention(grid(na_q * NA_HEAD_DIM ** -0.5), grid(na_k), grid(na_v), na_rpb)
    qkv = jax.nn.silu(_dwconv_centred(jnp.concatenate([g_q, g_k, g_v], -1), gdn_conv_w)).astype(f32)
    gq, gk, gv = jnp.split(qkv, [GDN_QK_WIDTH, 2 * GDN_QK_WIDTH], axis=-1)
    heads = lambda t: t.reshape(b, s, GDN_HEADS, -1)
    gq = _l2norm(heads(gq)) * GDN_DK ** -0.5
    gk = _l2norm(heads(gk))
    gv = heads(gv)
    a_log = gdn_a_log.astype(f32)
    dt_bias = gdn_dt_bias.astype(f32)
    beta_f = jax.nn.sigmoid(bf.astype(f32))
    beta_b = jax.nn.sigmoid(bb.astype(f32))
    g_f = -jnp.exp(a_log[0]) * jax.nn.softplus(af.astype(f32) + dt_bias[0])
    g_b = -jnp.exp(a_log[1]) * jax.nn.softplus(ab.astype(f32) + dt_bias[1])
    flip = lambda t: jnp.flip(t, axis=1)
    o_f = _gated_delta_chunked(gq, gk, gv, beta_f, g_f)
    o_b = flip(_gated_delta_chunked(flip(gq), flip(gk), flip(gv), flip(beta_b), flip(g_b)))
    o = o_f + o_b
    o = o * lax.rsqrt(jnp.mean(o * o, -1, keepdims=True) + RMS_EPS) * gdn_norm_w.astype(f32) \
        * jax.nn.silu(heads(g_z).astype(f32))
    gdn_out = o.reshape(b, s, GDN_V_WIDTH).astype(x.dtype)
    mix = jnp.concatenate([na_out, gdn_out], axis=-1) @ w_out
    x = _layer_norm(DEEPNORM_ALPHA * x + mix, ln1_g, ln1_b)
    hdn = _dwconv_centred(x @ ffn_w_up, ffn_conv_w) + ffn_conv_b
    gate, val = jnp.split(hdn, 2, axis=-1)
    ffn = (jax.nn.silu(gate) * val) @ ffn_w_down
    return _layer_norm(DEEPNORM_ALPHA * x + ffn, ln2_g, ln2_b)

def _trunk(x, w_in, na_rpb, gdn_conv_w, gdn_a_log, gdn_dt_bias, gdn_norm_w, w_out,
           ln1_g, ln1_b, ffn_w_up, ffn_conv_w, ffn_conv_b, ffn_w_down, ln2_g, ln2_b):
    for l in range(DEPTH):
        x = _layer(x, w_in[l], na_rpb[l], gdn_conv_w[l], gdn_a_log[l], gdn_dt_bias[l], gdn_norm_w[l],
                   w_out[l], ln1_g[l], ln1_b[l], ffn_w_up[l], ffn_conv_w[l], ffn_conv_b[l],
                   ffn_w_down[l], ln2_g[l], ln2_b[l])
    return x

def setup_inputs(seed: int = 0) -> dict:
    key = jax.random.key(seed)
    ks = jax.random.split(key, 20)
    nrm = lambda k, shp: jax.random.normal(k, shp, jnp.float32)
    x_prompt = nrm(ks[0], (BATCH, SEQ, D_MODEL))
    x_sample = nrm(ks[1], (DEC_BATCH, DEC_SEQ, D_MODEL))
    col_scale = np.ones((IN_COLS,), np.float32)
    offs = np.concatenate([[0], np.cumsum(IN_SPLITS)])
    col_scale[offs[2]:offs[3]] = DEEPNORM_BETA
    col_scale[offs[5]:offs[6]] = DEEPNORM_BETA
    w_in = nrm(ks[2], (DEPTH, D_MODEL, IN_COLS)) * D_MODEL ** -0.5 * jnp.asarray(col_scale)
    na_rpb = 0.02 * nrm(ks[3], (DEPTH, NA_HEADS, 2 * NA_WIN_ROWS - 1, 2 * NA_WIN_COLS - 1))
    gdn_conv_w = nrm(ks[4], (DEPTH, GDN_CONV, GDN_CONV_CH)) * GDN_CONV ** -0.5
    gdn_a_log = jnp.log(jax.random.uniform(ks[5], (DEPTH, 2, GDN_HEADS), jnp.float32, 1.0, 16.0))
    dt = jnp.exp(jax.random.uniform(ks[6], (DEPTH, 2, GDN_HEADS), jnp.float32,
                                    float(np.log(1e-3)), float(np.log(0.1))))
    gdn_dt_bias = dt + jnp.log(-jnp.expm1(-dt))
    gdn_norm_w = 1.0 + 0.02 * nrm(ks[7], (DEPTH, GDN_DV))
    w_out = nrm(ks[8], (DEPTH, MIX_W, D_MODEL)) * MIX_W ** -0.5 * DEEPNORM_BETA
    ln1_g = 1.0 + 0.02 * nrm(ks[9], (DEPTH, D_MODEL))
    ln1_b = 0.02 * nrm(ks[10], (DEPTH, D_MODEL))
    ffn_w_up = nrm(ks[11], (DEPTH, D_MODEL, 2 * D_FF)) * D_MODEL ** -0.5 * DEEPNORM_BETA
    ffn_conv_w = nrm(ks[12], (DEPTH, FFN_CONV, 2 * D_FF)) * FFN_CONV ** -0.5
    ffn_conv_b = 0.02 * nrm(ks[13], (DEPTH, 2 * D_FF))
    ffn_w_down = nrm(ks[14], (DEPTH, D_FF, D_MODEL)) * D_FF ** -0.5 * DEEPNORM_BETA
    ln2_g = 1.0 + 0.02 * nrm(ks[15], (DEPTH, D_MODEL))
    ln2_b = 0.02 * nrm(ks[16], (DEPTH, D_MODEL))
    return {'x_prompt': x_prompt, 'x_sample': x_sample, 'w_in': w_in, 'na_rpb': na_rpb,
            'gdn_conv_w': gdn_conv_w, 'gdn_a_log': gdn_a_log, 'gdn_dt_bias': gdn_dt_bias,
            'gdn_norm_w': gdn_norm_w, 'w_out': w_out, 'ln1_g': ln1_g, 'ln1_b': ln1_b,
            'ffn_w_up': ffn_w_up, 'ffn_conv_w': ffn_conv_w, 'ffn_conv_b': ffn_conv_b,
            'ffn_w_down': ffn_w_down, 'ln2_g': ln2_g, 'ln2_b': ln2_b}

def reference(x_prompt, x_sample, w_in, na_rpb, gdn_conv_w, gdn_a_log, gdn_dt_bias, gdn_norm_w,
              w_out, ln1_g, ln1_b, ffn_w_up, ffn_conv_w, ffn_conv_b, ffn_w_down, ln2_g, ln2_b):
    y_prompt = _trunk(x_prompt, w_in, na_rpb, gdn_conv_w, gdn_a_log, gdn_dt_bias, gdn_norm_w, w_out,
                      ln1_g, ln1_b, ffn_w_up, ffn_conv_w, ffn_conv_b, ffn_w_down, ln2_g, ln2_b)
    y_sample = _trunk(x_sample, w_in, na_rpb, gdn_conv_w, gdn_a_log, gdn_dt_bias, gdn_norm_w, w_out,
                      ln1_g, ln1_b, ffn_w_up, ffn_conv_w, ffn_conv_b, ffn_w_down, ln2_g, ln2_b)
    return (y_prompt, y_sample)


_drawn_inputs = setup_inputs


def setup_inputs(seed=0):
    import zlib

    import numpy as np

    out = dict(_drawn_inputs(seed))
    spreads = {}
    factors = {'na_rpb': 200.0,
     'gdn_norm_w': 24.236,
     'ln1_g': 7.663,
     'ln1_b': 7.915,
     'ffn_conv_b': 8.0,
     'ln2_g': 23.384,
     'ln2_b': 23.371}
    for name, (base, spread) in spreads.items():
        noise = np.random.default_rng([zlib.crc32(name.encode()), seed]).standard_normal(out[name].shape)
        drawn = base * np.exp(spread * noise) if base else spread * noise
        out[name] = __import__('jax').numpy.asarray(drawn.astype(out[name].dtype))
    for name, factor in factors.items():
        out[name] = (out[name] * factor).astype(out[name].dtype)
    return out
```

```python
import numpy as np
import concourse.bass as bass
from concourse import mybir
from concourse.alu_op_type import AluOpType as ALU

F32 = mybir.dt.float32
F32R = mybir.dt.float32r
ACT = mybir.ActivationFunctionType
AX = mybir.AxisListType

P = 128
D = 1024
SEQS, L = 2, 512
T = SEQS * L
KT = D // P
GRID_W, ROWS = 64, L // 64
NA_HEADS, HD = 8, 64
PAIRS = NA_HEADS // 2
WIN_R, WIN_C, QB = 8, 16, 16
SPAN = QB + WIN_C
BLOCKS = GRID_W // QB
KEYS = ROWS * SPAN
DC = 2 * WIN_C - 1
DR = 2 * WIN_R - 1
KC0 = [min(max(b * QB - WIN_C // 2, 0), GRID_W - SPAN) for b in range(BLOCKS)]
SHIFT = [KC0[b] - b * QB for b in range(BLOCKS)]
SHIFTS = sorted(set(SHIFT), reverse=True)
BIAS_RUN = (ROWS - 1) * DC + SPAN - SHIFTS[-1]
PAD = -SHIFTS[-1]
assert PAD == WIN_C
GH = 4
TAPS = 5
CH = L // P
GROUPS = 2 * SEQS
LEVELS = 7
FF = 2816
FJ = FF // P
ALPHA = 2.0 ** 0.25
LN_EPS, RMS_EPS = 1e-5, 1e-6
NEG = -1e30

GATE0 = 0
NAT0 = GATE0 + 1
GDN0 = NAT0 + 3 * PAIRS
OUT0 = GDN0 + 4 * GH
UP0 = OUT0 + KT
DOWN0 = UP0 + 2 * FJ
DPASS = FJ // 2
END = DOWN0 + 2 * DPASS

BETA, NEG_EG, KAPPA, CDECAY, NEG_GC, GLOG = range(6)
HQ = 6 * 2 * SEQS * CH
GDN_STEPS = 27


def encoder_layer(nc, xT, w_gate, w_nat, w_gdn, w_out, w_up, w_down, rpb, gdn_conv, gate_vec, a_log,
                  norm_w, ln_par, ffn_conv, consts, nat_mask, yT):
    from contextlib import ExitStack
    ctx = ExitStack()
    with ctx:
        arena = nc.sbuf_base
        top = nc.sbuf_usable_end
        arena = (arena + 63) // 64 * 64
        used = []

        def place(name, shape, dt, at):
            size = 4
            for n in shape[1:]:
                size *= n
            assert at + size <= top, (name, at + size - top)
            used.append((name, at, size))
            return nc.alloc_sbuf_tensor_at(name, shape, dt, offset=at), at + (size + 31) // 32 * 32

        ln_sb, at = place("ln_sb", [P, 4, KT], F32, arena)
        fw, at = place("fw", [P, 2 * FJ, 4], F32, at)
        one, at = place("one", [P, 1], F32, at)
        fw_j, at = place("fw_j", [P, 2, 4], F32, at)
        mean_w, at = place("mean_w", [P, P], F32, at)
        eps, at = place("eps", [P, 4], F32, at)
        x_hi, at_hi = place("x_hi", [P, KT, T], F32R, at)
        z_all, _ = place("z_all", [P, KT, T], F32, at)
        x_lo, at = place("x_lo", [P, KT, T], F32R, at_hi)
        w_raw, w_hi, w_lo = [], [], []
        for u in range(2):
            t, at = place(f"w_raw{u}", [P, D], F32, at)
            w_raw.append(t)
            t, at = place(f"w_hi{u}", [P, D], F32R, at)
            w_hi.append(t)
            t, at = place(f"w_lo{u}", [P, D], F32R, at)
            w_lo.append(t)
        mix0 = at
        mix, at = place("mix", [P, KT, T], F32, at)
        region = at
        cv, m = place("cv", [P, 4, L], F32, mix0)
        a_hi, a_lo = [], []
        for u in range(2):
            t, m = place(f"a_hi{u}", [P, T], F32R, m)
            a_hi.append(t)
            t, m = place(f"a_lo{u}", [P, T], F32R, m)
            a_lo.append(t)
        act, _ = place("act", [P, FJ, T], F32, m)
        rs2, m = place("rs2", [P, SEQS, L], F32, mix0)
        sq2, m = place("sq2", [P, 2, L], F32, m)

        cst, at = place("cst", [P, consts.shape[1]], F32, region)
        sc, at = place("sc", [P, GH, HQ], F32, at)
        cw_all, at = place("cw_all", [P, 3 * GH, TAPS], F32, at)
        nw, at = place("nw", [P, 1], F32, at)
        mixer = at
        ident = cst[:, 0:P]
        tri = [cst[:, P:2 * P], cst[:, 2 * P:3 * P]]
        ones = cst[:, 3 * P:4 * P]
        negm = [cst[:, 4 * P:5 * P], cst[:, 5 * P:6 * P]]
        turned_round = cst[:, (6 + LEVELS) * P:(7 + LEVELS) * P]
        lmask = [cst[:, (6 + v) * P:(7 + v) * P] for v in range(LEVELS)]

        bm, at = place("bm", [P, len(SHIFTS), NA_HEADS, KEYS], F32, mixer)
        q_nat, at = place("q_nat", [P, SEQS, L], F32, at)
        k_nat, at = place("k_nat", [P, SEQS, L], F32, at)
        v_nat, at = place("v_nat", [P, SEQS, BLOCKS, KEYS], F32, at)
        gT, _ = place("gT", [64, T], F32, at)
        v_tok, at = place("v_tok", [P, SEQS, BLOCKS, 2, P], F32, at)
        s_sb, p_sb, pt_sb, nmax, psum_row, rrow = [], [], [], [], [], []
        for u in range(2):
            for lst, nm, n in ((s_sb, "s_sb", 2 * KEYS), (p_sb, "p_sb", 2 * KEYS),
                               (pt_sb, "pt_sb", 2 * KEYS), (nmax, "nmax", 2),
                               (psum_row, "psum_row", 2), (rrow, "rrow", 2)):
                t, at = place(f"{nm}{u}", [P, n], F32, at)
                lst.append(t)
        bw, at = place("bw", [P, NA_HEADS, BIAS_RUN], F32, at)
        nmask, at = place("nmask", [P, len(SHIFTS), KEYS], F32, at)
        gv, at = place("gv", [P, 1], F32, at)
        al, at = place("al", [P, 8], F32, at)
        NG = SEQS * CH
        ga, at = place("ga", [P, NG, 64], F32, at)
        gt_ = {}
        for nm in ("e1", "ab", "e2", "lp", "beta", "sp", "g", "dif", "kd"):
            gt_[nm], at = place("gs_" + nm, [P, NG, 8], F32, at)
        ea, at = place("ea", [P, 8], F32, at)
        gcs, at = place("gcs", [P, 2 * 8 * NG], F32, at)
        ecs, at = place("ecs", [P, 2 * 8 * NG], F32, at)

        qkv, at = place("qkv", [P, 3, SEQS, L], F32, mixer)
        k_tok, at = place("k_tok", [P, SEQS, L], F32, at)
        vg_tok, at = place("vg_tok", [P, SEQS, L], F32, at)
        att, at = place("att", [P, GROUPS, L], F32, at)
        m_t, at = place("m_t", [P, GROUPS, L], F32, at)
        o_sb = m_t
        u_t, at = place("u_t", [P, GROUPS, L], F32, at)
        d_n, at = place("d_n", [P, GROUPS, L], F32, at)
        x_1, at = place("x_1", [P, GROUPS, L], F32, at)
        q_d, at = place("q_d", [P, GROUPS, L], F32, at)
        dt_, at = place("dt_", [P, 2, L], F32, at)
        egr, at = place("egr", [P, 2, L], F32, at)
        hs, at = place("hs", [P, HQ], F32, at)
        cw, at = place("cw", [P, 3, TAPS], F32, at)
        KX, QX, VX = 0, 1, 2

        m_hi, at = place("m_hi", [P, KT, T], F32R, region + 512 * 0)
        m_lo, at = place("m_lo", [P, KT, T], F32R, at)
        rs1, at = place("rs1", [P, SEQS, L], F32, at)
        sq1, at = place("sq1", [P, 2, L], F32, at)

        banks = ctx.enter_context(nc.psum_tensor("banks", [P, 8, 512], F32))
        ps = [banks[:, b, :] for b in range(8)]

        names = []

        def sem(name):
            names.append(name)
            return ctx.enter_context(nc.semaphore(name))

        x_landed = [sem(f"x_landed{k}") for k in range(KT)]
        cst_landed, gate_landed, bias_landed, al_landed = (sem("cst_landed"), sem("gate_landed"),
                                                           sem("bias_landed"), sem("al_landed"))
        par_landed = sem("par_landed")
        w_landed = [sem("w_landed0"), sem("w_landed1")]
        w_high, w_ready, proj_done = sem("w_high"), sem("w_ready"), sem("proj_done")
        x_high, x_ready = sem("x_high"), sem("x_ready")
        dstep, astep, eps_set = sem("dstep"), sem("astep"), sem("eps_set")
        bm_ready, bias_turned = sem("bm_ready"), sem("bias_turned")
        gate_tr, gate_tok, gate_soft, gate_g, gate_cum, gate_exp, sc_ready, g_e = (
            sem("gate_tr"), sem("gate_tok"), sem("gate_soft"), sem("gate_g"), sem("gate_cum"),
            sem("gate_exp"), sem("sc_ready"), sem("g_e"))
        nat_evac, qk_done, s_biased, s_max, p_exp, p_ready = (
            sem("nat_evac"), sem("qk_done"), sem("s_biased"), sem("s_max"), sem("p_exp"), sem("p_ready"))
        vt_done, v_evac, pt_done, pt_evac, pv_done, o_evac = (
            sem("vt_done"), sem("v_evac"), sem("pt_done"), sem("pt_evac"), sem("pv_done"), sem("o_evac"))
        hs_ready, center, conv_done, silu_done, sq_done, nsum_done, rs_ready, normed = (
            sem("hs_ready"), sem("center"), sem("conv_done"), sem("silu_done"), sem("sq_done"),
            sem("nsum_done"), sem("rs_ready"), sem("normed"))
        ktr_done, k_tok_ready, vtr_done, vg_tok_ready, kk_done, kq_done, gc_done = (
            sem("ktr_done"), sem("k_tok_ready"), sem("vtr_done"), sem("vg_tok_ready"), sem("kk_done"),
            sem("kq_done"), sem("gc_done"))
        dt_ready, dt_exp, egr_ready, u1_ready, m_ready, att_ready, qd_ready, d1_done, d1_evac = (
            sem("dt_ready"), sem("dt_exp"), sem("egr_ready"), sem("u1_ready"), sem("m_ready"),
            sem("att_ready"), sem("qd_ready"), sem("d1_done"), sem("d1_evac"))
        x1_done, x1_evac, yy_done, ud_ready = sem("x1_done"), sem("x1_evac"), sem("yy_done"), sem("ud_ready")
        p1_done, r_ready, p2_done, vn_ready, su_done, s_ready, o_done, o_sum = (
            sem("p1_done"), sem("r_ready"), sem("p2_done"), sem("vn_ready"), sem("su_done"),
            sem("s_ready"), sem("o_done"), sem("o_sum"))
        osq_done, osum_done, ors_ready, z_silu, head_out = (
            sem("osq_done"), sem("osum_done"), sem("ors_ready"), sem("z_silu"), sem("head_out"))
        mix_high, mix_ready, res_read, z_ready = (
            sem("mix_high"), sem("mix_ready"), sem("res_read"), sem("z_ready"))
        mean_done, centred, var_sq, var_done, ln_rs, ln_out, x1_high, x1_ready = (
            sem("mean_done"), sem("centred"), sem("var_sq"), sem("var_done"), sem("ln_rs"),
            sem("ln_out"), sem("x1_high"), sem("x1_ready"))
        fw_copied, one_set = sem("fw_copied"), sem("one_set")
        norm_ln, out_ln, ln1_step, ln2_step = sem("norm_ln"), sem("out_ln"), sem("ln1_step"), sem("ln2_step")
        up_center, up_conv, up_silu, up_act = sem("up_center"), sem("up_conv"), sem("up_silu"), sem("up_act")
        a_high, a_ready, acc_read, z2_ready = sem("a_high"), sem("a_ready"), sem("acc_read"), sem("z2_ready")
        mean2_done, centred2, var2_sq, var2_done, ln2_rs, y_ready, y_stored = (
            sem("mean2_done"), sem("centred2"), sem("var2_sq"), sem("var2_done"), sem("ln2_rs"),
            sem("y_ready"), sem("y_stored"))

        def slot(c):
            return c % 2

        def seq(ap, s):
            return ap[:, s * L:(s + 1) * L]

        def flat(ap):
            return ap.rearrange("p a n -> p (a n)")

        def unit(n):
            return n // BLOCKS, n % BLOCKS

        class Chain:

            def __init__(self, eng, s):
                self.eng, self.s, self.n, self.base = eng, s, 0, 0

            def __call__(self, ins):
                self.n += 1
                ins.then_inc(self.s, 1)
                self.eng.wait_ge(self.s, self.base + self.n)

            def enter(self, i, per, first):
                self.base, self.n, self.first = first + i * per, 0, first
                self.per = per

            def leave(self, times):
                assert self.n == self.per, (self.n, self.per)
                self.base, self.n = self.first + times * self.per, 0

        block = ctx.enter_context(nc.Block())

        @block.sync
        def _(sp):
            def load(src, c, u):
                sp.wait_ge(w_ready, c - 1)
                sp.dma_start(w_raw[u][:, :], src).then_inc(w_landed[u], 16)

            sp.dma_start(w_raw[0][:, :], w_gate).then_inc(w_landed[0], 16)
            sp.dma_start(w_raw[1][:, :], w_nat[0, :, :]).then_inc(w_landed[1], 16)
            load(w_nat[1, :, :], NAT0 + 1, slot(NAT0 + 1))
            load(w_nat[2, :, :], NAT0 + 2, slot(NAT0 + 2))
            load(w_nat[3, :, :], NAT0 + 3, slot(NAT0 + 3))
            for w, c0, done, n in ((w_nat, NAT0, 4, 3 * PAIRS), (w_gdn, GDN0, 0, 4 * GH), (w_out, OUT0, 0, KT),
                                   (w_up, UP0, 0, 2 * FJ), (w_down, DOWN0, 0, 2 * DPASS)):
                with sp.Fori(0, (n - done) // 2) as i:
                    for u in range(2):
                        load(w[bass.ds(2 * i + (done + u), 1), :, :].rearrange("a p n -> (a p) n"),
                             2 * i + (c0 + done + u), slot(c0 + u))
            for s in range(SEQS):
                for k in range(KT):
                    sp.wait_ge(y_ready, s * KT + k + 1)
                    sp.dma_start(yT[k, :, s * L:(s + 1) * L], seq(z_all[:, k, :], s)).then_inc(y_stored, 16)
            sp.wait_ge(y_stored, 16 * SEQS * KT)

        @block.gpsimd
        def _(pool):
            def split(c, u, landed, first=False):
                pool.wait_ge(w_landed[u], landed)
                if not first:
                    pool.wait_ge(proj_done, 2 * c - 2)
                nc.gpsimd.tensor_tensor(w_hi[u][:, :], w_raw[u][:, :], one[:, :].to_broadcast([P, D]),
                                        ALU.mult).then_inc(w_high, 1)
                pool.wait_ge(w_high, c + 1)
                nc.gpsimd.tensor_tensor(w_lo[u][:, :], w_raw[u][:, :], w_hi[u][:, :].bitcast(F32),
                                        ALU.subtract).then_inc(w_ready, 1)

            nc.gpsimd.memset(one[:, :], 1.0).then_inc(one_set, 1)
            pool.wait_ge(one_set, 1)
            split(0, 0, 16, first=True)
            split(1, 1, 16, first=True)
            split(2, 0, 32)
            for c0, n in ((NAT0 + 2, 3 * PAIRS - 2), (GDN0, 4 * GH), (OUT0, KT), (UP0, 2 * FJ), (DOWN0, 2 * DPASS)):
                with pool.Fori(0, n // 2) as i:
                    for u in range(2):
                        split(2 * i + (c0 + u), slot(c0 + u), 16 * i + 16 * ((c0 + u) // 2 + 1))

        @block.tensor
        def _(pe):
            mm = nc.tensor.matmul

            def project(c, bank, u, s, xh=None, xl=None, wait_k=None):
                xh = x_hi if xh is None else xh
                xl = x_lo if xl is None else xl
                n = 0
                for k in range(KT):
                    if wait_k is not None:
                        wait_k(k)
                    for w, x in ((w_hi, xh), (w_hi, xl), (w_lo, xh)):
                        last = mm(ps[bank][:, :], w[u][:, k * P:(k + 1) * P], seq(x[:, k, :], s),
                                  start=n == 0, stop=n == 3 * KT - 1)
                        n += 1
                last.then_inc(proj_done, 1)

            pe.wait_ge(w_ready, 1)
            for s in range(SEQS):
                project(0, s, 0, s, wait_k=(lambda k: pe.wait_ge(x_ready, k + 1)) if s == 0 else None)
            pe.wait_ge(cst_landed, 16)
            pe.wait_ge(nat_evac, 2)
            for t in range(NG):
                last = nc.tensor.transpose(ps[2][:, t * 64:(t + 1) * 64], gT[:, t * P:(t + 1) * P],
                                           ident[0:64, 0:64])
            last.then_inc(gate_tr, 1)
            pe.wait_ge(gate_g, 1)
            for d in range(2):
                mm(ps[3][:, d * 4 * NG:(d + 1) * 4 * NG].rearrange("p (t h) -> p t h", h=4),
                   tri[d], gt_["g"][:, :, 4 * d:4 * d + 4], start=True, stop=True)
            mm(ps[3][:, 8 * NG:16 * NG], ones, flat(gt_["g"][:, :, :]), start=True, stop=True).then_inc(gate_cum, 1)
            pe.wait_ge(gate_exp, 1)
            pe.wait_ge(bias_landed, 16 * (ROWS + 1))
            for hh in range(NA_HEADS):
                if hh >= 4:
                    pe.wait_ge(bm_ready, len(SHIFTS) * (hh - 3))
                mm(ps[4 + hh % 4][:, 0:BIAS_RUN], turned_round, bw[:, hh, :], start=True, stop=True).then_inc(bias_turned, 1)
            pe.wait_ge(bm_ready, len(SHIFTS) * NA_HEADS)

            def nat_pair(i, u2):
                pair = 2 * i + u2
                for j in range(3):
                    c = 3 * pair + (NAT0 + j)
                    pe.wait_ge(w_ready, c + 1)
                    for s in range(SEQS):
                        pe.wait_ge(nat_evac, 6 * pair + (2 * j + s + 1))
                        project(c, s, (NAT0 + 3 * u2 + j) % 2, s)
                        if j == 2 and s == 0:
                            scores(pair, 1)
                    if j == 1:
                        pe.wait_ge(nat_evac, 6 * pair + 6)
                        scores(pair, 0)
                for n in range(4):
                    s, half = n // 2, n % 2
                    pe.wait_ge(nat_evac, 6 * pair + (7 + s))
                    if s == 0:
                        pe.wait_ge(o_evac, 2 * pair + 1)
                    else:
                        pe.wait_ge(v_evac, 4 * pair + (n - 1))
                    for b in (2 * half, 2 * half + 1):
                        for kt in range(2):
                            keys = v_nat[:, s, b, kt * P:(kt + 1) * P]
                            last = nc.tensor.transpose(ps[6 + half][:, ((b % 2) * 2 + kt) * P:((b % 2) * 2 + kt + 1) * P],
                                                       keys, ident)
                    last.then_inc(vt_done, 1)
                turn(pair, 0)
                for n in range(2, 2 + SEQS * BLOCKS):
                    if n < SEQS * BLOCKS:
                        scores(pair, n)
                    if n - 1 < SEQS * BLOCKS:
                        turn(pair, n - 1)
                    values(pair, n - 2)

            def scores(pair, n):
                s, b = unit(n)
                if n:
                    pe.wait_ge(s_biased, 8 * pair + n)
                for h in range(2):
                    keys = k_nat[64 * h:64 * h + 64, s, :].rearrange("p (r c) -> p r c", c=GRID_W)[
                        :, :, KC0[b]:KC0[b] + SPAN]
                    last = mm(ps[2 + h][:, 0:KEYS].rearrange("p (r c) -> p r c", c=SPAN),
                              q_nat[64 * h:64 * h + 64, s, b * P:(b + 1) * P], keys, start=True, stop=True)
                last.then_inc(qk_done, 1)

            def turn(pair, n):
                pe.wait_ge(p_ready, 8 * pair + (n + 1))
                if n >= 2:
                    pe.wait_ge(pt_evac, 8 * pair + (n - 1))
                for j in range(4):
                    last = nc.tensor.transpose(ps[4 + n % 2][:, j * P:(j + 1) * P],
                                               p_sb[n % 2][:, j * P:(j + 1) * P], ident)
                last.then_inc(pt_done, 1)

            def values(pair, n):
                s, b = unit(n)
                pe.wait_ge(pt_evac, 8 * pair + (n + 1))
                if n == 0:
                    pe.wait_ge(v_evac, 4 * pair + 4)
                for h in range(2):
                    for kt in range(2):
                        last = mm(ps[6 + s][64 * h:64 * h + 64, b * P:(b + 1) * P],
                                  v_tok[:, s, b, kt, 64 * h:64 * h + 64],
                                  pt_sb[n % 2][:, (2 * h + kt) * P:(2 * h + kt + 1) * P],
                                  start=kt == 0, stop=kt == 1)
                last.then_inc(pv_done, 1)

            with pe.Fori(0, PAIRS // 2) as i:
                for u2 in range(2):
                    nat_pair(i, u2)

            pe.wait_ge(nat_evac, 2 + 6 * PAIRS)
            pe.wait_ge(o_evac, 2 * PAIRS + 1)

            def tile(ap, c):
                return ap[:, c * P:(c + 1) * P]

            def norm_sum(h, x, s):
                pe.wait_ge(sq_done, 4 * h + (2 * x + s + 1))
                mm(ps[2 + 2 * x + s][:, :], ones, q_d[:, 2 * x + s, :], start=True, stop=True).then_inc(nsum_done, 1)

            with pe.Fori(0, GH) as h:
                c = 4 * h + GDN0
                pe.wait_ge(w_ready, c + 1)
                pe.wait_ge(head_out, 2 * h + 1)
                for s in range(SEQS):
                    project(c, s, slot(GDN0), s)
                pe.wait_ge(w_ready, c + 2)
                pe.wait_ge(conv_done, 6 * h + 1)
                project(c, 0, slot(GDN0 + 1), 0)
                norm_sum(h, KX, 0)
                norm_sum(h, KX, 1)
                pe.wait_ge(conv_done, 6 * h + 2)
                project(c, 1, slot(GDN0 + 1), 1)
                pe.wait_ge(w_ready, c + 3)
                pe.wait_ge(conv_done, 6 * h + 3)
                project(c, 0, slot(GDN0 + 2), 0)
                norm_sum(h, QX, 0)
                norm_sum(h, QX, 1)
                pe.wait_ge(conv_done, 6 * h + 4)
                project(c, 1, slot(GDN0 + 2), 1)
                pe.wait_ge(hs_ready, h + 1)
                for s in range(SEQS):
                    pe.wait_ge(normed, 4 * h + (s + 1))
                    for cc in range(CH):
                        last = nc.tensor.transpose(tile(ps[6 + s], cc), tile(qkv[:, KX, s, :], cc), ident)
                    last.then_inc(ktr_done, 1)
                for s in range(SEQS):
                    for cc in range(CH):
                        kc = tile(qkv[:, KX, s, :], cc)
                        last = mm(tile(ps[2 + s], cc), kc, kc, start=True, stop=True)
                    last.then_inc(kk_done, 1)

                def cumulate(g):
                    s, d = g // 2, g % 2
                    if g < 2:
                        pe.wait_ge(k_tok_ready, 2 * h + (g + 1))
                    else:
                        pe.wait_ge(egr_ready, 4 * h + (g - 1))
                    for cc in range(CH):
                        col = GLOG * 16 + d * 8 + s * CH + cc
                        last = mm(tile(ps[6 + g % 2], cc), hs[:, col:col + 1].to_broadcast([P, P]), tri[d],
                                  start=True, stop=True)
                    last.then_inc(gc_done, 1)

                cumulate(0)
                cumulate(1)
                for s in range(SEQS):
                    pe.wait_ge(normed, 4 * h + (2 + s + 1))
                    for cc in range(CH):
                        last = mm(tile(ps[4 + s], cc), tile(qkv[:, KX, s, :], cc), tile(qkv[:, QX, s, :], cc),
                                  start=True, stop=True)
                    last.then_inc(kq_done, 1)
                for s in range(SEQS):
                    pe.wait_ge(silu_done, 6 * h + (4 + s + 1))
                    for cc in range(CH):
                        last = nc.tensor.transpose(tile(ps[s], cc), tile(qkv[:, VX, s, :], cc), ident)
                    last.then_inc(vtr_done, 1)
                cumulate(2)
                cumulate(3)
                for g in range(GROUPS):
                    pe.wait_ge(u1_ready, 4 * h + (g + 1))
                    if g < 2:
                        pe.wait_ge(vg_tok_ready, 2 * h + (g + 1))
                    else:
                        pe.wait_ge(d1_evac, 4 * h + (g - 1))
                    for cc in range(CH):
                        last = nc.tensor.transpose(tile(ps[g % 2], cc), tile(u_t[:, g, :], cc), ident)
                    last.then_inc(d1_done, 1)
                NL = LEVELS - 1
                for lv in range(NL):
                    for g in range(GROUPS):
                        if lv == 0:
                            pe.wait_ge(d1_evac, 4 * h + GROUPS if g == 0 else 4 * h + (g + 1))
                            if g == 1:
                                pe.wait_ge(m_ready, 4 * h + 4)
                            if g == 2:
                                pe.wait_ge(att_ready, 4 * h + 4)
                            if g == 3:
                                pe.wait_ge(egr_ready, 4 * h + 4)
                        else:
                            pe.wait_ge(ud_ready, 4 * NL * h + (4 * (lv - 1) + g + 1))
                        for cc in range(CH):
                            last = mm(tile(ps[2 * g], cc), tile(m_t[:, g, :], cc), tile(d_n[:, g, :], cc),
                                      start=True, stop=True)
                        last.then_inc(x1_done, 1)
                    for g in range(GROUPS):
                        pe.wait_ge(x1_evac, 4 * NL * h + (4 * lv + g + 1))
                        if lv < NL - 1:
                            for cc in range(CH):
                                mm(tile(ps[2 * g], cc), tile(u_t[:, g, :], cc), tile(x_1[:, g, :], cc),
                                   start=True, stop=True)
                        for cc in range(CH):
                            last = mm(tile(ps[2 * g + 1], cc), tile(x_1[:, g, :], cc), tile(u_t[:, g, :], cc),
                                      start=True, stop=True)
                        last.then_inc(yy_done, 1)
                for k in range(CH):
                    def at_chunk(g):
                        return k if g % 2 == 0 else CH - 1 - k
                    if k:
                        for g in range(GROUPS):
                            pe.wait_ge(s_ready, 12 * h + (4 * (k - 1) + g + 1))
                            mm(ps[2 * g][:, 0:P], tile(qkv[:, KX, g // 2, :], at_chunk(g)), d_n[:, g, 0:P],
                               start=True, stop=True).then_inc(p1_done, 1)
                    for g in range(GROUPS):
                        if k:
                            pe.wait_ge(r_ready, 12 * h + (4 * (k - 1) + g + 1))
                            rhs = x_1[:, g, 0:P]
                        else:
                            pe.wait_ge(ud_ready, 4 * NL * h + (4 * (NL - 1) + g + 1))
                            rhs = tile(vg_tok[:, g // 2, :], at_chunk(g))
                        mm(ps[2 * g][:, P:2 * P], tile(u_t[:, g, :], at_chunk(g)), rhs,
                           start=True, stop=True).then_inc(p2_done, 1)
                    for g in range(GROUPS):
                        cc = at_chunk(g)
                        if k == 0:
                            pe.wait_ge(qd_ready, 4 * h + (g + 1))
                        pe.wait_ge(vn_ready, 16 * h + (4 * k + g + 1))
                        if k:
                            mm(tile(ps[2 * g + 1], cc), d_n[:, g, 0:P], tile(q_d[:, g, :], cc), start=True, stop=False)
                        last = mm(tile(ps[2 * g + 1], cc), x_1[:, g, P:2 * P], tile(att[:, g, :], cc),
                                  start=k == 0, stop=True)
                        if k < CH - 1:
                            mm(ps[2 * g][:, 2 * P:3 * P], tile(k_tok[:, g // 2, :], cc), x_1[:, g, 2 * P:3 * P],
                               start=True, stop=True).then_inc(su_done, 1)
                        else:
                            last.then_inc(o_done, 1)
                pe.wait_ge(w_ready, c + 4)
                project(c, 0, slot(GDN0 + 3), 0)
                for s in range(SEQS):
                    pe.wait_ge(osq_done, 2 * h + (s + 1))
                    mm(ps[2 + s][:, :], ones, q_d[:, s, :], start=True, stop=True).then_inc(osum_done, 1)
                project(c, 1, slot(GDN0 + 3), 1)

            pe.wait_ge(head_out, 2 * GH + 1)
            with pe.Fori(0, KT // 2) as i:
                for u in range(2):
                    c = 2 * i + (OUT0 + u)
                    pe.wait_ge(w_ready, c + 1)
                    for s in range(SEQS):
                        if u:
                            pe.wait_ge(res_read, 4 * i + (s + 2))
                        elif s == 0:
                            pe.wait_ge(res_read, 4 * i + 1)
                        project(c, s, slot(OUT0 + u), s, m_hi, m_lo,
                                (lambda k: pe.wait_ge(mix_ready, k + 1)) if s == 0 else None)

            def norm_means(z, centred_s, mean_s, sq, sq_s, var_s, ready, b0):
                for s in range(SEQS):
                    ready(s)
                    for k in range(KT):
                        last = mm(ps[b0 + s][:, :], mean_w[:, :], seq(z[:, k, :], s), start=k == 0, stop=k == KT - 1)
                    last.then_inc(mean_s, 1)
                for s in range(SEQS):
                    for k in range(KT):
                        n = s * KT + k
                        pe.wait_ge(sq_s, n + 1)
                        last = mm(ps[b0 + 2 + s][:, :], mean_w[:, :], sq[:, n % 2, :], start=k == 0, stop=k == KT - 1)
                        last.then_inc(var_s, 1)

            norm_means(mix, centred, mean_done, sq1, var_sq, var_done,
                       lambda s: pe.wait_ge(z_ready, 2 * KT - 1 + s), 2)

            def up(j, first):
                for x in range(2):
                    c = 2 * j + (UP0 + x)
                    pe.wait_ge(w_ready, c + 1)
                    for s in range(SEQS):
                        b = 2 * x + s
                        if not first:
                            pe.wait_ge(up_conv, 4 * j + (b - 3))
                        elif b == 2:
                            pe.wait_ge(ln_out, SEQS * KT)
                        project(c, b, slot(UP0 + x), s,
                                wait_k=(lambda k, s=s: pe.wait_ge(x1_ready, s * KT + k + 1)) if first and x == 0 else None)

            up(0, True)
            with pe.Fori(1, FJ) as j:
                up(j, False)

            def down(q, cc, c, u, first=False, last=False):
                pe.wait_ge(w_ready, c + 1)
                for t in range(2):
                    pe.wait_ge(a_ready, 2 * cc + (q * FJ + t + 1))
                    for m in range(4):
                        for s in range(SEQS):
                            if first and t == 0 and q:
                                pe.wait_ge(acc_read, 2 * m + s + 1)
                            for n, (w, a) in enumerate(((w_hi, a_hi), (w_hi, a_lo), (w_lo, a_hi))):
                                ins = mm(ps[2 * m + s][:, :], w[u][:, t * 512 + m * P:t * 512 + (m + 1) * P],
                                         seq(a[t], s), start=first and t == 0 and n == 0,
                                         stop=last and t == 1 and n == 2)
                    ins.then_inc(proj_done, 1)

            pe.wait_ge(up_conv, 4 * FJ)
            for q in range(2):
                c0 = DOWN0 + q * DPASS
                down(q, 0, c0, slot(c0), first=True)
                with pe.Fori(0, (DPASS - 3) // 2) as i:
                    for u in range(2):
                        down(q, 2 * i + (1 + u), 2 * i + (c0 + 1 + u), slot(c0 + 1 + u))
                down(q, DPASS - 2, c0 + DPASS - 2, slot(c0 + DPASS - 2))
                down(q, DPASS - 1, c0 + DPASS - 1, slot(c0 + DPASS - 1), last=True)

            def ready2(s):
                pe.wait_ge(z2_ready, 2 * KT)

            norm_means(z_all, centred2, mean2_done, sq2, var2_sq, var2_done, ready2, 0)

        @block.scalar
        def _(act_e):
            A = nc.scalar.activation
            for k in range(KT):
                act_e.dma_start(mix[:, k, :], xT[k, :, :]).then_inc(x_landed[k], 16)
                if k == 1:
                    act_e.dma_start(cst[:, :], consts).then_inc(cst_landed, 16)
                    act_e.dma_start(gv[:, :], gate_vec).then_inc(gate_landed, 16)
            act_e.dma_start(al[:, :], bass.AP(a_log.tensor, 0, [[0, P], [1, 8]])
                            ).then_inc(al_landed, 16)
            for r in range(ROWS):
                src = bass.AP(rpb.tensor, r * DC, [[1, QB], [DR * DC, NA_HEADS], [1, BIAS_RUN]])
                act_e.dma_start(bw[r * QB:(r + 1) * QB, :, :], src).then_inc(bias_landed, 16)
            act_e.dma_start(nmask[:, :, :], nat_mask).then_inc(bias_landed, 16)
            act_e.dma_start(cw_all[:, :, :], gdn_conv).then_inc(par_landed, 16)
            act_e.dma_start(nw[:, :], norm_w).then_inc(par_landed, 16)
            act_e.dma_start(ln_sb[:, :, :], ln_par).then_inc(par_landed, 16)
            act_e.dma_start(fw[:, :, :], ffn_conv).then_inc(par_landed, 16)
            for k in range(KT):
                act_e.wait_ge(x_landed[k], 16)
                nc.scalar.copy(x_hi[:, k, :], mix[:, k, :]).then_inc(x_high, 1)
            act_e.wait_ge(gate_landed, 16)
            for s in range(SEQS):
                act_e.wait_ge(proj_done, s + 1)
                A(seq(gT, s), ps[s][0:64, :], ACT.Identity, bias=gv[0:64, 0:1]).then_inc(nat_evac, 1)
            act_e.wait_ge(gate_tr, 1)
            nc.scalar.copy(flat(ga[:, :, :]), ps[2][:, :]).then_inc(gate_tok, 1)
            act_e.wait_ge(gate_tok, 1)
            step = Chain(act_e, astep)
            step(A(gt_["e1"][:, :, :], ga[:, :, 0:8], ACT.Exp, scale=-1.0))
            step(A(gt_["ab"][:, :, :], ga[:, :, 32:40], ACT.Abs))
            act_e.wait_ge(al_landed, 16)
            step(A(ea[:, :], al[:, :], ACT.Exp))
            step(A(gt_["e2"][:, :, :], gt_["ab"][:, :, :], ACT.Exp, scale=-1.0))
            act_e.wait_ge(eps_set, 4)
            A(gt_["lp"][:, :, :], gt_["e2"][:, :, :], ACT.Ln, bias=eps[:, 3:4]).then_inc(gate_soft, 1)
            act_e.wait_ge(gate_cum, 1)
            step(nc.scalar.copy(gcs[:, :], ps[3][:, 0:16 * NG]))
            A(ecs[:, :], gcs[:, :], ACT.Exp).then_inc(gate_exp, 1)
            act_e.wait_ge(g_e, 1)
            A(gt_["kd"][:, :, :], gt_["dif"][:, :, :], ACT.Exp).then_inc(gate_exp, 1)

            def exps(pair, n):
                act_e.wait_ge(s_max, 8 * pair + (n + 1))
                if n >= 2:
                    act_e.wait_ge(pt_done, 8 * pair + (n - 1))
                for h in range(2):
                    ins = A(p_sb[n % 2][:, h * KEYS:(h + 1) * KEYS], s_sb[n % 2][:, h * KEYS:(h + 1) * KEYS], ACT.Exp,
                            bias=nmax[n % 2][:, h:h + 1], accum_out=psum_row[n % 2][:, h:h + 1])
                ins.then_inc(p_exp, 1)

            def turned(pair, n):
                act_e.wait_ge(pt_done, 8 * pair + (n + 1))
                if n >= 2:
                    act_e.wait_ge(pv_done, 8 * pair + (n - 1))
                nc.scalar.copy(pt_sb[n % 2][:, :], ps[4 + n % 2][:, :]).then_inc(pt_evac, 1)

            def nat_pair(i, u2):
                pair = 2 * i + u2
                for j in range(3):
                    for s in range(SEQS):
                        act_e.wait_ge(proj_done, 6 * pair + (2 * (NAT0 + j) + s + 1))
                        if j == 0:
                            out = q_nat[:, s, :].rearrange("p (b r c) -> p r b c", b=BLOCKS, r=ROWS)
                            A(out, ps[s][:, :].rearrange("p (r b c) -> p r b c", r=ROWS, b=BLOCKS), ACT.Copy,
                              scale=HD ** -0.5).then_inc(nat_evac, 1)
                        elif j == 1:
                            nc.scalar.copy(k_nat[:, s, :], ps[s][:, :]).then_inc(nat_evac, 1)
                        else:
                            for b, d in ((0, 3), (1, 1)):
                                src = bass.AP(ps[s].tensor, s * 512 + KC0[b],
                                              [[8 * 512, P], [KC0[b + d] - KC0[b], 2], [GRID_W, ROWS], [1, SPAN]])
                                ins = nc.scalar.copy(v_nat[:, s, b:b + d + 1:d, :].rearrange(
                                    "p b (r c) -> p b r c", c=SPAN), src)
                            ins.then_inc(nat_evac, 1)
                    if j == 1:
                        exps(pair, 0)
                        exps(pair, 1)
                for n in range(4):
                    s, half = n // 2, n % 2
                    act_e.wait_ge(vt_done, 4 * pair + (n + 1))
                    nc.scalar.copy(v_tok[:, s, 2 * half:2 * half + 2, :, :].rearrange("p b k n -> p (b k n)"),
                                   ps[6 + half][:, :]).then_inc(v_evac, 1)
                turned(pair, 0)
                for n in range(2, 1 + SEQS * BLOCKS):
                    if n < SEQS * BLOCKS:
                        exps(pair, n)
                    turned(pair, n - 1)

            with act_e.Fori(0, PAIRS // 2) as i:
                for u2 in range(2):
                    nat_pair(i, u2)

            act_e.wait_ge(o_evac, 2 * PAIRS + 1)
            with act_e.Fori(0, GH) as h:
                def centre(x, s):
                    act_e.wait_ge(proj_done, 8 * h + (2 * (GDN0 + x) + s + 1))
                    A(qkv[:, x, s, :], ps[s][:, :], ACT.Identity,
                      scale=cw[:, x, TAPS // 2:TAPS // 2 + 1]).then_inc(center, 1)

                def silu(x, s):
                    act_e.wait_ge(conv_done, 6 * h + (2 * x + s + 1))
                    A(qkv[:, x, s, :], qkv[:, x, s, :], ACT.Silu).then_inc(silu_done, 1)
                    if x < 2:
                        act_e.wait_ge(silu_done, 6 * h + (2 * x + s + 1))
                        A(q_d[:, 2 * x + s, :], qkv[:, x, s, :], ACT.Square).then_inc(sq_done, 1)

                def inverse_roots(x):
                    for s in range(SEQS):
                        act_e.wait_ge(nsum_done, 4 * h + (2 * x + s + 1))
                        A(x_1[:, 2 * x + s, :], ps[2 + 2 * x + s][:, :], ACT.Ln, scale=1.0 if x == KX else float(P),
                          bias=eps[:, x:x + 1]).then_inc(norm_ln, 1)
                    act_e.wait_ge(norm_ln, 4 * h + (2 * x + 2))
                    for s in range(SEQS):
                        A(x_1[:, 2 * x + s, :], x_1[:, 2 * x + s, :], ACT.Exp, scale=-0.5).then_inc(rs_ready, 1)

                act_e.wait_ge(hs_ready, h + 1)
                centre(KX, 0)
                centre(KX, 1)
                silu(KX, 0)
                silu(KX, 1)
                centre(QX, 0)
                inverse_roots(KX)
                centre(QX, 1)
                silu(QX, 0)
                silu(QX, 1)
                centre(VX, 0)
                inverse_roots(QX)
                centre(VX, 1)
                silu(VX, 0)
                silu(VX, 1)
                for s in range(SEQS):
                    act_e.wait_ge(ktr_done, 2 * h + (s + 1))
                    nc.scalar.copy(k_tok[:, s, :], ps[6 + s][:, :]).then_inc(k_tok_ready, 1)

                def decays(g):
                    act_e.wait_ge(dt_ready, 4 * h + (g + 1))
                    A(dt_[:, g % 2, :], dt_[:, g % 2, :], ACT.Exp).then_inc(dt_exp, 1)
                    if g >= 2:
                        act_e.wait_ge(qd_ready, 4 * h + (g - 1))
                    A(egr[:, g % 2, :], ps[6 + g % 2][:, :], ACT.Exp).then_inc(egr_ready, 1)

                decays(0)
                decays(1)
                for s in range(SEQS):
                    act_e.wait_ge(vtr_done, 2 * h + (s + 1))
                    nc.scalar.copy(vg_tok[:, s, :], ps[s][:, :]).then_inc(vg_tok_ready, 1)
                for g in range(GROUPS):
                    act_e.wait_ge(d1_done, 4 * h + (g + 1))
                    nc.scalar.copy(d_n[:, g, :], ps[g % 2][:, :]).then_inc(d1_evac, 1)
                    if g < 2:
                        decays(2 + g)
                for k in range(CH):
                    for g in range(GROUPS):
                        s, d = g // 2, g % 2
                        cc = k if d == 0 else CH - 1 - k
                        col = d * 8 + s * CH + cc
                        act_e.wait_ge(p2_done, 16 * h + (4 * k + g + 1))
                        A(x_1[:, g, P:2 * P], ps[2 * g][:, P:2 * P], ACT.Identity,
                          scale=hs[:, BETA * 16 + col:BETA * 16 + col + 1])
                        A(x_1[:, g, 2 * P:3 * P], ps[2 * g][:, P:2 * P], ACT.Identity,
                          scale=hs[:, KAPPA * 16 + col:KAPPA * 16 + col + 1]).then_inc(vn_ready, 1)
                for s in range(SEQS):
                    act_e.wait_ge(o_sum, 2 * h + (s + 1))
                    A(q_d[:, s, :], o_sb[:, s, :], ACT.Square).then_inc(osq_done, 1)
                for s in range(SEQS):
                    act_e.wait_ge(osum_done, 2 * h + (s + 1))
                    A(x_1[:, s, :], ps[2 + s][:, :], ACT.Ln, scale=1.0 / P, bias=eps[:, 0:1]).then_inc(out_ln, 1)
                act_e.wait_ge(out_ln, 2 * h + 2)
                for s in range(SEQS):
                    A(x_1[:, s, :], x_1[:, s, :], ACT.Exp, scale=-0.5).then_inc(ors_ready, 1)
                for s in range(SEQS):
                    act_e.wait_ge(proj_done, 8 * h + (2 * (GDN0 + 3) + s + 1))
                    A(qkv[:, VX, s, :], ps[s][:, :], ACT.Silu).then_inc(z_silu, 1)

            act_e.wait_ge(head_out, 2 * GH + 1)
            for k in range(KT):
                nc.scalar.copy(m_hi[:, k, :], mix[:, k, :]).then_inc(mix_high, 1)

            def norm_act(z, rs, sq, centred_s, sq_s, var_s, rs_s, b0, lnstep):
                for s in range(SEQS):
                    for k in range(KT):
                        n = s * KT + k
                        act_e.wait_ge(centred_s, n + 1)
                        if n >= 2:
                            act_e.wait_ge(var_s, n - 1)
                        A(sq[:, n % 2, :], seq(z[:, k, :], s), ACT.Square).then_inc(sq_s, 1)
                    act_e.wait_ge(var_s, (s + 1) * KT)
                    A(rs[:, s, :], ps[b0 + 2 + s][:, :], ACT.Ln, bias=eps[:, 2:3]).then_inc(lnstep, 1)
                    act_e.wait_ge(lnstep, s + 1)
                    A(rs[:, s, :], rs[:, s, :], ACT.Exp, scale=-0.5).then_inc(rs_s, 1)

            norm_act(mix, rs1, sq1, centred, var_sq, var_done, ln_rs, 2, ln1_step)
            for s in range(SEQS):
                for k in range(KT):
                    act_e.wait_ge(ln_out, s * KT + k + 1)
                    nc.scalar.copy(seq(x_hi[:, k, :], s), seq(mix[:, k, :], s)).then_inc(x1_high, 1)
            act_e.wait_ge(x1_ready, SEQS * KT)

            def up(j, first):
                def centre(x, s):
                    b = 2 * x + s
                    act_e.wait_ge(proj_done, 4 * j + (2 * (UP0 + x) + s + 1))
                    if not first:
                        act_e.wait_ge(up_act, 2 * j + (s - 1))
                    A(cv[:, b, :], ps[b][:, :], ACT.Identity,
                      scale=fw_j[:, x, 1:2], bias=fw_j[:, x, 3:4]).then_inc(up_center, 1)
                nc.scalar.copy(fw_j[:, :, :], fw[:, bass.ds(2 * j, 2), :]).then_inc(fw_copied, 1)
                act_e.wait_ge(fw_copied, j + 1)
                centre(0, 0)
                centre(0, 1)
                for s in range(SEQS):
                    act_e.wait_ge(up_conv, 4 * j + (s + 1))
                    A(cv[:, s, :], cv[:, s, :], ACT.Silu).then_inc(up_silu, 1)
                centre(1, 0)
                centre(1, 1)
                act_e.wait_ge(up_center, 4 * j + 4)

            act_e.wait_ge(par_landed, 64)
            up(0, True)
            with act_e.Fori(1, FJ) as j:
                up(j, False)

            def high(j, jj, u):
                act_e.wait_ge(up_act, 2 * FJ)
                act_e.wait_ge(proj_done, j + (2 * DOWN0 - 1))
                nc.scalar.copy(a_hi[u][:, :], act[:, bass.ds(jj, 1), :].rearrange("p a n -> p (a n)")).then_inc(a_high, 1)

            for q in range(2):
                with act_e.Fori(0, FJ // 2) as i:
                    for u in range(2):
                        high(2 * i + (q * FJ + u), 2 * i + u, u)
            norm_act(z_all, rs2, sq2, centred2, var2_sq, var2_done, ln2_rs, 0, ln2_step)

        @block.vector
        def _(dve):
            TT, TS, STT = nc.vector.tensor_tensor, nc.vector.tensor_scalar, nc.vector.scalar_tensor_tensor
            nc.vector.memset(eps[:, 0:1], RMS_EPS).then_inc(eps_set, 1)
            nc.vector.memset(eps[:, 1:2], P * RMS_EPS).then_inc(eps_set, 1)
            nc.vector.memset(eps[:, 2:3], LN_EPS).then_inc(eps_set, 1)
            nc.vector.memset(eps[:, 3:4], 1.0).then_inc(eps_set, 1)
            for counter in (o_evac, head_out, res_read):
                dve.sem_inc(counter, 1)
            step = Chain(dve, dstep)
            step(nc.vector.memset(mean_w[:, :], 1.0 / D))
            for k in range(KT):
                dve.wait_ge(x_high, k + 1)
                TT(x_lo[:, k, :], mix[:, k, :], x_hi[:, k, :].bitcast(F32), ALU.subtract).then_inc(x_ready, 1)
            dve.wait_ge(gate_soft, 1)
            step(nc.vector.tensor_scalar_add(gt_["beta"][:, :, :], gt_["e1"][:, :, :], 1.0))
            step(nc.vector.reciprocal(gt_["beta"][:, :, :], gt_["beta"][:, :, :]))
            step(STT(gt_["sp"][:, :, :], ga[:, :, 32:40], 0.0, gt_["lp"][:, :, :], ALU.max, ALU.add))
            STT(gt_["g"][:, :, :], gt_["sp"][:, :, :], -1.0, ea[:, :].unsqueeze(1).to_broadcast([P, NG, 8]),
                ALU.mult, ALU.mult).then_inc(gate_g, 1)
            dve.wait_ge(gate_exp, 1)
            tot = gcs[:, 8 * NG:16 * NG].rearrange("p (t d h) -> p t d h", d=2, h=4)
            etot = ecs[:, 8 * NG:16 * NG].rearrange("p (t d h) -> p t d h", d=2, h=4)
            for d in range(2):
                gc = gcs[:, d * 4 * NG:(d + 1) * 4 * NG].rearrange("p (t h) -> p t h", h=4)
                ins = TT(gt_["dif"][:, :, 4 * d:4 * d + 4], tot[:, :, d, :], gc, ALU.subtract)
            ins.then_inc(g_e, 1)
            dve.wait_ge(gate_exp, 2)
            for d in range(2):
                hd = slice(4 * d, 4 * d + 4)
                gc = gcs[:, d * 4 * NG:(d + 1) * 4 * NG].rearrange("p (t h) -> p t h", h=4)
                eg = ecs[:, d * 4 * NG:(d + 1) * 4 * NG].rearrange("p (t h) -> p t h", h=4)

                def out(q):
                    return sc[:, :, q * 16 + d * 8:q * 16 + d * 8 + 8].rearrange("p h t -> p t h")
                nc.vector.tensor_copy(out(BETA), gt_["beta"][:, :, hd]).then_inc(sc_ready, 1)
                nc.vector.tensor_scalar_mul(out(NEG_EG), eg, -1.0).then_inc(sc_ready, 1)
                TT(out(KAPPA), gt_["kd"][:, :, hd], gt_["beta"][:, :, hd], ALU.mult).then_inc(sc_ready, 1)
                nc.vector.tensor_copy(out(CDECAY), etot[:, :, d, :]).then_inc(sc_ready, 1)
                nc.vector.tensor_scalar_mul(out(NEG_GC), gc, -1.0).then_inc(sc_ready, 1)
                nc.vector.tensor_copy(out(GLOG), gt_["g"][:, :, hd]).then_inc(sc_ready, 1)
            dve.wait_ge(sc_ready, 12)
            dve.wait_ge(bias_landed, 16 * (ROWS + 1))
            for hh in range(NA_HEADS):
                dve.wait_ge(bias_turned, hh + 1)
                for t, sh in enumerate(SHIFTS):
                    win = bass.AP(ps[0].tensor, (4 + hh % 4) * 512 + sh - SHIFTS[-1], [[8 * 512, P], [DC, ROWS], [1, SPAN]])
                    TT(bm[:, t, hh, :].rearrange("p (r c) -> p r c", c=SPAN), win,
                       nmask[:, t, :].rearrange("p (r c) -> p r c", c=SPAN), ALU.add).then_inc(bm_ready, 1)

            def biased(pair, n):
                s, b = unit(n)
                dve.wait_ge(qk_done, 8 * pair + (n + 1))
                if n >= 2:
                    dve.wait_ge(p_exp, 8 * pair + (n - 1))
                TT(s_sb[n % 2][:, :].rearrange("p (h n) -> p h n", h=2), banks[:, 2:4, 0:KEYS],
                   bm[:, SHIFTS.index(SHIFT[b]), bass.ds(2 * pair, 2), :], ALU.add).then_inc(s_biased, 1)
                dve.wait_ge(s_biased, 8 * pair + (n + 1))
                nc.vector.tensor_reduce(nmax[n % 2][:, :], s_sb[n % 2][:, :].rearrange("p (h n) -> p h n", h=2),
                                        AX.X, ALU.max, negate=True).then_inc(s_max, 1)

            def normalised(pair, n):
                dve.wait_ge(p_exp, 8 * pair + (n + 1))
                step(nc.vector.reciprocal(rrow[n % 2][:, :], psum_row[n % 2][:, :]))
                for h in range(2):
                    pr = p_sb[n % 2][:, h * KEYS:(h + 1) * KEYS]
                    ins = nc.vector.tensor_scalar_mul(pr, pr, rrow[n % 2][:, h:h + 1])
                ins.then_inc(p_ready, 1)

            def attended(pair, s):
                dve.wait_ge(pv_done, 8 * pair + 4 * (s + 1))
                nc.vector.tensor_copy(
                    mix[:, bass.ds(pair, 1), s * L:(s + 1) * L].rearrange("p a (r b c) -> p (a r) b c", r=ROWS, b=BLOCKS),
                    ps[6 + s][:, :].rearrange("p (b r c) -> p r b c", b=BLOCKS, r=ROWS)).then_inc(o_evac, 1)

            base = step.n
            dve.wait_ge(bm_ready, 3 * NA_HEADS)
            with dve.Fori(0, PAIRS // 2) as i:
                step.enter(i, 16, base)
                for u2 in range(2):
                    pair = 2 * i + u2
                    biased(pair, 0)
                    biased(pair, 1)
                    normalised(pair, 0)
                    for n in range(2, SEQS * BLOCKS):
                        biased(pair, n)
                        normalised(pair, n - 1)
                        if n == 6:
                            attended(pair, 0)
                    normalised(pair, SEQS * BLOCKS - 1)
                    attended(pair, 1)
            step.leave(PAIRS // 2)

            def tile(ap, c):
                return ap[:, c * P:(c + 1) * P]

            base = step.base
            dve.wait_ge(par_landed, 64)
            dve.wait_ge(o_evac, 2 * PAIRS + 1)
            with dve.Fori(0, GH) as h:
                step.enter(h, GDN_STEPS, base)
                step(nc.vector.tensor_copy(hs[:, :], sc[:, bass.ds(h, 1), :].rearrange("p a n -> p (a n)")))
                nc.vector.tensor_copy(cw[:, :, :], cw_all[:, bass.ds(3 * h, 3), :]).then_inc(hs_ready, 1)
                dve.wait_ge(hs_ready, h + 1)

                def convolve(x, s):
                    dve.wait_ge(center, 6 * h + (2 * x + s + 1))
                    dst, src = qkv[:, x, s, :], ps[s]
                    for n, tap in enumerate((0, 1, 3, 4)):
                        o = tap - TAPS // 2
                        a, b = max(0, -o), L - max(0, o)
                        ins = STT(dst[:, a:b], src[:, a + o:b + o], cw[:, x, tap:tap + 1], dst[:, a:b],
                                  ALU.mult, ALU.add)
                        if n < 3:
                            step(ins)
                    ins.then_inc(conv_done, 1)

                def normed_x(x):
                    for s in range(SEQS):
                        dve.wait_ge(rs_ready, 4 * h + (2 * x + s + 1))
                        TT(qkv[:, x, s, :], qkv[:, x, s, :], x_1[:, 2 * x + s, :], ALU.mult).then_inc(normed, 1)

                convolve(KX, 0)
                convolve(KX, 1)
                convolve(QX, 0)
                normed_x(KX)
                convolve(QX, 1)
                convolve(VX, 0)
                normed_x(QX)
                convolve(VX, 1)

                def log_decays(g):
                    s, d = g // 2, g % 2
                    dve.wait_ge(gc_done, 4 * h + (g + 1))
                    if g >= 2:
                        dve.wait_ge(att_ready, 4 * h + (g - 1))
                    for cc in range(CH):
                        col = NEG_GC * 16 + d * 8 + s * CH + cc
                        ins = STT(tile(dt_[:, g % 2, :], cc), tile(ps[6 + g % 2], cc), hs[:, col:col + 1], negm[d],
                                  ALU.add, ALU.add)
                    ins.then_inc(dt_ready, 1)

                def bcast(ap):
                    return ap.unsqueeze(1).to_broadcast([P, CH, P])

                def chunks(ap):
                    return ap.rearrange("p (c n) -> p c n", c=CH)

                def inverse_start(g):
                    s, d = g // 2, g % 2
                    dve.wait_ge(dt_exp, 4 * h + (g + 1))
                    dve.wait_ge(kk_done, 2 * h + (s + 1))
                    for cc in range(CH):
                        col = BETA * 16 + d * 8 + s * CH + cc
                        ins = STT(tile(m_t[:, g, :], cc), tile(ps[2 + s], cc), hs[:, col:col + 1],
                                  tile(dt_[:, g % 2, :], cc), ALU.mult, ALU.mult)
                    ins.then_inc(m_ready, 1)
                    dve.wait_ge(m_ready, 4 * h + (g + 1))
                    step(TT(chunks(x_1[:, g, :]), chunks(m_t[:, g, :]), bcast(lmask[0]), ALU.mult))
                    TT(chunks(u_t[:, g, :]), bcast(ident), chunks(x_1[:, g, :]), ALU.subtract).then_inc(u1_ready, 1)
                    dve.wait_ge(kq_done, 2 * h + (s + 1))
                    TT(att[:, g, :], ps[4 + s][:, :], dt_[:, g % 2, :], ALU.mult).then_inc(att_ready, 1)

                def decayed_q(g):
                    dve.wait_ge(egr_ready, 4 * h + (g + 1))
                    TT(q_d[:, g, :], qkv[:, QX, g // 2, :], egr[:, g % 2, :], ALU.mult).then_inc(qd_ready, 1)

                log_decays(0)
                log_decays(1)
                inverse_start(0)
                decayed_q(0)
                log_decays(2)
                inverse_start(1)
                decayed_q(1)
                log_decays(3)
                inverse_start(2)
                inverse_start(3)
                NL = LEVELS - 1
                for lv in range(NL):
                    for g in range(GROUPS):
                        dve.wait_ge(x1_done, 4 * NL * h + (4 * lv + g + 1))
                        TT(chunks(x_1[:, g, :]), chunks(ps[2 * g]), bcast(lmask[lv + 1]), ALU.mult).then_inc(x1_evac, 1)
                    for g in range(GROUPS):
                        dve.wait_ge(yy_done, 4 * NL * h + (4 * lv + g + 1))
                        if lv < NL - 1:
                            TT(d_n[:, g, :], d_n[:, g, :], ps[2 * g][:, :], ALU.subtract)
                        TT(u_t[:, g, :], u_t[:, g, :], ps[2 * g + 1][:, :], ALU.subtract).then_inc(ud_ready, 1)
                        if lv == 0:
                            dve.wait_ge(ud_ready, 4 * NL * h + (g + 1))
                    if lv == 0:
                        decayed_q(2)
                        decayed_q(3)
                for k in range(CH):
                    if k:
                        for g in range(GROUPS):
                            s, d = g // 2, g % 2
                            cc = k if d == 0 else CH - 1 - k
                            col = NEG_EG * 16 + d * 8 + s * CH + cc
                            dve.wait_ge(p1_done, 12 * h + (4 * (k - 1) + g + 1))
                            STT(x_1[:, g, 0:P], ps[2 * g][:, 0:P], hs[:, col:col + 1], tile(vg_tok[:, s, :], cc),
                                ALU.mult, ALU.add).then_inc(r_ready, 1)
                    if k < CH - 1:
                        for g in range(GROUPS):
                            s, d = g // 2, g % 2
                            cc = k if d == 0 else CH - 1 - k
                            col = CDECAY * 16 + d * 8 + s * CH + cc
                            dve.wait_ge(su_done, 12 * h + (4 * k + g + 1))
                            if k == 0:
                                nc.vector.tensor_copy(d_n[:, g, 0:P], ps[2 * g][:, 2 * P:3 * P]).then_inc(s_ready, 1)
                            else:
                                STT(d_n[:, g, 0:P], d_n[:, g, 0:P], hs[:, col:col + 1], ps[2 * g][:, 2 * P:3 * P],
                                    ALU.mult, ALU.add).then_inc(s_ready, 1)
                for s in range(SEQS):
                    dve.wait_ge(o_done, 4 * h + (2 * s + 2))
                    step(nc.vector.tensor_copy(o_sb[:, s, :], ps[4 * s + 1][:, :]))
                    TT(o_sb[:, s, :], o_sb[:, s, :], ps[4 * s + 3][:, :], ALU.add).then_inc(o_sum, 1)
                for s in range(SEQS):
                    dve.wait_ge(ors_ready, 2 * h + (s + 1))
                    step(TT(o_sb[:, s, :], o_sb[:, s, :], x_1[:, s, :], ALU.mult))
                for s in range(SEQS):
                    dve.wait_ge(z_silu, 2 * h + (s + 1))
                    STT(mix[:, bass.ds(h + PAIRS, 1), s * L:(s + 1) * L].rearrange("p a n -> p (a n)"), o_sb[:, s, :],
                        nw[:, 0:1], qkv[:, VX, s, :], ALU.mult, ALU.mult).then_inc(head_out, 1)
                dve.wait_ge(head_out, 2 * h + 3)
            step.leave(GH)

            for k in range(KT):
                dve.wait_ge(mix_high, k + 1)
                TT(m_lo[:, k, :], mix[:, k, :], m_hi[:, k, :].bitcast(F32), ALU.subtract).then_inc(mix_ready, 1)
            dve.wait_ge(mix_ready, KT)
            with dve.Fori(0, KT) as m:
                for s in range(SEQS):
                    dst = mix[:, bass.ds(m, 1), s * L:(s + 1) * L].rearrange("p a n -> p (a n)")
                    dve.wait_ge(proj_done, 2 * m + (2 * OUT0 + s + 1))
                    STT(dst, x_hi[:, bass.ds(m, 1), s * L:(s + 1) * L].bitcast(F32).rearrange("p a n -> p (a n)"), ALPHA,
                        ps[s][:, :], ALU.mult, ALU.add).then_inc(res_read, 1)
                    dve.wait_ge(res_read, 2 * m + (s + 2))
                    STT(dst, x_lo[:, bass.ds(m, 1), s * L:(s + 1) * L].bitcast(F32).rearrange("p a n -> p (a n)"), ALPHA,
                        dst, ALU.mult, ALU.add).then_inc(z_ready, 1)
            dve.wait_ge(z_ready, 2 * KT)

            def norm_dve(z, rs, mean_s, centred_s, rs_s, out_s, b0, gi):
                for s in range(SEQS):
                    dve.wait_ge(mean_s, s + 1)
                    for k in range(KT):
                        zt = seq(z[:, k, :], s)
                        TT(zt, zt, ps[b0 + s][:, :], ALU.subtract).then_inc(centred_s, 1)
                dve.wait_ge(centred_s, SEQS * KT)
                for s in range(SEQS):
                    dve.wait_ge(rs_s, s + 1)
                    for k in range(KT):
                        zt = seq(z[:, k, :], s)
                        step(TT(zt, zt, rs[:, s, :], ALU.mult))
                        TS(zt, zt, ln_sb[:, gi, k:k + 1], ln_sb[:, gi + 1, k:k + 1], ALU.mult, ALU.add).then_inc(out_s, 1)

            norm_dve(mix, rs1, mean_done, centred, ln_rs, ln_out, 2, 0)
            for s in range(SEQS):
                for k in range(KT):
                    dve.wait_ge(x1_high, s * KT + k + 1)
                    TT(seq(x_lo[:, k, :], s), seq(mix[:, k, :], s), seq(x_hi[:, k, :], s).bitcast(F32),
                       ALU.subtract).then_inc(x1_ready, 1)

            def up(j):
                def convolve(x, s):
                    b = 2 * x + s
                    dve.wait_ge(up_center, 4 * j + (b + 1))
                    for o, tap in ((-1, 0), (1, 2)):
                        a, e = max(0, -o), L - max(0, o)
                        ins = STT(cv[:, b, a:e], ps[b][:, a + o:e + o],
                                  fw[:, bass.ds(2 * j + x, 1), tap:tap + 1].rearrange("p a b -> p (a b)"),
                                  cv[:, b, a:e], ALU.mult, ALU.add)
                        if tap == 0:
                            step(ins)
                    ins.then_inc(up_conv, 1)

                def product(s):
                    dve.wait_ge(up_silu, 2 * j + (s + 1))
                    dve.wait_ge(up_conv, 4 * j + (3 + s))
                    TT(act[:, bass.ds(j, 1), s * L:(s + 1) * L].rearrange("p a n -> p (a n)"), cv[:, s, :], cv[:, 2 + s, :],
                       ALU.mult).then_inc(up_act, 1)

                convolve(0, 0)
                convolve(0, 1)
                convolve(1, 0)
                product(0)
                convolve(1, 1)
                product(1)

            base = step.base + step.n
            with dve.Fori(0, FJ) as j:
                step.enter(j, 4, base)
                up(j)
            step.leave(FJ)
            dve.wait_ge(up_act, 2 * FJ)

            def low(j, jj, u):
                dve.wait_ge(a_high, j + 1)
                TT(a_lo[u][:, :], act[:, bass.ds(jj, 1), :].rearrange("p a n -> p (a n)") if not isinstance(jj, int)
                   else act[:, jj, :], a_hi[u][:, :].bitcast(F32), ALU.subtract).then_inc(a_ready, 1)

            def accumulated(q):
                for m in range(4):
                    for s in range(SEQS):
                        zt = seq(z_all[:, 4 * q + m, :], s)
                        if m == 0 and s == 0:
                            dve.wait_ge(proj_done, 2 * DOWN0 + FJ * (q + 1))
                        STT(zt, seq(x_hi[:, 4 * q + m, :], s).bitcast(F32), ALPHA, ps[2 * m + s][:, :],
                            ALU.mult, ALU.add).then_inc(acc_read, 1)
                dve.wait_ge(acc_read, 8 * (q + 1))
                for m in range(4):
                    for s in range(SEQS):
                        zt = seq(z_all[:, 4 * q + m, :], s)
                        STT(zt, seq(x_lo[:, 4 * q + m, :], s).bitcast(F32), ALPHA, zt, ALU.mult, ALU.add).then_inc(z2_ready, 1)

            with dve.Fori(0, FJ // 2) as i:
                for u in range(2):
                    low(2 * i + u, 2 * i + u, u)
            low(FJ, 0, 0)
            low(FJ + 1, 1, 1)
            accumulated(0)
            with dve.Fori(1, FJ // 2) as i:
                for u in range(2):
                    low(2 * i + (FJ + u), 2 * i + u, u)
            accumulated(1)
            dve.wait_ge(z2_ready, 16)
            norm_dve(z_all, rs2, mean2_done, centred2, ln2_rs, y_ready, 0, 2)


def build(nc, arrays):
    args = {name: nc.dram_tensor(name, a.shape, F32, kind="ExternalInput").ap() for name, a in arrays.items()}
    yT = nc.dram_tensor("yT", (KT, P, T), F32, kind="ExternalOutput").ap()
    encoder_layer(nc, yT=yT, **args)


def shape_constants():
    i = np.arange(P)
    parts = [np.eye(P), i[:, None] <= i[None, :], i[:, None] >= i[None, :], np.ones((P, P))]
    parts += [np.where(i[:, None] <= i[None, :], 0.0, NEG), np.where(i[:, None] >= i[None, :], 0.0, NEG)]
    for v in range(LEVELS):
        half = i >> v
        parts.append((half[:, None] ^ half[None, :]) == 1)
    parts.append(np.eye(P)[::-1])
    consts = np.concatenate([p.astype(np.float32) for p in parts], axis=1)
    mask = np.zeros((P, len(SHIFTS), KEYS), np.float32)
    for t, sh in enumerate(SHIFTS):
        b = SHIFT.index(sh)
        qc = b * QB + np.arange(QB)
        start = np.clip(qc - WIN_C // 2, 0, GRID_W - WIN_C)
        kc = KC0[b] + np.arange(SPAN)
        seen = (kc[None, :] >= start[:, None]) & (kc[None, :] < start[:, None] + WIN_C)
        mask[:, t, :] = np.tile(np.where(seen, 0.0, NEG), (ROWS, ROWS))
    return consts, mask


def kernel(**inputs):
    import concourse.bacc as bacc
    from concourse.bass_utils import run_bass_kernel_spmd

    a = {n: np.asarray(v) for n, v in inputs.items()}
    x = np.concatenate([a["x_prompt"][0], a["x_sample"][0]], axis=0)
    w_in = a["w_in"][0]
    cuts = np.cumsum([0, 512, 512, 512, 512, 512, 512, 512, 16])

    def chunk(w):
        return w.reshape(KT, P, P).transpose(1, 0, 2).reshape(P, KT * P)

    def part(i, n):
        return chunk(w_in[:, cuts[i] + n * P:cuts[i] + (n + 1) * P])

    w_gate = np.zeros((D, P), np.float32)
    w_gate[:, 0:8] = w_in[:, cuts[7]:cuts[7] + 8]
    w_gate[:, 32:40] = w_in[:, cuts[7] + 8:cuts[7] + 16]
    gate_vec = np.zeros((P, 1), np.float32)
    gate_vec[32:40, 0] = a["gdn_dt_bias"][0].reshape(8)
    w_nat = np.stack([part(i, n) for n in range(PAIRS) for i in (0, 1, 2)])
    w_gdn = np.stack([part(i, h) for h in range(GH) for i in (4, 3, 5, 6)])
    w_out = np.stack([chunk(a["w_out"][0][:, m * P:(m + 1) * P]) for m in range(KT)])
    up = a["ffn_w_up"][0]
    w_up = np.stack([chunk(up[:, x0 + j * P:x0 + (j + 1) * P]) for j in range(FJ) for x0 in (0, FF)])
    w_down = a["ffn_w_down"][0].reshape(DPASS, 2, P, 2, 512).transpose(3, 0, 2, 1, 4).reshape(2 * DPASS, P, D)
    rpb = np.zeros(NA_HEADS * DR * DC + 2 * PAD, np.float32)
    rpb[PAD:-PAD] = a["na_rpb"][0].reshape(-1)
    gconv = a["gdn_conv_w"][0].reshape(TAPS, 3, GH, P)[:, [1, 0, 2]].transpose(3, 2, 1, 0).reshape(P, 3 * GH, TAPS)
    fconv = np.concatenate([a["ffn_conv_w"][0], a["ffn_conv_b"]], axis=0)
    fconv = fconv.reshape(4, 2, FJ, P).transpose(3, 2, 1, 0).reshape(P, 2 * FJ, 4)
    ln = np.stack([a[n][0].reshape(KT, P) for n in ("ln1_g", "ln1_b", "ln2_g", "ln2_b")]).transpose(2, 0, 1)
    consts, nat_mask = shape_constants()
    arrays = {
        "xT": x.T.reshape(KT, P, T), "w_gate": chunk(w_gate), "w_nat": w_nat, "w_gdn": w_gdn, "w_out": w_out,
        "w_up": w_up, "w_down": w_down, "rpb": rpb, "gdn_conv": gconv, "gate_vec": gate_vec,
        "a_log": a["gdn_a_log"][0].reshape(1, 8), "norm_w": a["gdn_norm_w"].reshape(P, 1), "ln_par": ln,
        "ffn_conv": fconv, "consts": consts, "nat_mask": nat_mask,
    }
    arrays = {n: np.ascontiguousarray(v) for n, v in arrays.items()}
    nc = bacc.Bacc("TRN2", target_bir_lowering=False, num_devices=1)
    build(nc, arrays)
    r = run_bass_kernel_spmd(nc, [arrays], core_ids=[0])
    y = r.results[0]["yT"].reshape(D, SEQS, L)
    return (np.ascontiguousarray(y[:, 0].T)[None], np.ascontiguousarray(y[:, 1].T)[None])
```

```python
import numpy as np
import concourse.bass as bass
from concourse import mybir
from concourse.alu_op_type import AluOpType as ALU

F32 = mybir.dt.float32
F32R = mybir.dt.float32r
ACT = mybir.ActivationFunctionType
AX = mybir.AxisListType

P = 128
D = 1024
SEQS, L = 2, 512
T = SEQS * L
KT = D // P
GRID_W, ROWS = 64, L // 64
NA_HEADS, HD = 8, 64
PAIRS = NA_HEADS // 2
WIN_R, WIN_C, QB = 8, 16, 16
SPAN = QB + WIN_C
BLOCKS = GRID_W // QB
KEYS = ROWS * SPAN
DC = 2 * WIN_C - 1
DR = 2 * WIN_R - 1
KC0 = [min(max(b * QB - WIN_C // 2, 0), GRID_W - SPAN) for b in range(BLOCKS)]
SHIFT = [KC0[b] - b * QB for b in range(BLOCKS)]
SHIFTS = sorted(set(SHIFT), reverse=True)
BIAS_RUN = (ROWS - 1) * DC + SPAN - SHIFTS[-1]
PAD = -SHIFTS[-1]
assert PAD == WIN_C
GH = 4
TAPS = 5
CH = L // P
GROUPS = 2 * SEQS
IB = 16
LEVELS = [v for v in range(7) if 1 << v >= IB]
NL = len(LEVELS)
UNITS = SEQS * BLOCKS
INST = GROUPS * CH
assert INST * (P // IB) == P
FF = 2816
FJ = FF // P
ALPHA = 2.0 ** 0.25
FILL = 4
LN_EPS, RMS_EPS = 1e-5, 1e-6
NEG = -1e30

GATE0 = 0
NAT0 = GATE0 + 1
GDN0 = NAT0 + 3 * PAIRS
OUT0 = GDN0 + 4 * GH
UP0 = OUT0 + KT
DOWN0 = UP0 + 2 * FJ
CHUNKS = DOWN0 + 2 * (FJ // 2)
DPASS = FJ // 2

BETA, NEG_EG, KAPPA, CDECAY, NEG_GC, GLOG = range(6)
HQ = 6 * 2 * SEQS * CH
GDN_STEPS = 25
ELIM_STEPS = 4 * (IB - 1)


def encoder_layer(nc, xT, w_all, rpb, gdn_conv, gate_vec, a_log,
                  norm_w, ln_par, ffn_conv, consts, nat_mask, yT, block_dram, inverse_dram):
    from contextlib import ExitStack
    ctx = ExitStack()
    with ctx:
        arena = nc.sbuf_base
        top = nc.sbuf_usable_end
        arena = (arena + 63) // 64 * 64
        used = []

        def place(name, shape, dt, at):
            size = 4
            for n in shape[1:]:
                size *= n
            assert at + size <= top, (name, at + size - top)
            used.append((name, at, size))
            return nc.alloc_sbuf_tensor_at(name, shape, dt, offset=at), at + (size + 31) // 32 * 32

        ln_sb, at = place("ln_sb", [P, 4, KT], F32, arena)
        fw, at = place("fw", [P, 2 * FJ, 4], F32, at)
        one, at = place("one", [P, 1], F32, at)
        fw_j, at = place("fw_j", [P, 2, 4], F32, at)
        mean_w, at = place("mean_w", [P, P], F32, at)
        eps, at = place("eps", [P, 4], F32, at)
        x_hi, at_hi = place("x_hi", [P, KT, T], F32R, at)
        z_all, _ = place("z_all", [P, KT, T], F32, at)
        x_lo, at = place("x_lo", [P, KT, T], F32R, at_hi)
        w_raw, w_hi, w_lo = [], [], []
        for u in range(2):
            t, at = place(f"w_raw{u}", [P, D], F32, at)
            w_raw.append(t)
            t, at = place(f"w_hi{u}", [P, D], F32R, at)
            w_hi.append(t)
            t, at = place(f"w_lo{u}", [P, D], F32R, at)
            w_lo.append(t)
        mix0 = at
        mix, at = place("mix", [P, KT, T], F32, at)
        region = at
        cv, m = place("cv", [P, 4, L], F32, mix0)
        a_hi, a_lo = [], []
        for u in range(2):
            t, m = place(f"a_hi{u}", [P, T], F32R, m)
            a_hi.append(t)
            t, m = place(f"a_lo{u}", [P, T], F32R, m)
            a_lo.append(t)
        act, _ = place("act", [P, FJ, T], F32, m)
        rs2, m = place("rs2", [P, SEQS, L], F32, mix0)
        sq2, m = place("sq2", [P, 2, L], F32, m)

        cst, at = place("cst", [P, consts.shape[1]], F32, region)
        sc, at = place("sc", [P, GH, HQ], F32, at)
        cw_all, at = place("cw_all", [P, 3 * GH, TAPS], F32, at)
        nw, at = place("nw", [P, 1], F32, at)
        mixer = at
        ident = cst[:, 0:P]
        tri = [cst[:, P:2 * P], cst[:, 2 * P:3 * P]]
        ones = cst[:, 3 * P:4 * P]
        negm = [cst[:, 4 * P:5 * P], cst[:, 5 * P:6 * P]]
        lmask = [cst[:, (6 + v) * P:(7 + v) * P] for v in range(NL)]
        turned_round = cst[:, (6 + NL) * P:(7 + NL) * P]
        same_block = cst[:, (7 + NL) * P:(8 + NL) * P]
        fold = cst[:, (8 + NL) * P:(8 + NL) * P + IB]
        small_ident = cst[:, (8 + NL) * P + IB:(8 + NL) * P + IB + IB * IB]

        bm, at = place("bm", [P, len(SHIFTS), NA_HEADS, KEYS], F32, mixer)
        q_nat, at = place("q_nat", [P, SEQS, L], F32, at)
        k_nat, at = place("k_nat", [P, SEQS, L], F32, at)
        k_next, at = place("k_next", [P, SEQS, L], F32, at)
        v_nat, at = place("v_nat", [P, SEQS, BLOCKS, KEYS], F32, at)
        gT, _ = place("gT", [64, T], F32, at)
        v_tok, at = place("v_tok", [P, SEQS, BLOCKS, 2, P], F32, at)
        bw, _ = place("bw", [P, NA_HEADS, BIAS_RUN], F32, at)
        s_sb, p_sb, pt_sb, nmax, psum_row, rrow = [], [], [], [], [], []
        for u in range(2):
            for lst, nm, n in ((s_sb, "s_sb", 2 * KEYS), (p_sb, "p_sb", 2 * KEYS),
                               (pt_sb, "pt_sb", 2 * KEYS), (nmax, "nmax", 2),
                               (psum_row, "psum_row", 2), (rrow, "rrow", 2)):
                t, at = place(f"{nm}{u}", [P, n], F32, at)
                lst.append(t)
        nmask, at = place("nmask", [P, len(SHIFTS), KEYS], F32, at)
        gv, at = place("gv", [P, 1], F32, at)
        al, at = place("al", [P, 8], F32, at)
        NG = SEQS * CH
        ga, at = place("ga", [P, NG, 64], F32, at)
        gt_ = {}
        for nm in ("e1", "ab", "e2", "lp", "beta", "sp", "g", "dif", "kd"):
            gt_[nm], at = place("gs_" + nm, [P, NG, 8], F32, at)
        ea, at = place("ea", [P, 8], F32, at)
        gcs, at = place("gcs", [P, 2 * 8 * NG], F32, at)
        ecs, at = place("ecs", [P, 2 * 8 * NG], F32, at)

        qkv, at = place("qkv", [P, 3, SEQS, L], F32, mixer)
        k_tok, at = place("k_tok", [P, SEQS, L], F32, at)
        vg_tok, at = place("vg_tok", [P, SEQS, L], F32, at)
        att, at = place("att", [P, GROUPS, L], F32, at)
        m_t, at = place("m_t", [P, GROUPS, L], F32, at)
        o_sb = m_t
        u_t, at = place("u_t", [P, GROUPS, L], F32, at)
        d_n, at = place("d_n", [P, GROUPS, L], F32, at)
        x_1, at = place("x_1", [P, GROUPS, L], F32, at)
        q_d, at = place("q_d", [P, GROUPS, L], F32, at)
        dt_, egr = att, d_n
        z_s, at = place("z_s", [P, SEQS, L], F32, at)
        packed, at = place("packed", [P, 2 * INST, IB], F32, at)
        blk, at = place("blk", [P, IB * IB], F32, at)
        inv, at = place("inv", [P, 2, IB * IB], F32, at)
        outer, at = place("outer", [P, IB * IB // 4], F32, at)
        hs, at = place("hs", [P, HQ], F32, at)
        cw, at = place("cw", [P, 3, TAPS], F32, at)
        KX, QX, VX = 0, 1, 2

        m_hi, at = place("m_hi", [P, KT, T], F32R, region + 512 * 0)
        m_lo, at = place("m_lo", [P, KT, T], F32R, at)
        rs1, at = place("rs1", [P, SEQS, L], F32, at)
        sq1, at = place("sq1", [P, 2, L], F32, at)

        banks = ctx.enter_context(nc.psum_tensor("banks", [P, 8, 512], F32))
        ps = [banks[:, b, :] for b in range(8)]

        names = []

        def sem(name):
            names.append(name)
            return ctx.enter_context(nc.semaphore(name))

        x_landed = [sem(f"x_landed{k}") for k in range(SEQS * KT)]
        cst_landed, gate_landed, bias_landed, al_landed = (sem("cst_landed"), sem("gate_landed"),
                                                           sem("bias_landed"), sem("al_landed"))
        par_landed = sem("par_landed")
        w_landed = [sem("w_landed0"), sem("w_landed1")]
        w_high, w_ready, proj_done = sem("w_high"), sem("w_ready"), sem("proj_done")
        x_high, x_ready = sem("x_high"), sem("x_ready")
        dstep, astep, eps_set = sem("dstep"), sem("astep"), sem("eps_set")
        bm_ready, bias_turned = sem("bm_ready"), sem("bias_turned")
        gate_tr, gate_tok, gate_soft, gate_g, gate_cum, gate_exp, sc_ready, g_e = (
            sem("gate_tr"), sem("gate_tok"), sem("gate_soft"), sem("gate_g"), sem("gate_cum"),
            sem("gate_exp"), sem("sc_ready"), sem("g_e"))
        k_copied = sem("k_copied")
        nat_evac, qk_done, s_biased, s_max, p_exp, p_ready = (
            sem("nat_evac"), sem("qk_done"), sem("s_biased"), sem("s_max"), sem("p_exp"), sem("p_ready"))
        vt_done, v_evac, pt_done, pt_evac, pv_done, o_evac = (
            sem("vt_done"), sem("v_evac"), sem("pt_done"), sem("pt_evac"), sem("pv_done"), sem("o_evac"))
        hs_ready, center, conv_done, silu_done, sq_done, nsum_done, rs_ready, normed = (
            sem("hs_ready"), sem("center"), sem("conv_done"), sem("silu_done"), sem("sq_done"),
            sem("nsum_done"), sem("rs_ready"), sem("normed"))
        ktr_done, k_tok_ready, vtr_done, vg_tok_ready, kk_done, kq_done, gc_done = (
            sem("ktr_done"), sem("k_tok_ready"), sem("vtr_done"), sem("vg_tok_ready"), sem("kk_done"),
            sem("kq_done"), sem("gc_done"))
        o_copied, masked, folded, fold_copied, blocks_stored, blocks_landed, eliminated = (
            sem("o_copied"), sem("masked"), sem("folded"), sem("fold_copied"), sem("blocks_stored"),
            sem("blocks_landed"), sem("eliminated"))
        inv_ready, inv_stored, d_landed, u_landed, d_ready, u_ready = (
            sem("inv_ready"), sem("inv_stored"), sem("d_landed"), sem("u_landed"), sem("d_ready"), sem("u_ready"))
        dt_ready, dt_exp, egr_ready, m_ready, att_ready, qd_ready = (
            sem("dt_ready"), sem("dt_exp"), sem("egr_ready"), sem("m_ready"), sem("att_ready"), sem("qd_ready"))
        x1_done, x1_evac, yy_done, ud_ready = sem("x1_done"), sem("x1_evac"), sem("yy_done"), sem("ud_ready")
        p1_done, r_ready, p2_done, vn_ready, su_done, s_ready, o_done = (
            sem("p1_done"), sem("r_ready"), sem("p2_done"), sem("vn_ready"), sem("su_done"),
            sem("s_ready"), sem("o_done"))
        osq_done, osum_done, ors_ready, z_silu, head_out = (
            sem("osq_done"), sem("osum_done"), sem("ors_ready"), sem("z_silu"), sem("head_out"))
        mix_high, mix_ready, res_read, z_ready = (
            sem("mix_high"), sem("mix_ready"), sem("res_read"), sem("z_ready"))
        mean_done, centred, var_sq, var_done, ln_rs, ln_out, x1_high, x1_ready = (
            sem("mean_done"), sem("centred"), sem("var_sq"), sem("var_done"), sem("ln_rs"),
            sem("ln_out"), sem("x1_high"), sem("x1_ready"))
        fw_copied, one_set = sem("fw_copied"), sem("one_set")
        norm_ln, out_ln, ln1_step, ln2_step = sem("norm_ln"), sem("out_ln"), sem("ln1_step"), sem("ln2_step")
        up_center, up_conv, up_silu, up_act = sem("up_center"), sem("up_conv"), sem("up_silu"), sem("up_act")
        a_high, a_ready, acc_read, z2_ready = sem("a_high"), sem("a_ready"), sem("acc_read"), sem("z2_ready")
        mean2_done, centred2, var2_sq, var2_done, ln2_rs, y_ready, y_stored = (
            sem("mean2_done"), sem("centred2"), sem("var2_sq"), sem("var2_done"), sem("ln2_rs"),
            sem("y_ready"), sem("y_stored"))

        def slot(c):
            return c % 2

        def seq(ap, s):
            return ap[:, s * L:(s + 1) * L]

        def flat(ap):
            return ap.rearrange("p a n -> p (a n)")

        def inst(g, cc):
            return (g % 2) * (INST // 2) + (g // 2) * CH + cc

        def unit(n):
            return n // BLOCKS, n % BLOCKS

        class Chain:

            def __init__(self, eng, s):
                self.eng, self.s, self.n, self.base = eng, s, 0, 0

            def __call__(self, ins):
                self.n += 1
                ins.then_inc(self.s, 1)
                self.eng.wait_ge(self.s, self.base + self.n)

            def enter(self, i, per, first):
                self.base, self.n, self.first = first + i * per, 0, first
                self.per = per

            def leave(self, times):
                assert self.n == self.per, (self.n, self.per)
                self.base, self.n = self.first + times * self.per, 0

        block = ctx.enter_context(nc.Block())

        @block.sync
        def _(sp):
            def load(c):
                u, c = c
                sp.wait_ge(w_ready, c - 1)
                sp.dma_start(w_raw[u][:, :], w_all[bass.ds(c, 1), :, :].rearrange("a p n -> (a p) n")
                             ).then_inc(w_landed[u], 16)

            for c in range(2):
                sp.dma_start(w_raw[c][:, :], w_all[c, :, :]).then_inc(w_landed[c], 16)

            def load_chunks(first, end):
                if (end - first) % 2:
                    load((slot(first), first))
                    first += 1
                with sp.Fori(0, (end - first) // 2) as i:
                    for u in range(2):
                        load((slot(first + u), 2 * i + (first + u)))

            load_chunks(2, GDN0 + 6)
            with sp.Fori(0, GH) as h:
                sp.wait_ge(fold_copied, h + 1)
                sp.dma_start(block_dram.rearrange("(i b) (r c) -> (b r) i c", b=P // IB, c=IB), packed[:, 0:INST, :]
                             ).then_inc(blocks_stored, 16)
                sp.wait_ge(blocks_stored, 16 * h + 16)
                sp.dma_start(blk[:, :], block_dram).then_inc(blocks_landed, 16)
                load((slot(GDN0 + 6), 4 * h + (GDN0 + 6)))
                sp.wait_ge(inv_ready, h + 1)
                sp.dma_start(inverse_dram.rearrange("m k n -> k m n"), inv[:, :, :]).then_inc(inv_stored, 16)
                sp.wait_ge(inv_stored, 16 * h + 16)
                for m, landed in enumerate((d_landed, u_landed)):
                    sp.dma_start(packed[:, m * INST:(m + 1) * INST, :],
                                 inverse_dram[m, :, :].rearrange("(i b) (r c) -> (b r) i c", b=P // IB, c=IB)
                                 ).then_inc(landed, 16)
                for n in range(7, 10):
                    load((slot(GDN0 + n), 4 * h + (GDN0 + n)))
            load_chunks(GDN0 + 4 * GH + 6, CHUNKS)
            for s in range(SEQS):
                for k in range(KT):
                    sp.wait_ge(y_ready, s * KT + k + 1)
                    sp.dma_start(yT[k, :, s * L:(s + 1) * L], seq(z_all[:, k, :], s)).then_inc(y_stored, 16)
            sp.wait_ge(y_stored, 16 * SEQS * KT)
            sp.wait_ge(d_landed, 16 * GH)
            sp.wait_ge(u_landed, 16 * GH)

        @block.gpsimd
        def _(pool):
            def split(c, u, landed, first=False):
                pool.wait_ge(w_landed[u], landed)
                if not first:
                    pool.wait_ge(proj_done, 2 * c - 2)
                nc.gpsimd.tensor_tensor(w_hi[u][:, :], w_raw[u][:, :], one[:, :].to_broadcast([P, D]),
                                        ALU.mult).then_inc(w_high, 1)
                pool.wait_ge(w_high, c + 1)
                nc.gpsimd.tensor_tensor(w_lo[u][:, :], w_raw[u][:, :], w_hi[u][:, :].bitcast(F32),
                                        ALU.subtract).then_inc(w_ready, 1)

            nc.gpsimd.memset(one[:, :], 1.0).then_inc(one_set, 1)
            pool.wait_ge(one_set, 1)
            split(0, 0, 16, first=True)
            split(1, 1, 16, first=True)
            split(2, 0, 32)
            with pool.Fori(0, (CHUNKS - 3) // 2) as i:
                for u in range(2):
                    split(2 * i + (3 + u), slot(3 + u), 16 * i + 16 * ((3 + u) // 2 + 1))

        @block.tensor
        def _(pe):
            mm = nc.tensor.matmul

            def project(c, bank, u, s, xh=None, xl=None, wait_k=None):
                xh = x_hi if xh is None else xh
                xl = x_lo if xl is None else xl
                n = 0
                for k in range(KT):
                    if wait_k is not None:
                        wait_k(k)
                    for w, x in ((w_hi, xh), (w_hi, xl), (w_lo, xh)):
                        last = mm(ps[bank][:, :], w[u][:, k * P:(k + 1) * P], seq(x[:, k, :], s),
                                  start=n == 0, stop=n == 3 * KT - 1)
                        n += 1
                last.then_inc(proj_done, 1)

            class Filler:

                def __init__(self, chunks, free):
                    self.todo = [(j, c, u, s) for j, (c, u) in enumerate(chunks) for s in range(SEQS)]
                    self.free, self.n = free, 0

                def __call__(self, count):
                    for _ in range(count):
                        at, i = divmod(self.n, 3 * KT)
                        if at == len(self.todo):
                            return
                        j, c, u, s = self.todo[at]
                        if i == 0:
                            if s == 0:
                                pe.wait_ge(w_ready, c + 1)
                            self.free(j, s)
                        k, part = divmod(i, 3)
                        w, x = ((w_hi, x_hi), (w_hi, x_lo), (w_lo, x_hi))[part]
                        ins = mm(ps[s][:, :], w[u][:, k * P:(k + 1) * P], seq(x[:, k, :], s),
                                 start=i == 0, stop=i == 3 * KT - 1)
                        if i == 3 * KT - 1:
                            ins.then_inc(proj_done, 1)
                        self.n += 1

                def finish(self):
                    self(3 * KT * len(self.todo) - self.n)

            def nat_filler(pair, n, u0):
                return Filler([(3 * pair + (NAT0 + j), slot(u0 + j)) for j in range(n)],
                              lambda j, s: pe.wait_ge(nat_evac, 6 * pair + (2 * j + s + 1)))

            pe.wait_ge(w_ready, 1)
            for s in range(SEQS):
                project(0, s, 0, s, wait_k=lambda k, s=s: pe.wait_ge(x_ready, s * KT + k + 1))
            fill = nat_filler(0, 3, NAT0)
            fill(3 * KT)
            pe.wait_ge(cst_landed, 16)
            pe.wait_ge(nat_evac, 2)
            for t in range(NG):
                last = nc.tensor.transpose(ps[2][:, t * 64:(t + 1) * 64], gT[:, t * P:(t + 1) * P],
                                           ident[0:64, 0:64])
            last.then_inc(gate_tr, 1)
            fill(3 * KT)
            pe.wait_ge(bias_landed, 16 * (ROWS + 1))
            for hh in range(NA_HEADS):
                if hh == 4:
                    fill(3 * KT)
                    pe.wait_ge(gate_g, 1)
                    for d in range(2):
                        mm(ps[3][:, d * 4 * NG:(d + 1) * 4 * NG].rearrange("p (t h) -> p t h", h=4),
                           tri[d], gt_["g"][:, :, 4 * d:4 * d + 4], start=True, stop=True)
                    mm(ps[3][:, 8 * NG:16 * NG], ones, flat(gt_["g"][:, :, :]), start=True, stop=True
                       ).then_inc(gate_cum, 1)
                    fill(3 * KT)
                if hh >= 4:
                    pe.wait_ge(bm_ready, len(SHIFTS) * (hh - 3))
                mm(ps[4 + hh % 4][:, 0:BIAS_RUN], turned_round, bw[:, hh, :], start=True, stop=True).then_inc(bias_turned, 1)
            fill.finish()
            pe.wait_ge(gate_exp, 1)
            pe.wait_ge(bm_ready, len(SHIFTS) * NA_HEADS)

            def turn_values(pair, n):
                s, half = n // 2, n % 2
                pe.wait_ge(nat_evac, 6 * pair + (5 + s))
                if s == 0:
                    pe.wait_ge(o_evac, 2 * pair + 1)
                else:
                    pe.wait_ge(v_evac, 4 * pair + (n - 1))
                for b in (2 * half, 2 * half + 1):
                    for kt in range(2):
                        keys = v_nat[:, s, b, kt * P:(kt + 1) * P]
                        last = nc.tensor.transpose(ps[6 + half][:, ((b % 2) * 2 + kt) * P:((b % 2) * 2 + kt + 1) * P],
                                                   keys, ident)
                last.then_inc(vt_done, 1)

            def attend(pair, odd, last_pair):
                following = 1 if last_pair else 3
                fill = nat_filler(pair + 1, following, NAT0 + 3 * (odd + 1))
                per = following * SEQS * 3 * KT // (UNITS + 1)
                scores(pair, 0)
                fill(per)
                scores(pair, 1)
                turn_values(pair, 0)
                turn_values(pair, 1)
                fill(per)
                turn(pair, 0)
                turn_values(pair, 2)
                turn_values(pair, 3)
                for n in range(2, UNITS + 2):
                    if n < UNITS:
                        scores(pair, n)
                    fill(per)
                    if n == UNITS:
                        fill.finish()
                    if n - 1 < UNITS:
                        turn(pair, n - 1)
                    values(pair, n - 2)

            def scores(pair, n):
                s, b = unit(n)
                if b == 0:
                    pe.wait_ge(nat_evac, 6 * pair + (7 + s))
                    pe.wait_ge(k_copied, 2 * pair + (s + 1))
                if n:
                    pe.wait_ge(s_biased, 8 * pair + n)
                for h in range(2):
                    keys = k_nat[64 * h:64 * h + 64, s, :].rearrange("p (r c) -> p r c", c=GRID_W)[
                        :, :, KC0[b]:KC0[b] + SPAN]
                    last = mm(ps[2 + h][:, 0:KEYS].rearrange("p (r c) -> p r c", c=SPAN),
                              q_nat[64 * h:64 * h + 64, s, b * P:(b + 1) * P], keys, start=True, stop=True)
                last.then_inc(qk_done, 1)

            def turn(pair, n):
                pe.wait_ge(p_ready, 8 * pair + (n + 1))
                if n >= 2:
                    pe.wait_ge(pt_evac, 8 * pair + (n - 1))
                for j in range(4):
                    last = nc.tensor.transpose(ps[4 + n % 2][:, j * P:(j + 1) * P],
                                               p_sb[n % 2][:, j * P:(j + 1) * P], ident)
                last.then_inc(pt_done, 1)

            def values(pair, n):
                s, b = unit(n)
                pe.wait_ge(pt_evac, 8 * pair + (n + 1))
                if n == 0:
                    pe.wait_ge(v_evac, 4 * pair + 4)
                for h in range(2):
                    for kt in range(2):
                        last = mm(ps[6 + s][64 * h:64 * h + 64, b * P:(b + 1) * P],
                                  v_tok[:, s, b, kt, 64 * h:64 * h + 64],
                                  pt_sb[n % 2][:, (2 * h + kt) * P:(2 * h + kt + 1) * P],
                                  start=kt == 0, stop=kt == 1)
                last.then_inc(pv_done, 1)

            with pe.Fori(0, PAIRS // 2 - 1) as i:
                for odd in range(2):
                    attend(2 * i + odd, odd, False)
            attend(PAIRS - 2, 0, False)
            attend(PAIRS - 1, 1, True)

            pe.wait_ge(o_evac, 2 * PAIRS + 1)

            def tile(ap, c):
                return ap[:, c * P:(c + 1) * P]

            def norm_sum(h, x, s):
                pe.wait_ge(sq_done, 4 * h + (2 * x + s + 1))
                mm(ps[2 + 2 * x + s][:, :], ones, q_d[:, 2 * x + s, :], start=True, stop=True).then_inc(nsum_done, 1)

            def delta_head(h, last_head):
                c = 4 * h + GDN0

                def cumulate(g):
                    s, d = g // 2, g % 2
                    if g >= 2:
                        pe.wait_ge(o_copied, 2 * h + (g - 1))
                    for cc in range(CH):
                        col = GLOG * 16 + d * 8 + s * CH + cc
                        ins = mm(tile(ps[4 + g], cc), hs[:, col:col + 1].to_broadcast([P, P]), tri[d],
                                 start=True, stop=True)
                    ins.then_inc(gc_done, 1)

                def cumulated(g):
                    pe.wait_ge(dt_ready, 4 * h + (g + 1))
                    pe.wait_ge(egr_ready, 4 * h + (g + 1))

                pe.wait_ge(hs_ready, h + 1)
                for g in range(GROUPS):
                    cumulate(g)
                pe.wait_ge(w_ready, c + 2)
                pe.wait_ge(conv_done, 6 * h + 1)
                project(c, 0, slot(GDN0 + 1), 0)
                norm_sum(h, KX, 0)
                norm_sum(h, KX, 1)
                pe.wait_ge(conv_done, 6 * h + 2)
                project(c, 1, slot(GDN0 + 1), 1)
                for s in range(SEQS):
                    pe.wait_ge(normed, 4 * h + (s + 1))
                    for cc in range(CH):
                        kc = tile(qkv[:, KX, s, :], cc)
                        ins = mm(tile(ps[2 + s], cc), kc, kc, start=True, stop=True)
                    ins.then_inc(kk_done, 1)
                for s in range(SEQS):
                    cumulated(2 + s)
                    for cc in range(CH):
                        ins = nc.tensor.transpose(tile(ps[6 + s], cc), tile(qkv[:, KX, s, :], cc), ident)
                    ins.then_inc(ktr_done, 1)
                pe.wait_ge(w_ready, c + 3)
                pe.wait_ge(conv_done, 6 * h + 3)
                project(c, 0, slot(GDN0 + 2), 0)
                for s in range(SEQS):
                    cumulated(s)
                    norm_sum(h, QX, s)
                pe.wait_ge(k_tok_ready, 2 * h + 1)
                for g in range(GROUPS):
                    pe.wait_ge(masked, 4 * h + (g + 1))
                    for cc in range(CH):
                        n = inst(g, cc)
                        ins = mm(ps[6][:, n * IB:(n + 1) * IB], tile(u_t[:, g, :], cc), fold, start=True, stop=True)
                ins.then_inc(folded, 1)
                pe.wait_ge(conv_done, 6 * h + 4)
                project(c, 1, slot(GDN0 + 2), 1)
                for s in range(SEQS):
                    pe.wait_ge(normed, 4 * h + (2 + s + 1))
                    for cc in range(CH):
                        ins = mm(tile(ps[4 + s], cc), tile(qkv[:, KX, s, :], cc), tile(qkv[:, QX, s, :], cc),
                                 start=True, stop=True)
                    ins.then_inc(kq_done, 1)
                pe.wait_ge(w_ready, c + 4)
                for s in range(SEQS):
                    pe.wait_ge(conv_done, 6 * h + (4 + s + 1))
                    project(c, s, slot(GDN0 + 3), s)
                    pe.wait_ge(silu_done, 6 * h + (4 + s + 1))
                    if s == 0:
                        pe.wait_ge(k_tok_ready, 2 * h + 2)
                    else:
                        pe.wait_ge(fold_copied, h + 1)
                    for cc in range(CH):
                        ins = nc.tensor.transpose(tile(ps[7 - s], cc), tile(qkv[:, VX, s, :], cc), ident)
                    ins.then_inc(vtr_done, 1)
                for lv in range(NL):
                    for g in range(GROUPS):
                        if lv == 0:
                            pe.wait_ge(d_ready, 4 * h + (g + 1))
                            if g == 0:
                                pe.wait_ge(z_silu, 2 * h + 2)
                            if g == 1:
                                pe.wait_ge(m_ready, 4 * h + 4)
                            if g == 2:
                                pe.wait_ge(att_ready, 4 * h + 4)
                            if g == 3:
                                pe.wait_ge(vg_tok_ready, 2 * h + 2)
                        else:
                            pe.wait_ge(ud_ready, 4 * NL * h + (4 * (lv - 1) + g + 1))
                        for cc in range(CH):
                            ins = mm(tile(ps[2 * g], cc), tile(m_t[:, g, :], cc), tile(d_n[:, g, :], cc),
                                     start=True, stop=True)
                        ins.then_inc(x1_done, 1)
                    for g in range(GROUPS):
                        if lv == 0:
                            pe.wait_ge(u_ready, 4 * h + (g + 1))
                        pe.wait_ge(x1_evac, 4 * NL * h + (4 * lv + g + 1))
                        if lv < NL - 1:
                            for cc in range(CH):
                                mm(tile(ps[2 * g], cc), tile(u_t[:, g, :], cc), tile(x_1[:, g, :], cc),
                                   start=True, stop=True)
                        for cc in range(CH):
                            ins = mm(tile(ps[2 * g + 1], cc), tile(x_1[:, g, :], cc), tile(u_t[:, g, :], cc),
                                     start=True, stop=True)
                        ins.then_inc(yy_done, 1)

                fill = Filler([] if last_head else [(c + 4, slot(GDN0))], lambda j, s: None)
                for k in range(CH):
                    def at_chunk(g):
                        return k if g % 2 == 0 else CH - 1 - k
                    if k:
                        for g in range(GROUPS):
                            pe.wait_ge(s_ready, 12 * h + (4 * (k - 1) + g + 1))
                            mm(ps[2 + g][:, 0:P], tile(qkv[:, KX, g // 2, :], at_chunk(g)), d_n[:, g, 0:P],
                               start=True, stop=True).then_inc(p1_done, 1)
                        fill(FILL)
                    for g in range(GROUPS):
                        if k:
                            pe.wait_ge(r_ready, 12 * h + (4 * (k - 1) + g + 1))
                            rhs = x_1[:, g, 0:P]
                        else:
                            pe.wait_ge(ud_ready, 4 * NL * h + (4 * (NL - 1) + max(g, (2 + g) // 2) + 1))
                            rhs = tile(vg_tok[:, g // 2, :], at_chunk(g))
                        mm(ps[2 + g][:, P:2 * P], tile(u_t[:, g, :], at_chunk(g)), rhs,
                           start=True, stop=True).then_inc(p2_done, 1)
                    fill(FILL)
                    for g in range(GROUPS):
                        cc = at_chunk(g)
                        out = tile(ps[6 + g // 2], cc)
                        pe.wait_ge(vn_ready, 16 * h + (4 * k + g + 1))
                        if k < CH - 1:
                            mm(ps[2 + g][:, 2 * P:3 * P], tile(k_tok[:, g // 2, :], cc), x_1[:, g, 2 * P:3 * P],
                               start=True, stop=True).then_inc(su_done, 1)
                        if k:
                            mm(out, d_n[:, g, 0:P], tile(q_d[:, g, :], cc), start=False, stop=False)
                        elif g == 0:
                            pe.wait_ge(qd_ready, 4 * h + 4)
                        ins = mm(out, x_1[:, g, P:2 * P], tile(att[:, g, :], cc), start=k == 0 and g % 2 == 0,
                                 stop=k == CH - 1 and g % 2 == 1)
                        if k:
                            ins.then_inc(o_done, 1)
                    if k < CH - 1:
                        fill(FILL)
                fill.finish()
                for s in range(SEQS):
                    pe.wait_ge(osq_done, 2 * h + (s + 1))
                    mm(ps[2 + s][:, :], ones, q_d[:, s, :], start=True, stop=True).then_inc(osum_done, 1)

            with pe.Fori(0, GH - 1) as h:
                delta_head(h, False)
            delta_head(GH - 1, True)

            pe.wait_ge(head_out, 2 * GH + 1)
            with pe.Fori(0, KT // 2) as i:
                for u in range(2):
                    c = 2 * i + (OUT0 + u)
                    pe.wait_ge(w_ready, c + 1)
                    for s in range(SEQS):
                        if u:
                            pe.wait_ge(res_read, 4 * i + (s + 2))
                        elif s == 0:
                            pe.wait_ge(res_read, 4 * i + 1)
                        project(c, s, slot(OUT0 + u), s, m_hi, m_lo,
                                (lambda k: pe.wait_ge(mix_ready, k + 1)) if s == 0 else None)

            def norm_means(z, centred_s, mean_s, sq, sq_s, var_s, ready, b0):
                for s in range(SEQS):
                    ready(s)
                    for k in range(KT):
                        last = mm(ps[b0 + s][:, :], mean_w[:, :], seq(z[:, k, :], s), start=k == 0, stop=k == KT - 1)
                    last.then_inc(mean_s, 1)
                for s in range(SEQS):
                    for k in range(KT):
                        n = s * KT + k
                        pe.wait_ge(sq_s, n + 1)
                        last = mm(ps[b0 + 2 + s][:, :], mean_w[:, :], sq[:, n % 2, :], start=k == 0, stop=k == KT - 1)
                        last.then_inc(var_s, 1)

            norm_means(mix, centred, mean_done, sq1, var_sq, var_done,
                       lambda s: pe.wait_ge(z_ready, 2 * KT - 1 + s), 2)

            def up(j, first):
                for x in range(2):
                    c = 2 * j + (UP0 + x)
                    pe.wait_ge(w_ready, c + 1)
                    for s in range(SEQS):
                        b = 2 * x + s
                        if not first:
                            pe.wait_ge(up_conv, 4 * j + (b - 3))
                        elif b == 2:
                            pe.wait_ge(ln_out, SEQS * KT)
                        project(c, b, slot(UP0 + x), s,
                                wait_k=(lambda k, s=s: pe.wait_ge(x1_ready, s * KT + k + 1)) if first and x == 0 else None)

            up(0, True)
            with pe.Fori(1, FJ) as j:
                up(j, False)

            def down(q, cc, c, u, first=False, last=False):
                pe.wait_ge(w_ready, c + 1)
                for t in range(2):
                    pe.wait_ge(a_ready, 2 * cc + (q * FJ + t + 1))
                    for m in range(4):
                        for s in range(SEQS):
                            if first and t == 0 and q:
                                pe.wait_ge(acc_read, 2 * m + s + 1)
                            for n, (w, a) in enumerate(((w_hi, a_hi), (w_hi, a_lo), (w_lo, a_hi))):
                                ins = mm(ps[2 * m + s][:, :], w[u][:, t * 512 + m * P:t * 512 + (m + 1) * P],
                                         seq(a[t], s), start=first and t == 0 and n == 0,
                                         stop=last and t == 1 and n == 2)
                    ins.then_inc(proj_done, 1)

            pe.wait_ge(up_conv, 4 * FJ)
            for q in range(2):
                c0 = DOWN0 + q * DPASS
                down(q, 0, c0, slot(c0), first=True)
                with pe.Fori(0, (DPASS - 3) // 2) as i:
                    for u in range(2):
                        down(q, 2 * i + (1 + u), 2 * i + (c0 + 1 + u), slot(c0 + 1 + u))
                down(q, DPASS - 2, c0 + DPASS - 2, slot(c0 + DPASS - 2))
                down(q, DPASS - 1, c0 + DPASS - 1, slot(c0 + DPASS - 1), last=True)

            def ready2(s):
                pe.wait_ge(z2_ready, 2 * KT)

            norm_means(z_all, centred2, mean2_done, sq2, var2_sq, var2_done, ready2, 0)

        @block.scalar
        def _(act_e):
            A = nc.scalar.activation
            for n in range(SEQS * KT):
                s, k = divmod(n, KT)
                act_e.dma_start(seq(mix[:, k, :], s), xT[k, :, s * L:(s + 1) * L]).then_inc(x_landed[n], 16)
            act_e.dma_start(cst[:, :], consts).then_inc(cst_landed, 16)
            act_e.dma_start(gv[:, :], gate_vec).then_inc(gate_landed, 16)
            act_e.dma_start(al[:, :], bass.AP(a_log.tensor, 0, [[0, P], [1, 8]])
                            ).then_inc(al_landed, 16)
            for r in range(ROWS):
                src = bass.AP(rpb.tensor, r * DC, [[1, QB], [DR * DC, NA_HEADS], [1, BIAS_RUN]])
                act_e.dma_start(bw[r * QB:(r + 1) * QB, :, :], src).then_inc(bias_landed, 16)
            act_e.dma_start(nmask[:, :, :], nat_mask).then_inc(bias_landed, 16)
            act_e.dma_start(cw_all[:, :, :], gdn_conv).then_inc(par_landed, 16)
            act_e.dma_start(nw[:, :], norm_w).then_inc(par_landed, 16)
            act_e.dma_start(ln_sb[:, :, :], ln_par).then_inc(par_landed, 16)
            act_e.dma_start(fw[:, :, :], ffn_conv).then_inc(par_landed, 16)
            for n in range(SEQS * KT):
                s, k = divmod(n, KT)
                act_e.wait_ge(x_landed[n], 16)
                nc.scalar.copy(seq(x_hi[:, k, :], s), seq(mix[:, k, :], s)).then_inc(x_high, 1)

            def projected(pair, n):
                j, s = divmod(n, SEQS)
                act_e.wait_ge(proj_done, 6 * pair + (2 * (NAT0 + j) + s + 1))
                if j == 0:
                    nc.scalar.copy(k_next[:, s, :], ps[s][:, :]).then_inc(nat_evac, 1)
                elif j == 1:
                    for b, d in ((0, 3), (1, 1)):
                        src = bass.AP(ps[s].tensor, s * 512 + KC0[b],
                                      [[8 * 512, P], [KC0[b + d] - KC0[b], 2], [GRID_W, ROWS], [1, SPAN]])
                        ins = nc.scalar.copy(v_nat[:, s, b:b + d + 1:d, :].rearrange(
                            "p b (r c) -> p b r c", c=SPAN), src)
                    ins.then_inc(nat_evac, 1)
                else:
                    out = q_nat[:, s, :].rearrange("p (b r c) -> p r b c", b=BLOCKS, r=ROWS)
                    A(out, ps[s][:, :].rearrange("p (r b c) -> p r b c", r=ROWS, b=BLOCKS), ACT.Copy,
                      scale=HD ** -0.5).then_inc(nat_evac, 1)

            act_e.wait_ge(gate_landed, 16)
            for s in range(SEQS):
                act_e.wait_ge(proj_done, s + 1)
                A(seq(gT, s), ps[s][0:64, :], ACT.Identity, bias=gv[0:64, 0:1]).then_inc(nat_evac, 1)
            projected(0, 0)
            act_e.wait_ge(gate_tr, 1)
            nc.scalar.copy(flat(ga[:, :, :]), ps[2][:, :]).then_inc(gate_tok, 1)
            act_e.wait_ge(gate_tok, 1)
            step = Chain(act_e, astep)
            step(A(gt_["e1"][:, :, :], ga[:, :, 0:8], ACT.Exp, scale=-1.0))
            step(A(gt_["ab"][:, :, :], ga[:, :, 32:40], ACT.Abs))
            act_e.wait_ge(al_landed, 16)
            step(A(ea[:, :], al[:, :], ACT.Exp))
            step(A(gt_["e2"][:, :, :], gt_["ab"][:, :, :], ACT.Exp, scale=-1.0))
            act_e.wait_ge(eps_set, 4)
            A(gt_["lp"][:, :, :], gt_["e2"][:, :, :], ACT.Ln, bias=eps[:, 3:4]).then_inc(gate_soft, 1)
            projected(0, 1)
            projected(0, 2)
            act_e.wait_ge(gate_cum, 1)
            step(nc.scalar.copy(gcs[:, :], ps[3][:, 0:16 * NG]))
            A(ecs[:, :], gcs[:, :], ACT.Exp).then_inc(gate_exp, 1)
            projected(0, 3)
            act_e.wait_ge(g_e, 1)
            A(gt_["kd"][:, :, :], gt_["dif"][:, :, :], ACT.Exp).then_inc(gate_exp, 1)
            projected(0, 4)
            projected(0, 5)

            def exps(pair, n):
                act_e.wait_ge(s_max, 8 * pair + (n + 1))
                if n >= 2:
                    act_e.wait_ge(pt_done, 8 * pair + (n - 1))
                for h in range(2):
                    ins = A(p_sb[n % 2][:, h * KEYS:(h + 1) * KEYS], s_sb[n % 2][:, h * KEYS:(h + 1) * KEYS], ACT.Exp,
                            bias=nmax[n % 2][:, h:h + 1], accum_out=psum_row[n % 2][:, h:h + 1])
                ins.then_inc(p_exp, 1)

            def turned(pair, n):
                act_e.wait_ge(pt_done, 8 * pair + (n + 1))
                if n >= 2:
                    act_e.wait_ge(pv_done, 8 * pair + (n - 1))
                nc.scalar.copy(pt_sb[n % 2][:, :], ps[4 + n % 2][:, :]).then_inc(pt_evac, 1)

            def attend(pair, last_pair):
                exps(pair, 0)
                exps(pair, 1)
                for n in range(2):
                    turned_values(pair, n)
                turned(pair, 0)
                for n in range(2, 4):
                    turned_values(pair, n)
                done_at = {1: 0, 2: 1, 4: 2, 5: 3, 7: 4, 8: 5}
                for n in range(1, UNITS + 1):
                    if 2 <= n < UNITS:
                        exps(pair, n)
                    if n >= 2:
                        turned(pair, n - 1)
                    if not last_pair and n in done_at:
                        if n == 1:
                            act_e.wait_ge(k_copied, 2 * pair + 2)
                        if n == 7:
                            act_e.wait_ge(qk_done, 8 * pair + 8)
                        projected(pair + 1, done_at[n])

            def turned_values(pair, n):
                act_e.wait_ge(vt_done, 4 * pair + (n + 1))
                s, half = n // 2, n % 2
                nc.scalar.copy(v_tok[:, s, 2 * half:2 * half + 2, :, :].rearrange("p b k n -> p (b k n)"),
                               ps[6 + half][:, :]).then_inc(v_evac, 1)

            with act_e.Fori(0, PAIRS // 2 - 1) as i:
                for odd in range(2):
                    attend(2 * i + odd, False)
            attend(PAIRS - 2, False)
            attend(PAIRS - 1, True)

            act_e.wait_ge(o_evac, 2 * PAIRS + 1)

            def centre(h, x, s):
                act_e.wait_ge(proj_done, 8 * h + (2 * (GDN0 + x) + s + 1))
                A(qkv[:, x, s, :], ps[s][:, :], ACT.Identity,
                  scale=cw[:, x, TAPS // 2:TAPS // 2 + 1]).then_inc(center, 1)

            def delta_head(h, last_head):
                def silu(x, s):
                    act_e.wait_ge(conv_done, 6 * h + (2 * x + s + 1))
                    A(qkv[:, x, s, :], qkv[:, x, s, :], ACT.Silu).then_inc(silu_done, 1)
                    if x < 2:
                        act_e.wait_ge(silu_done, 6 * h + (2 * x + s + 1))
                        A(q_d[:, 2 * x + s, :], qkv[:, x, s, :], ACT.Square).then_inc(sq_done, 1)

                def inverse_roots(x):
                    for s in range(SEQS):
                        act_e.wait_ge(nsum_done, 4 * h + (2 * x + s + 1))
                        A(x_1[:, 2 * x + s, :], ps[2 + 2 * x + s][:, :], ACT.Ln, scale=1.0 if x == KX else float(P),
                          bias=eps[:, x:x + 1]).then_inc(norm_ln, 1)
                    act_e.wait_ge(norm_ln, 4 * h + (2 * x + 2))
                    for s in range(SEQS):
                        A(x_1[:, 2 * x + s, :], x_1[:, 2 * x + s, :], ACT.Exp, scale=-0.5).then_inc(rs_ready, 1)

                def turned_v(s):
                    act_e.wait_ge(vtr_done, 2 * h + (s + 1))
                    nc.scalar.copy(vg_tok[:, s, :], ps[7 - s][:, :]).then_inc(vg_tok_ready, 1)

                def gate(s):
                    act_e.wait_ge(proj_done, 8 * h + (2 * (GDN0 + 3) + s + 1))
                    A(z_s[:, s, :], ps[s][:, :], ACT.Silu).then_inc(z_silu, 1)

                silu(KX, 0)
                silu(KX, 1)
                centre(h, QX, 0)
                act_e.wait_ge(head_out, 2 * h + 1)
                inverse_roots(KX)
                for g in range(GROUPS):
                    act_e.wait_ge(dt_ready, 4 * h + (g + 1))
                    A(dt_[:, g, :], dt_[:, g, :], ACT.Exp).then_inc(dt_exp, 1)
                    A(egr[:, g, :], ps[4 + g][:, :], ACT.Exp).then_inc(egr_ready, 1)
                centre(h, QX, 1)
                silu(QX, 0)
                silu(QX, 1)
                for s in range(SEQS):
                    act_e.wait_ge(ktr_done, 2 * h + (s + 1))
                    nc.scalar.copy(k_tok[:, s, :], ps[6 + s][:, :]).then_inc(k_tok_ready, 1)
                centre(h, VX, 0)
                inverse_roots(QX)
                act_e.wait_ge(folded, h + 1)
                nc.scalar.copy(packed[:, 0:INST, :].rearrange("p i c -> p (i c)"), ps[6][:, 0:INST * IB]
                               ).then_inc(fold_copied, 1)
                silu(VX, 0)
                centre(h, VX, 1)
                silu(VX, 1)
                gate(0)
                turned_v(0)
                gate(1)
                turned_v(1)
                for k in range(CH):
                    for g in range(GROUPS):
                        s, d = g // 2, g % 2
                        cc = k if d == 0 else CH - 1 - k
                        col = d * 8 + s * CH + cc
                        act_e.wait_ge(p2_done, 16 * h + (4 * k + g + 1))
                        A(x_1[:, g, 2 * P:3 * P], ps[2 + g][:, P:2 * P], ACT.Identity,
                          scale=hs[:, KAPPA * 16 + col:KAPPA * 16 + col + 1])
                        A(x_1[:, g, P:2 * P], ps[2 + g][:, P:2 * P], ACT.Identity,
                          scale=hs[:, BETA * 16 + col:BETA * 16 + col + 1]).then_inc(vn_ready, 1)
                for s in range(SEQS):
                    act_e.wait_ge(o_done, 12 * h + (10 + 2 * s))
                    if s == 0:
                        act_e.wait_ge(ud_ready, 4 * NL * h + 4 * NL)
                    A(q_d[:, s, :], ps[6 + s][:, :], ACT.Square).then_inc(osq_done, 1)
                    nc.scalar.copy(o_sb[:, s, :], ps[6 + s][:, :]).then_inc(o_copied, 1)
                if not last_head:
                    act_e.wait_ge(hs_ready, h + 2)
                    for s in range(SEQS):
                        centre(h + 1, KX, s)
                for s in range(SEQS):
                    act_e.wait_ge(osum_done, 2 * h + (s + 1))
                    A(x_1[:, s, :], ps[2 + s][:, :], ACT.Ln, scale=1.0 / P, bias=eps[:, 0:1]).then_inc(out_ln, 1)
                act_e.wait_ge(out_ln, 2 * h + 2)
                for s in range(SEQS):
                    A(x_1[:, s, :], x_1[:, s, :], ACT.Exp, scale=-0.5).then_inc(ors_ready, 1)

            act_e.sem_inc(o_copied, 2)
            act_e.wait_ge(hs_ready, 1)
            for s in range(SEQS):
                centre(0, KX, s)
            with act_e.Fori(0, GH - 1) as h:
                delta_head(h, False)
            delta_head(GH - 1, True)

            act_e.wait_ge(head_out, 2 * GH + 1)
            for k in range(KT):
                nc.scalar.copy(m_hi[:, k, :], mix[:, k, :]).then_inc(mix_high, 1)

            def norm_act(z, rs, sq, centred_s, sq_s, var_s, rs_s, b0, lnstep):
                for s in range(SEQS):
                    for k in range(KT):
                        n = s * KT + k
                        act_e.wait_ge(centred_s, n + 1)
                        if n >= 2:
                            act_e.wait_ge(var_s, n - 1)
                        A(sq[:, n % 2, :], seq(z[:, k, :], s), ACT.Square).then_inc(sq_s, 1)
                    act_e.wait_ge(var_s, (s + 1) * KT)
                    A(rs[:, s, :], ps[b0 + 2 + s][:, :], ACT.Ln, bias=eps[:, 2:3]).then_inc(lnstep, 1)
                    act_e.wait_ge(lnstep, s + 1)
                    A(rs[:, s, :], rs[:, s, :], ACT.Exp, scale=-0.5).then_inc(rs_s, 1)

            norm_act(mix, rs1, sq1, centred, var_sq, var_done, ln_rs, 2, ln1_step)
            for s in range(SEQS):
                for k in range(KT):
                    act_e.wait_ge(ln_out, s * KT + k + 1)
                    nc.scalar.copy(seq(x_hi[:, k, :], s), seq(mix[:, k, :], s)).then_inc(x1_high, 1)
            act_e.wait_ge(x1_ready, SEQS * KT)

            def up(j, first):
                def centre(x, s):
                    b = 2 * x + s
                    act_e.wait_ge(proj_done, 4 * j + (2 * (UP0 + x) + s + 1))
                    if not first:
                        act_e.wait_ge(up_act, 2 * j + (s - 1))
                    A(cv[:, b, :], ps[b][:, :], ACT.Identity,
                      scale=fw_j[:, x, 1:2], bias=fw_j[:, x, 3:4]).then_inc(up_center, 1)
                nc.scalar.copy(fw_j[:, :, :], fw[:, bass.ds(2 * j, 2), :]).then_inc(fw_copied, 1)
                act_e.wait_ge(fw_copied, j + 1)
                centre(0, 0)
                centre(0, 1)
                for s in range(SEQS):
                    act_e.wait_ge(up_conv, 4 * j + (s + 1))
                    A(cv[:, s, :], cv[:, s, :], ACT.Silu).then_inc(up_silu, 1)
                centre(1, 0)
                centre(1, 1)
                act_e.wait_ge(up_center, 4 * j + 4)

            act_e.wait_ge(par_landed, 64)
            up(0, True)
            with act_e.Fori(1, FJ) as j:
                up(j, False)

            def high(j, jj, u):
                act_e.wait_ge(up_act, 2 * FJ)
                act_e.wait_ge(proj_done, j + (2 * DOWN0 - 1))
                nc.scalar.copy(a_hi[u][:, :], act[:, bass.ds(jj, 1), :].rearrange("p a n -> p (a n)")).then_inc(a_high, 1)

            for q in range(2):
                with act_e.Fori(0, FJ // 2) as i:
                    for u in range(2):
                        high(2 * i + (q * FJ + u), 2 * i + u, u)
            norm_act(z_all, rs2, sq2, centred2, var2_sq, var2_done, ln2_rs, 0, ln2_step)

        @block.vector
        def _(dve):
            TT, TS, STT = nc.vector.tensor_tensor, nc.vector.tensor_scalar, nc.vector.scalar_tensor_tensor
            nc.vector.memset(eps[:, 0:1], RMS_EPS).then_inc(eps_set, 1)
            nc.vector.memset(eps[:, 1:2], P * RMS_EPS).then_inc(eps_set, 1)
            nc.vector.memset(eps[:, 2:3], LN_EPS).then_inc(eps_set, 1)
            nc.vector.memset(eps[:, 3:4], 1.0).then_inc(eps_set, 1)
            for counter in (o_evac, head_out, res_read):
                dve.sem_inc(counter, 1)
            step = Chain(dve, dstep)
            step(nc.vector.memset(mean_w[:, :], 1.0 / D))
            for n in range(SEQS * KT):
                s, k = divmod(n, KT)
                dve.wait_ge(x_high, n + 1)
                TT(seq(x_lo[:, k, :], s), seq(mix[:, k, :], s), seq(x_hi[:, k, :], s).bitcast(F32),
                   ALU.subtract).then_inc(x_ready, 1)
            dve.wait_ge(gate_soft, 1)
            step(nc.vector.tensor_scalar_add(gt_["beta"][:, :, :], gt_["e1"][:, :, :], 1.0))
            step(nc.vector.reciprocal(gt_["beta"][:, :, :], gt_["beta"][:, :, :]))
            step(STT(gt_["sp"][:, :, :], ga[:, :, 32:40], 0.0, gt_["lp"][:, :, :], ALU.max, ALU.add))
            STT(gt_["g"][:, :, :], gt_["sp"][:, :, :], -1.0, ea[:, :].unsqueeze(1).to_broadcast([P, NG, 8]),
                ALU.mult, ALU.mult).then_inc(gate_g, 1)
            dve.wait_ge(gate_exp, 1)
            tot = gcs[:, 8 * NG:16 * NG].rearrange("p (t d h) -> p t d h", d=2, h=4)
            etot = ecs[:, 8 * NG:16 * NG].rearrange("p (t d h) -> p t d h", d=2, h=4)
            for d in range(2):
                gc = gcs[:, d * 4 * NG:(d + 1) * 4 * NG].rearrange("p (t h) -> p t h", h=4)
                ins = TT(gt_["dif"][:, :, 4 * d:4 * d + 4], tot[:, :, d, :], gc, ALU.subtract)
            ins.then_inc(g_e, 1)
            dve.wait_ge(gate_exp, 2)
            for d in range(2):
                hd = slice(4 * d, 4 * d + 4)
                gc = gcs[:, d * 4 * NG:(d + 1) * 4 * NG].rearrange("p (t h) -> p t h", h=4)
                eg = ecs[:, d * 4 * NG:(d + 1) * 4 * NG].rearrange("p (t h) -> p t h", h=4)

                def out(q):
                    return sc[:, :, q * 16 + d * 8:q * 16 + d * 8 + 8].rearrange("p h t -> p t h")
                nc.vector.tensor_copy(out(BETA), gt_["beta"][:, :, hd]).then_inc(sc_ready, 1)
                nc.vector.tensor_scalar_mul(out(NEG_EG), eg, -1.0).then_inc(sc_ready, 1)
                TT(out(KAPPA), gt_["kd"][:, :, hd], gt_["beta"][:, :, hd], ALU.mult).then_inc(sc_ready, 1)
                nc.vector.tensor_copy(out(CDECAY), etot[:, :, d, :]).then_inc(sc_ready, 1)
                nc.vector.tensor_scalar_mul(out(NEG_GC), gc, -1.0).then_inc(sc_ready, 1)
                nc.vector.tensor_copy(out(GLOG), gt_["g"][:, :, hd]).then_inc(sc_ready, 1)
            dve.wait_ge(sc_ready, 12)
            dve.wait_ge(bias_landed, 16 * (ROWS + 1))
            for hh in range(NA_HEADS):
                dve.wait_ge(bias_turned, hh + 1)
                for t, sh in enumerate(SHIFTS):
                    win = bass.AP(ps[0].tensor, (4 + hh % 4) * 512 + sh - SHIFTS[-1], [[8 * 512, P], [DC, ROWS], [1, SPAN]])
                    TT(bm[:, t, hh, :].rearrange("p (r c) -> p r c", c=SPAN), win,
                       nmask[:, t, :].rearrange("p (r c) -> p r c", c=SPAN), ALU.add).then_inc(bm_ready, 1)

            def biased(pair, n):
                s, b = unit(n)
                dve.wait_ge(qk_done, 8 * pair + (n + 1))
                if n >= 2:
                    dve.wait_ge(p_exp, 8 * pair + (n - 1))
                TT(s_sb[n % 2][:, :].rearrange("p (h n) -> p h n", h=2), banks[:, 2:4, 0:KEYS],
                   bm[:, SHIFTS.index(SHIFT[b]), bass.ds(2 * pair, 2), :], ALU.add).then_inc(s_biased, 1)
                dve.wait_ge(s_biased, 8 * pair + (n + 1))
                nc.vector.tensor_reduce(nmax[n % 2][:, :], s_sb[n % 2][:, :].rearrange("p (h n) -> p h n", h=2),
                                        AX.X, ALU.max, negate=True).then_inc(s_max, 1)

            def normalised(pair, n):
                dve.wait_ge(p_exp, 8 * pair + (n + 1))
                step(nc.vector.reciprocal(rrow[n % 2][:, :], psum_row[n % 2][:, :]))
                for h in range(2):
                    pr = p_sb[n % 2][:, h * KEYS:(h + 1) * KEYS]
                    ins = nc.vector.tensor_scalar_mul(pr, pr, rrow[n % 2][:, h:h + 1])
                ins.then_inc(p_ready, 1)

            def attended(pair, s):
                dve.wait_ge(pv_done, 8 * pair + 4 * (s + 1))
                nc.vector.tensor_copy(
                    mix[:, bass.ds(pair, 1), s * L:(s + 1) * L].rearrange("p a (r b c) -> p (a r) b c", r=ROWS, b=BLOCKS),
                    ps[6 + s][:, :].rearrange("p (b r c) -> p r b c", b=BLOCKS, r=ROWS)).then_inc(o_evac, 1)

            def next_keys(pair, first=False):
                for s in range(SEQS):
                    dve.wait_ge(nat_evac, 6 * pair + (s + 3))
                    if not first:
                        dve.wait_ge(qk_done, 8 * pair)
                    nc.vector.tensor_copy(k_nat[:, s, :], k_next[:, s, :]).then_inc(k_copied, 1)

            def attend(pair, last_pair):
                biased(pair, 0)
                biased(pair, 1)
                normalised(pair, 0)
                for n in range(2, UNITS):
                    biased(pair, n)
                    normalised(pair, n - 1)
                    if n == 6:
                        attended(pair, 0)
                if not last_pair:
                    next_keys(pair + 1)
                normalised(pair, UNITS - 1)
                attended(pair, 1)

            next_keys(0, first=True)
            base = step.n
            dve.wait_ge(bm_ready, 3 * NA_HEADS)
            with dve.Fori(0, PAIRS // 2 - 1) as i:
                step.enter(i, 2 * UNITS, base)
                for odd in range(2):
                    attend(2 * i + odd, False)
            step.leave(PAIRS // 2 - 1)
            attend(PAIRS - 2, False)
            attend(PAIRS - 1, True)

            def tile(ap, c):
                return ap[:, c * P:(c + 1) * P]

            dve.wait_ge(par_landed, 64)
            dve.wait_ge(o_evac, 2 * PAIRS + 1)

            def head_constants(h):
                step(nc.vector.tensor_copy(hs[:, :], sc[:, bass.ds(h, 1), :].rearrange("p a n -> p (a n)")))
                nc.vector.tensor_copy(cw[:, :, :], cw_all[:, bass.ds(3 * h, 3), :]).then_inc(hs_ready, 1)
                dve.wait_ge(hs_ready, h + 1)

            def convolve(h, x, s):
                dve.wait_ge(center, 6 * h + (2 * x + s + 1))
                dst, src = qkv[:, x, s, :], ps[s]
                for n, tap in enumerate((0, 1, 3, 4)):
                    o = tap - TAPS // 2
                    a, b = max(0, -o), L - max(0, o)
                    ins = STT(dst[:, a:b], src[:, a + o:b + o], cw[:, x, tap:tap + 1], dst[:, a:b],
                              ALU.mult, ALU.add)
                    if n < 3:
                        step(ins)
                ins.then_inc(conv_done, 1)

            def bcast(ap):
                return ap.unsqueeze(1).to_broadcast([P, CH, P])

            def chunks(ap):
                return ap.rearrange("p (c n) -> p c n", c=CH)

            def delta_head(h, last_head):
                def normed_x(x):
                    for s in range(SEQS):
                        dve.wait_ge(rs_ready, 4 * h + (2 * x + s + 1))
                        TT(qkv[:, x, s, :], qkv[:, x, s, :], x_1[:, 2 * x + s, :], ALU.mult).then_inc(normed, 1)

                def log_decays(g):
                    s, d = g // 2, g % 2
                    dve.wait_ge(gc_done, 4 * h + (g + 1))
                    for cc in range(CH):
                        col = NEG_GC * 16 + d * 8 + s * CH + cc
                        ins = STT(tile(dt_[:, g, :], cc), tile(ps[4 + g], cc), hs[:, col:col + 1], negm[d],
                                  ALU.add, ALU.add)
                    ins.then_inc(dt_ready, 1)

                def lower(g):
                    s, d = g // 2, g % 2
                    dve.wait_ge(dt_exp, 4 * h + (g + 1))
                    dve.wait_ge(kk_done, 2 * h + (s + 1))
                    for cc in range(CH):
                        col = BETA * 16 + d * 8 + s * CH + cc
                        ins = STT(tile(m_t[:, g, :], cc), tile(ps[2 + s], cc), hs[:, col:col + 1],
                                  tile(dt_[:, g, :], cc), ALU.mult, ALU.mult)
                    ins.then_inc(m_ready, 1)

                def scores(g):
                    dve.wait_ge(kq_done, 2 * h + (g // 2 + 1))
                    TT(att[:, g, :], ps[4 + g // 2][:, :], dt_[:, g, :], ALU.mult).then_inc(att_ready, 1)

                def decayed_q(g):
                    dve.wait_ge(egr_ready, 4 * h + (g + 1))
                    TT(q_d[:, g, :], qkv[:, QX, g // 2, :], egr[:, g, :], ALU.mult).then_inc(qd_ready, 1)

                def eliminate():
                    halves = []
                    for d in range(2):
                        pt = slice(d * (P // 2), (d + 1) * (P // 2))
                        lo = blk[pt, :].rearrange("p (i j) -> p i j" if d == 0 else "p (j i) -> p i j", i=IB)
                        halves.append((pt, lo, inv[pt, d, :].rearrange("p (r c) -> p r c", c=IB)))
                    n = 0
                    for j in range(IB - 1):
                        rows, cols = IB - 1 - j, j + 1
                        for stage in range(2):
                            for d, (pt, lo, y) in enumerate(halves):
                                prod = outer[pt, 0:rows * cols].rearrange("p (r c) -> p r c", c=cols)
                                if n >= 2:
                                    dve.wait_ge(eliminated, ELIM_STEPS * h + (n - 1))
                                below = y[:, j + 1:IB, 0:cols]
                                if stage == 0:
                                    ins = TT(prod, lo[:, j + 1:IB, j:j + 1].to_broadcast([P // 2, rows, cols]),
                                             y[:, j:j + 1, 0:cols].to_broadcast([P // 2, rows, cols]), ALU.mult)
                                else:
                                    ins = TT(below, below, prod, ALU.subtract)
                                ins.then_inc(eliminated, 1)
                                n += 1
                    dve.wait_ge(eliminated, ELIM_STEPS * h + n)
                    for d, (pt, lo, y) in enumerate(halves):
                        step(nc.vector.tensor_copy(inv[pt, 1 - d, :].rearrange("p (r c) -> p r c", c=IB),
                                                   y.rearrange("p r c -> p c r")))

                def expand(m, g, out, landed, ready):
                    dve.wait_ge(landed, 16 * h + 16)
                    n = m * INST + inst(g, 0)
                    TT(out[:, g, :].rearrange("p (i b c) -> p i b c", i=CH, c=IB),
                       packed[:, n:n + CH, :].unsqueeze(2).to_broadcast([P, CH, P // IB, IB]),
                       same_block.rearrange("p (b c) -> p b c", c=IB).unsqueeze(1).to_broadcast([P, CH, P // IB, IB]),
                       ALU.mult).then_inc(ready, 1)

                for g in range(GROUPS):
                    log_decays(g)
                convolve(h, QX, 0)
                normed_x(KX)
                convolve(h, QX, 1)
                for g in range(GROUPS):
                    lower(g)
                for g in range(GROUPS):
                    dve.wait_ge(m_ready, 4 * h + (g + 1))
                    TT(chunks(u_t[:, g, :]), chunks(m_t[:, g, :]), bcast(same_block), ALU.mult).then_inc(masked, 1)
                convolve(h, VX, 0)
                for d in range(2):
                    pt = slice(d * (P // 2), (d + 1) * (P // 2))
                    step(nc.vector.tensor_copy(inv[pt, d, :], small_ident[pt, :]))
                normed_x(QX)
                dve.wait_ge(blocks_landed, 16 * h + 16)
                eliminate()
                dve.sem_inc(inv_ready, 1)
                convolve(h, VX, 1)
                dve.wait_ge(normed, 4 * h + 4)
                for g in range(GROUPS):
                    scores(g)
                for g in range(GROUPS):
                    decayed_q(g)
                for g in range(GROUPS):
                    dve.wait_ge(qd_ready, 4 * h + (g + 1))
                    expand(0, g, d_n, d_landed, d_ready)
                for g in range(GROUPS):
                    expand(1, g, u_t, u_landed, u_ready)
                dve.wait_ge(u_ready, 4 * h + 4)
                for lv in range(NL):
                    for g in range(GROUPS):
                        dve.wait_ge(x1_done, 4 * NL * h + (4 * lv + g + 1))
                        TT(chunks(x_1[:, g, :]), chunks(ps[2 * g]), bcast(lmask[lv]), ALU.mult).then_inc(x1_evac, 1)
                    for g in range(GROUPS):
                        dve.wait_ge(yy_done, 4 * NL * h + (4 * lv + g + 1))
                        if lv < NL - 1:
                            TT(d_n[:, g, :], d_n[:, g, :], ps[2 * g][:, :], ALU.subtract)
                        TT(u_t[:, g, :], u_t[:, g, :], ps[2 * g + 1][:, :], ALU.subtract).then_inc(ud_ready, 1)
                for k in range(CH):
                    if k:
                        for g in range(GROUPS):
                            s, d = g // 2, g % 2
                            cc = k if d == 0 else CH - 1 - k
                            col = NEG_EG * 16 + d * 8 + s * CH + cc
                            dve.wait_ge(p1_done, 12 * h + (4 * (k - 1) + g + 1))
                            STT(x_1[:, g, 0:P], ps[2 + g][:, 0:P], hs[:, col:col + 1], tile(vg_tok[:, s, :], cc),
                                ALU.mult, ALU.add).then_inc(r_ready, 1)
                    if k < CH - 1:
                        for g in range(GROUPS):
                            s, d = g // 2, g % 2
                            cc = k if d == 0 else CH - 1 - k
                            col = CDECAY * 16 + d * 8 + s * CH + cc
                            dve.wait_ge(su_done, 12 * h + (4 * k + g + 1))
                            if k == 0:
                                nc.vector.tensor_copy(d_n[:, g, 0:P], ps[2 + g][:, 2 * P:3 * P]).then_inc(s_ready, 1)
                            else:
                                dve.wait_ge(o_done, 12 * h + (4 * (k - 1) + g + 1))
                                STT(d_n[:, g, 0:P], d_n[:, g, 0:P], hs[:, col:col + 1], ps[2 + g][:, 2 * P:3 * P],
                                    ALU.mult, ALU.add).then_inc(s_ready, 1)
                if not last_head:
                    dve.wait_ge(vn_ready, 16 * h + 16)
                    head_constants(h + 1)
                    for s in range(SEQS):
                        convolve(h + 1, KX, s)
                for s in range(SEQS):
                    dve.wait_ge(ors_ready, 2 * h + (s + 1))
                    step(TT(o_sb[:, s, :], o_sb[:, s, :], x_1[:, s, :], ALU.mult))
                    dve.wait_ge(z_silu, 2 * h + (s + 1))
                    STT(mix[:, bass.ds(h + PAIRS, 1), s * L:(s + 1) * L].rearrange("p a n -> p (a n)"), o_sb[:, s, :],
                        nw[:, 0:1], z_s[:, s, :], ALU.mult, ALU.mult).then_inc(head_out, 1)
                dve.wait_ge(head_out, 2 * h + 3)

            head_constants(0)
            for s in range(SEQS):
                convolve(0, KX, s)
            base = step.base + step.n
            with dve.Fori(0, GH - 1) as h:
                step.enter(h, GDN_STEPS, base)
                delta_head(h, False)
            step.leave(GH - 1)
            delta_head(GH - 1, True)

            for k in range(KT):
                dve.wait_ge(mix_high, k + 1)
                TT(m_lo[:, k, :], mix[:, k, :], m_hi[:, k, :].bitcast(F32), ALU.subtract).then_inc(mix_ready, 1)
            dve.wait_ge(mix_ready, KT)
            with dve.Fori(0, KT) as m:
                for s in range(SEQS):
                    dst = mix[:, bass.ds(m, 1), s * L:(s + 1) * L].rearrange("p a n -> p (a n)")
                    dve.wait_ge(proj_done, 2 * m + (2 * OUT0 + s + 1))
                    STT(dst, x_hi[:, bass.ds(m, 1), s * L:(s + 1) * L].bitcast(F32).rearrange("p a n -> p (a n)"), ALPHA,
                        ps[s][:, :], ALU.mult, ALU.add).then_inc(res_read, 1)
                    dve.wait_ge(res_read, 2 * m + (s + 2))
                    STT(dst, x_lo[:, bass.ds(m, 1), s * L:(s + 1) * L].bitcast(F32).rearrange("p a n -> p (a n)"), ALPHA,
                        dst, ALU.mult, ALU.add).then_inc(z_ready, 1)
            dve.wait_ge(z_ready, 2 * KT)

            def norm_dve(z, rs, mean_s, centred_s, rs_s, out_s, b0, gi):
                for s in range(SEQS):
                    dve.wait_ge(mean_s, s + 1)
                    for k in range(KT):
                        zt = seq(z[:, k, :], s)
                        TT(zt, zt, ps[b0 + s][:, :], ALU.subtract).then_inc(centred_s, 1)
                dve.wait_ge(centred_s, SEQS * KT)
                for s in range(SEQS):
                    dve.wait_ge(rs_s, s + 1)
                    for k in range(KT):
                        zt = seq(z[:, k, :], s)
                        step(TT(zt, zt, rs[:, s, :], ALU.mult))
                        TS(zt, zt, ln_sb[:, gi, k:k + 1], ln_sb[:, gi + 1, k:k + 1], ALU.mult, ALU.add).then_inc(out_s, 1)

            norm_dve(mix, rs1, mean_done, centred, ln_rs, ln_out, 2, 0)
            for s in range(SEQS):
                for k in range(KT):
                    dve.wait_ge(x1_high, s * KT + k + 1)
                    TT(seq(x_lo[:, k, :], s), seq(mix[:, k, :], s), seq(x_hi[:, k, :], s).bitcast(F32),
                       ALU.subtract).then_inc(x1_ready, 1)

            def up(j):
                def convolve(x, s):
                    b = 2 * x + s
                    dve.wait_ge(up_center, 4 * j + (b + 1))
                    for o, tap in ((-1, 0), (1, 2)):
                        a, e = max(0, -o), L - max(0, o)
                        ins = STT(cv[:, b, a:e], ps[b][:, a + o:e + o],
                                  fw[:, bass.ds(2 * j + x, 1), tap:tap + 1].rearrange("p a b -> p (a b)"),
                                  cv[:, b, a:e], ALU.mult, ALU.add)
                        if tap == 0:
                            step(ins)
                    ins.then_inc(up_conv, 1)

                def product(s):
                    dve.wait_ge(up_silu, 2 * j + (s + 1))
                    dve.wait_ge(up_conv, 4 * j + (3 + s))
                    TT(act[:, bass.ds(j, 1), s * L:(s + 1) * L].rearrange("p a n -> p (a n)"), cv[:, s, :], cv[:, 2 + s, :],
                       ALU.mult).then_inc(up_act, 1)

                convolve(0, 0)
                convolve(0, 1)
                convolve(1, 0)
                product(0)
                convolve(1, 1)
                product(1)

            base = step.base + step.n
            with dve.Fori(0, FJ) as j:
                step.enter(j, 4, base)
                up(j)
            step.leave(FJ)
            dve.wait_ge(up_act, 2 * FJ)

            def low(j, jj, u):
                dve.wait_ge(a_high, j + 1)
                TT(a_lo[u][:, :], act[:, bass.ds(jj, 1), :].rearrange("p a n -> p (a n)") if not isinstance(jj, int)
                   else act[:, jj, :], a_hi[u][:, :].bitcast(F32), ALU.subtract).then_inc(a_ready, 1)

            def accumulated(q):
                for m in range(4):
                    for s in range(SEQS):
                        zt = seq(z_all[:, 4 * q + m, :], s)
                        if m == 0 and s == 0:
                            dve.wait_ge(proj_done, 2 * DOWN0 + FJ * (q + 1))
                        STT(zt, seq(x_hi[:, 4 * q + m, :], s).bitcast(F32), ALPHA, ps[2 * m + s][:, :],
                            ALU.mult, ALU.add).then_inc(acc_read, 1)
                dve.wait_ge(acc_read, 8 * (q + 1))
                for m in range(4):
                    for s in range(SEQS):
                        zt = seq(z_all[:, 4 * q + m, :], s)
                        STT(zt, seq(x_lo[:, 4 * q + m, :], s).bitcast(F32), ALPHA, zt, ALU.mult, ALU.add).then_inc(z2_ready, 1)

            with dve.Fori(0, FJ // 2) as i:
                for u in range(2):
                    low(2 * i + u, 2 * i + u, u)
            low(FJ, 0, 0)
            low(FJ + 1, 1, 1)
            accumulated(0)
            with dve.Fori(1, FJ // 2) as i:
                for u in range(2):
                    low(2 * i + (FJ + u), 2 * i + u, u)
            accumulated(1)
            dve.wait_ge(z2_ready, 16)
            norm_dve(z_all, rs2, mean2_done, centred2, ln2_rs, y_ready, 0, 2)


def build(nc, arrays):
    args = {name: nc.dram_tensor(name, a.shape, F32, kind="ExternalInput").ap() for name, a in arrays.items()}
    yT = nc.dram_tensor("yT", (KT, P, T), F32, kind="ExternalOutput").ap()
    block_dram = nc.dram_tensor("block_dram", (P, IB * IB), F32, kind="Internal").ap()
    inverse_dram = nc.dram_tensor("inverse_dram", (2, P, IB * IB), F32, kind="Internal").ap()
    encoder_layer(nc, yT=yT, block_dram=block_dram, inverse_dram=inverse_dram, **args)


def shape_constants():
    i = np.arange(P)
    parts = [np.eye(P), i[:, None] <= i[None, :], i[:, None] >= i[None, :], np.ones((P, P))]
    parts += [np.where(i[:, None] <= i[None, :], 0.0, NEG), np.where(i[:, None] >= i[None, :], 0.0, NEG)]
    for v in LEVELS:
        half = i >> v
        parts.append((half[:, None] ^ half[None, :]) == 1)
    parts.append(np.eye(P)[::-1])
    parts.append(i[:, None] // IB == i[None, :] // IB)
    parts.append(i[:, None] % IB == np.arange(IB)[None, :])
    parts.append(np.tile(np.eye(IB).reshape(1, -1), (P, 1)))
    consts = np.concatenate([p.astype(np.float32) for p in parts], axis=1)
    mask = np.zeros((P, len(SHIFTS), KEYS), np.float32)
    for t, sh in enumerate(SHIFTS):
        b = SHIFT.index(sh)
        qc = b * QB + np.arange(QB)
        start = np.clip(qc - WIN_C // 2, 0, GRID_W - WIN_C)
        kc = KC0[b] + np.arange(SPAN)
        seen = (kc[None, :] >= start[:, None]) & (kc[None, :] < start[:, None] + WIN_C)
        mask[:, t, :] = np.tile(np.where(seen, 0.0, NEG), (ROWS, ROWS))
    return consts, mask


def kernel(**inputs):
    import concourse.bacc as bacc
    from concourse.bass_utils import run_bass_kernel_spmd

    a = {n: np.asarray(v) for n, v in inputs.items()}
    x = np.concatenate([a["x_prompt"][0], a["x_sample"][0]], axis=0)
    w_in = a["w_in"][0]
    cuts = np.cumsum([0, 512, 512, 512, 512, 512, 512, 512, 16])

    def chunk(w):
        return w.reshape(KT, P, P).transpose(1, 0, 2).reshape(P, KT * P)

    def part(i, n):
        return chunk(w_in[:, cuts[i] + n * P:cuts[i] + (n + 1) * P])

    w_gate = np.zeros((D, P), np.float32)
    w_gate[:, 0:8] = w_in[:, cuts[7]:cuts[7] + 8]
    w_gate[:, 32:40] = w_in[:, cuts[7] + 8:cuts[7] + 16]
    gate_vec = np.zeros((P, 1), np.float32)
    gate_vec[32:40, 0] = a["gdn_dt_bias"][0].reshape(8)
    w_nat = np.stack([part(i, n) for n in range(PAIRS) for i in (1, 2, 0)])
    w_gdn = np.stack([part(i, h) for h in range(GH) for i in (4, 3, 5, 6)])
    w_out = np.stack([chunk(a["w_out"][0][:, m * P:(m + 1) * P]) for m in range(KT)])
    up = a["ffn_w_up"][0]
    w_up = np.stack([chunk(up[:, x0 + j * P:x0 + (j + 1) * P]) for j in range(FJ) for x0 in (0, FF)])
    w_down = a["ffn_w_down"][0].reshape(DPASS, 2, P, 2, 512).transpose(3, 0, 2, 1, 4).reshape(2 * DPASS, P, D)
    w_all = np.concatenate([chunk(w_gate)[None], w_nat, w_gdn, w_out, w_up, w_down], axis=0)
    rpb = np.zeros(NA_HEADS * DR * DC + 2 * PAD, np.float32)
    rpb[PAD:-PAD] = a["na_rpb"][0].reshape(-1)
    gconv = a["gdn_conv_w"][0].reshape(TAPS, 3, GH, P)[:, [1, 0, 2]].transpose(3, 2, 1, 0).reshape(P, 3 * GH, TAPS)
    fconv = np.concatenate([a["ffn_conv_w"][0], a["ffn_conv_b"]], axis=0)
    fconv = fconv.reshape(4, 2, FJ, P).transpose(3, 2, 1, 0).reshape(P, 2 * FJ, 4)
    ln = np.stack([a[n][0].reshape(KT, P) for n in ("ln1_g", "ln1_b", "ln2_g", "ln2_b")]).transpose(2, 0, 1)
    consts, nat_mask = shape_constants()
    arrays = {
        "xT": x.T.reshape(KT, P, T), "w_all": w_all, "rpb": rpb, "gdn_conv": gconv, "gate_vec": gate_vec,
        "a_log": a["gdn_a_log"][0].reshape(1, 8), "norm_w": a["gdn_norm_w"].reshape(P, 1), "ln_par": ln,
        "ffn_conv": fconv, "consts": consts, "nat_mask": nat_mask,
    }
    arrays = {n: np.ascontiguousarray(v) for n, v in arrays.items()}
    nc = bacc.Bacc("TRN2", target_bir_lowering=False, num_devices=1)
    build(nc, arrays)
    r = run_bass_kernel_spmd(nc, [arrays], core_ids=[0])
    y = r.results[0]["yT"].reshape(D, SEQS, L)
    return (np.ascontiguousarray(y[:, 0].T)[None], np.ascontiguousarray(y[:, 1].T)[None])
```

```python
import numpy as np
import concourse.bass as bass
from concourse import mybir
from concourse.alu_op_type import AluOpType as ALU

F32 = mybir.dt.float32
F32R = mybir.dt.float32r
ACT = mybir.ActivationFunctionType
AX = mybir.AxisListType

P = 128
D = 1024
SEQS, L = 2, 512
T = SEQS * L
KT = D // P
GRID_W, ROWS = 64, L // 64
NA_HEADS, HD = 8, 64
PAIRS = NA_HEADS // 2
WIN_R, WIN_C, QB = 8, 16, 16
SPAN = QB + WIN_C
BLOCKS = GRID_W // QB
KEYS = ROWS * SPAN
DC = 2 * WIN_C - 1
DR = 2 * WIN_R - 1
KC0 = [min(max(b * QB - WIN_C // 2, 0), GRID_W - SPAN) for b in range(BLOCKS)]
SHIFT = [KC0[b] - b * QB for b in range(BLOCKS)]
SHIFTS = sorted(set(SHIFT), reverse=True)
BIAS_RUN = (ROWS - 1) * DC + SPAN - SHIFTS[-1]
PAD = -SHIFTS[-1]
assert PAD == WIN_C
GH = 4
TAPS = 5
CH = L // P
GROUPS = 2 * SEQS
IB = 16
LEVELS = [v for v in range(7) if 1 << v >= IB]
NL = len(LEVELS)
UNITS = SEQS * BLOCKS
INST = GROUPS * CH
assert INST * (P // IB) == P
FF = 2816
FJ = FF // P
ALPHA = 2.0 ** 0.25
LN_EXP = "natural_log_exp_and_others"
FIRST_FILL = 6
LEVEL_FILL = 5
FILL = 2
LN_EPS, RMS_EPS = 1e-5, 1e-6
NEG = -1e30

GATE0 = 0
NAT0 = GATE0 + 1
GDN0 = NAT0 + 3 * PAIRS
OUT0 = GDN0 + 4 * GH
UP0 = OUT0 + KT
DOWN0 = UP0 + 2 * FJ
CHUNKS = DOWN0 + 2 * (FJ // 2)
DPASS = FJ // 2

GATE_COLS = 64
OUT_END = 2 * UP0
POOL_TILES = (2, 5)

BETA, NEG_EG, KAPPA, CDECAY, NEG_GC, GLOG = range(6)
HQ = 6 * 2 * SEQS * CH
GDN_STEPS = 31
ELIM_STEPS = 2 * (IB - 1)


def encoder_layer(nc, xT, w_gate, w_all, rpb, gdn_conv, gate_vec, a_log,
                  norm_w, ln_par, ffn_conv, consts, nat_mask, yT, block_dram, inverse_dram):
    from contextlib import ExitStack
    ctx = ExitStack()
    with ctx:
        arena = nc.sbuf_base
        top = nc.sbuf_usable_end
        arena = (arena + 63) // 64 * 64
        used = []

        def place(name, shape, dt, at):
            size = 4
            for n in shape[1:]:
                size *= n
            assert at + size <= top, (name, at + size - top)
            used.append((name, at, size))
            return nc.alloc_sbuf_tensor_at(name, shape, dt, offset=at), at + (size + 31) // 32 * 32

        ln_sb, at = place("ln_sb", [P, 4, KT], F32, arena)
        fw, at = place("fw", [P, 2 * FJ, 4], F32, at)
        one, at = place("one", [P, 1], F32, at)
        fw_j, at = place("fw_j", [P, 2, 4], F32, at)
        mean_w, at = place("mean_w", [P, P], F32, at)
        eps, at = place("eps", [P, 4], F32, at)
        x_hi, at_hi = place("x_hi", [P, KT, T], F32R, at)
        z_all, _ = place("z_all", [P, KT, T], F32, at)
        x_lo, at = place("x_lo", [P, KT, T], F32R, at_hi)
        w_raw, w_hi, w_lo = [], [], []
        for u in range(2):
            t, at = place(f"w_raw{u}", [P, D], F32, at)
            w_raw.append(t)
            t, at = place(f"w_hi{u}", [P, D], F32R, at)
            w_hi.append(t)
            t, at = place(f"w_lo{u}", [P, D], F32R, at)
            w_lo.append(t)
        mix0 = at
        mix, at = place("mix", [P, KT, T], F32, at)
        region = at
        cv, m = place("cv", [P, 4, L], F32, mix0)
        a_hi, a_lo = [], []
        for u in range(2):
            t, m = place(f"a_hi{u}", [P, T], F32R, m)
            a_hi.append(t)
            t, m = place(f"a_lo{u}", [P, T], F32R, m)
            a_lo.append(t)
        act, _ = place("act", [P, FJ, T], F32, m)
        c2, m2 = place("c2", [P, SEQS, L], F32, mix0)
        sum2, m2 = place("sum2", [P, SEQS, L], F32, m2)
        assert m2 <= mix0 + 4 * L * 4
        sq_last, _ = place("sq_last", [P, 4, SEQS, L], F32, m)
        sumsq2, m2 = place("sumsq2", [P, SEQS, L], F32, m + FJ * T * 4)
        sq2, m2 = place("sq2", [P, L], F32, m2)

        cst, at = place("cst", [P, consts.shape[1]], F32, region)
        sc, at = place("sc", [P, GH, HQ], F32, at)
        cw_all, at = place("cw_all", [P, 3 * GH, TAPS], F32, at)
        nw, at = place("nw", [P, 1], F32, at)
        mixer = at
        ident = cst[:, 0:P]
        tri = [cst[:, P:2 * P], cst[:, 2 * P:3 * P]]
        negm = [cst[:, 3 * P:4 * P], cst[:, 4 * P:5 * P]]
        lmask = [cst[:, (5 + v) * P:(6 + v) * P] for v in range(NL)]
        select = [cst[:, (5 + NL + v) * P:(6 + NL + v) * P] for v in range(NL)]
        turned_round = cst[:, (5 + 2 * NL) * P:(6 + 2 * NL) * P]
        same_block = cst[:, (6 + 2 * NL) * P:(7 + 2 * NL) * P]
        fold = cst[:, (7 + 2 * NL) * P:(7 + 2 * NL) * P + IB]
        small_select = cst[:, (7 + 2 * NL) * P + IB:(7 + 2 * NL) * P + 2 * IB]

        bm, at = place("bm", [P, len(SHIFTS), NA_HEADS, KEYS], F32, mixer)
        q_nat, at = place("q_nat", [P, SEQS, L], F32, at)
        k_nat, at = place("k_nat", [P, SEQS, L], F32, at)
        k_next, at = place("k_next", [P, SEQS, L], F32, at)
        v_nat, at = place("v_nat", [P, SEQS, BLOCKS, KEYS], F32, at)
        gT, _ = place("gT", [64, T], F32, at)
        v_tok, at = place("v_tok", [P, SEQS, BLOCKS, 2, P], F32, at)
        bw, _ = place("bw", [P, NA_HEADS, BIAS_RUN], F32, at)
        s_sb, p_sb, pt_sb, nmax, psum_row, rrow = [], [], [], [], [], []
        for u in range(2):
            for lst, nm, n in ((s_sb, "s_sb", 2 * KEYS), (p_sb, "p_sb", 2 * KEYS),
                               (pt_sb, "pt_sb", 2 * KEYS), (nmax, "nmax", 2),
                               (psum_row, "psum_row", 2), (rrow, "rrow", 2)):
                t, at = place(f"{nm}{u}", [P, n], F32, at)
                lst.append(t)
        nmask, at = place("nmask", [P, len(SHIFTS), KEYS], F32, at)
        gv, at = place("gv", [P, 1], F32, at)
        al, at = place("al", [P, 8], F32, at)
        NG = SEQS * CH
        ga, at = place("ga", [P, NG, 64], F32, at)
        gt_ = {}
        for nm in ("e1", "ab", "e2", "lp", "beta", "sp", "g", "dif", "kd"):
            gt_[nm], at = place("gs_" + nm, [P, NG, 8], F32, at)
        ea, at = place("ea", [P, 8], F32, at)
        gcs, at = place("gcs", [P, 2 * 8 * NG], F32, at)
        ecs, at = place("ecs", [P, 2 * 8 * NG], F32, at)

        qkv, at = place("qkv", [P, 3, SEQS, L], F32, mixer)
        k_tok, at = place("k_tok", [P, SEQS, L], F32, at)
        vg_tok, at = place("vg_tok", [P, SEQS, L], F32, at)
        att, at = place("att", [P, GROUPS, L], F32, at)
        m_t, at = place("m_t", [P, GROUPS, L], F32, at)
        o_sb = m_t
        u_t, at = place("u_t", [P, GROUPS, L], F32, at)
        d_n, at = place("d_n", [P, GROUPS, L], F32, at)
        x_1, at = place("x_1", [P, GROUPS, L], F32, at)
        q_d, at = place("q_d", [P, GROUPS, L], F32, at)
        dt_, egr = att, d_n
        z_s, at = place("z_s", [P, SEQS, L], F32, at)
        packed, at = place("packed", [P, 2 * INST, IB], F32, at)
        blk, at = place("blk", [P, IB * IB], F32, at)
        inv, at = place("inv", [P, 2, IB * IB], F32, at)
        outer, at = place("outer", [P, IB * IB // 4], F32, at)
        hs, at = place("hs", [P, HQ], F32, at)
        cw, at = place("cw", [P, 3, TAPS], F32, at)
        KX, QX, VX = 0, 1, 2

        at, m_hi, m_lo = region, [None] * KT, [None] * KT

        def place_part(lst, k, name):
            nonlocal at
            lst[k], at = place(f"{name}{k}", [P, T], F32R, at)

        place_part(m_hi, 7, "m_hi")
        place_part(m_lo, 7, "m_lo")
        at = mixer
        place_part(m_hi, 3, "m_hi")
        place_part(m_hi, 0, "m_hi")
        place_part(m_lo, 0, "m_lo")
        for k in (1, 2):
            place_part(m_hi, k, "m_hi")
            place_part(m_lo, k, "m_lo")
        for lst, k, name in ((m_hi, 6, "m_hi"), (m_lo, 6, "m_lo"),
                             (m_lo, 3, "m_lo"), (m_hi, 4, "m_hi"), (m_lo, 4, "m_lo"), (m_hi, 5, "m_hi"),
                             (m_lo, 5, "m_lo")):
            place_part(lst, k, name)
        assert all(t is not None for t in m_hi + m_lo)
        c1, at = place("c1", [P, SEQS, L], F32, at)
        sum1, at = place("sum1", [P, SEQS, L], F32, at)
        sumsq1, at = place("sumsq1", [P, SEQS, L], F32, at)
        sq1, at = place("sq1", [P, L], F32, at)
        t, at = place("w_hi2", [P, D], F32R, at)
        w_hi.append(t)
        t, at = place("w_lo2", [P, D], F32R, at)
        w_lo.append(t)

        banks = ctx.enter_context(nc.psum_tensor("banks", [P, 8, 512], F32))
        ps = [banks[:, b, :] for b in range(8)]

        names = []

        def sem(name):
            names.append(name)
            return ctx.enter_context(nc.semaphore(name))

        x_landed = [sem(f"x_landed{k}") for k in range(SEQS * KT)]
        cst_landed, gate_landed, bias_landed, al_landed = (sem("cst_landed"), sem("gate_landed"),
                                                           sem("bias_landed"), sem("al_landed"))
        par_landed = sem("par_landed")
        w_landed = [sem("w_landed0"), sem("w_landed1")]
        w_high, w_ready, proj_done = sem("w_high"), sem("w_ready"), sem("proj_done")
        x_high, x_ready = sem("x_high"), sem("x_ready")
        dstep, astep, eps_set = sem("dstep"), sem("astep"), sem("eps_set")
        bm_ready, bias_turned = sem("bm_ready"), sem("bias_turned")
        gate_tr, gate_tok, gate_soft, gate_g, gate_cum, gate_exp, sc_ready, g_e = (
            sem("gate_tr"), sem("gate_tok"), sem("gate_soft"), sem("gate_g"), sem("gate_cum"),
            sem("gate_exp"), sem("sc_ready"), sem("g_e"))
        k_copied = sem("k_copied")
        nat_evac, qk_done, s_biased, s_max, p_exp, p_ready = (
            sem("nat_evac"), sem("qk_done"), sem("s_biased"), sem("s_max"), sem("p_exp"), sem("p_ready"))
        vt_done, v_evac, pt_done, pt_evac, pv_done, o_evac = (
            sem("vt_done"), sem("v_evac"), sem("pt_done"), sem("pt_evac"), sem("pv_done"), sem("o_evac"))
        hs_ready, center, conv_done, silu_done, sq_done, nsum_done, rs_ready, normed = (
            sem("hs_ready"), sem("center"), sem("conv_done"), sem("silu_done"), sem("sq_done"),
            sem("nsum_done"), sem("rs_ready"), sem("normed"))
        ktr_done, k_tok_ready, vtr_done, vg_tok_ready, kk_done, kq_done, gc_done = (
            sem("ktr_done"), sem("k_tok_ready"), sem("vtr_done"), sem("vg_tok_ready"), sem("kk_done"),
            sem("kq_done"), sem("gc_done"))
        o_copied, masked, folded, fold_copied, blocks_stored, blocks_landed, eliminated = (
            sem("o_copied"), sem("masked"), sem("folded"), sem("fold_copied"), sem("blocks_stored"),
            sem("blocks_landed"), sem("eliminated"))
        inv_ready, inv_stored, d_landed, u_landed = (
            sem("inv_ready"), sem("inv_stored"), sem("d_landed"), sem("u_landed"))
        w_updated, v_updated = sem("w_updated"), sem("v_updated")
        joined_l, c_ready, r_selected, s_selected, expanded = (
            sem("joined_l"), sem("c_ready"), sem("r_selected"), sem("s_selected"), sem("expanded"))
        dt_ready, dt_exp, egr_ready, m_ready, att_ready, qd_ready = (
            sem("dt_ready"), sem("dt_exp"), sem("egr_ready"), sem("m_ready"), sem("att_ready"), sem("qd_ready"))
        x1_done, x1_evac, yy_done, ud_ready = sem("x1_done"), sem("x1_evac"), sem("yy_done"), sem("ud_ready")
        p1_done, r_ready, p2_done, vn_ready, su_done, s_ready, o_done = (
            sem("p1_done"), sem("r_ready"), sem("p2_done"), sem("vn_ready"), sem("su_done"),
            sem("s_ready"), sem("o_done"))
        osq_done, osum_done, ors_ready, z_silu, head_out = (
            sem("osq_done"), sem("osum_done"), sem("ors_ready"), sem("z_silu"), sem("head_out"))
        norm_ln, out_ln = sem("norm_ln"), sem("out_ln")
        var_ready, ln_step, rs_rows = sem("var_ready"), sem("ln_step"), sem("rs_rows")
        var_ready2, ln_step2, rs_rows2 = sem("var_ready2"), sem("ln_step2"), sem("rs_rows2")
        mix_high, mix_ready = sem("mix_high"), sem("mix_ready")
        z_first, shift_summed, shift_copied, d_ready1, squared, sq_added, stats_done, scaled = (
            sem("z_first"), sem("shift_summed"), sem("shift_copied"), sem("d_ready1"), sem("squared"),
            sem("sq_added"), sem("stats_done"), sem("scaled"))
        x1_scaled, x1_high, x1_ready, fw_copied, one_set = (
            sem("x1_scaled"), sem("x1_high"), sem("x1_ready"), sem("fw_copied"), sem("one_set"))
        acc_read, shift_summed2, shift_copied2, d_ready2, squared2, sq_added2, sq_last_ready = (
            sem("acc_read"), sem("shift_summed2"), sem("shift_copied2"), sem("d_ready2"), sem("squared2"),
            sem("sq_added2"), sem("sq_last_ready"))
        summed2, stats_done2, rows2_ready, scaled2, pool_step, pool_scaled, y_ready, y_stored = (
            sem("summed2"), sem("stats_done2"), sem("rows2_ready"), sem("scaled2"), sem("pool_step"),
            sem("pool_scaled"), sem("y_ready"), sem("y_stored"))
        up_center, up_conv, up_silu, up_act = sem("up_center"), sem("up_conv"), sem("up_silu"), sem("up_act")
        a_high, a_ready = sem("a_high"), sem("a_ready")

        def slot(c):
            return 2 if c == UP0 else (c - (c > UP0)) % 2

        def raw(c):
            return c % 2

        def seq(ap, s):
            return ap[:, s * L:(s + 1) * L]

        def flat(ap):
            return ap.rearrange("p a n -> p (a n)")

        def inst(g, cc):
            return (g % 2) * (INST // 2) + (g // 2) * CH + cc

        def v_bank(s):
            return 3 * s

        def z_bank(s):
            return 2 - s

        def c_at(lv):
            return 2 * (1 - lv % 2)

        def unit(n):
            return n // BLOCKS, n % BLOCKS

        class Chain:

            def __init__(self, eng, s):
                self.eng, self.s, self.n, self.base = eng, s, 0, 0

            def __call__(self, ins):
                self.n += 1
                ins.then_inc(self.s, 1)
                self.eng.wait_ge(self.s, self.base + self.n)

            def enter(self, i, per, first):
                self.base, self.n, self.first = first + i * per, 0, first
                self.per = per

            def leave(self, times):
                assert self.n == self.per, (self.n, self.per)
                self.base, self.n = self.first + times * self.per, 0

        block = ctx.enter_context(nc.Block())

        @block.sync
        def _(sp):
            def load(u, c):
                sp.wait_ge(w_ready, c - 1)
                sp.dma_start(w_raw[u][:, :], w_all[bass.ds(c - 1, 1), :, :].rearrange("a p n -> (a p) n")
                             ).then_inc(w_landed[u], 16)

            sp.dma_start(seq(mix[:, 0, :], 0), xT[0, :, 0:L]).then_inc(x_landed[0], 16)
            sp.dma_start(w_raw[0][:, 0:KT * GATE_COLS], w_gate).then_inc(w_landed[0], 16)
            for k in range(2, KT, 2):
                sp.dma_start(seq(mix[:, k, :], 0), xT[k, :, 0:L]).then_inc(x_landed[k], 16)
            sp.dma_start(w_raw[1][:, :], w_all[0, :, :]).then_inc(w_landed[1], 16)
            for k in range(KT):
                sp.dma_start(seq(mix[:, k, :], 1), xT[k, :, L:2 * L]).then_inc(x_landed[KT + k], 16)
            sp.dma_start(cst[:, :], consts).then_inc(cst_landed, 16)
            sp.dma_start(gv[:, :], gate_vec).then_inc(gate_landed, 16)

            def load_chunks(first, end):
                if (end - first) % 2:
                    load(raw(first), first)
                    first += 1
                with sp.Fori(0, (end - first) // 2) as i:
                    for u in range(2):
                        load(raw(first + u), 2 * i + (first + u))

            load(raw(2), 2)
            sp.dma_start(al[:, :], bass.AP(a_log.tensor, 0, [[0, P], [1, 8]])
                            ).then_inc(al_landed, 16)
            for r in range(ROWS):
                src = bass.AP(rpb.tensor, r * DC, [[1, QB], [DR * DC, NA_HEADS], [1, BIAS_RUN]])
                sp.dma_start(bw[r * QB:(r + 1) * QB, :, :], src).then_inc(bias_landed, 16)
            sp.dma_start(nmask[:, :, :], nat_mask).then_inc(bias_landed, 16)
            sp.dma_start(cw_all[:, :, :], gdn_conv).then_inc(par_landed, 16)
            sp.dma_start(nw[:, :], norm_w).then_inc(par_landed, 16)
            sp.dma_start(ln_sb[:, :, :], ln_par).then_inc(par_landed, 16)
            sp.dma_start(fw[:, :, :], ffn_conv).then_inc(par_landed, 16)
            load_chunks(3, GDN0 + 6)
            with sp.Fori(0, GH) as h:
                sp.wait_ge(fold_copied, h + 1)
                sp.dma_start(block_dram.rearrange("(i b) (r c) -> (b r) i c", b=P // IB, c=IB), packed[:, 0:INST // 2, :]
                             ).then_inc(blocks_stored, 16)
                sp.wait_ge(blocks_stored, 16 * h + 16)
                half = P // 2
                sp.dma_start(packed[half:P, INST:2 * INST, :].rearrange("p i c -> p (i c)"), block_dram
                             ).then_inc(blocks_landed, 16)
                sp.dma_start(blk[0:half, :], block_dram).then_inc(blocks_landed, 16)
                load(raw(GDN0 + 6), 4 * h + (GDN0 + 6))
                sp.wait_ge(inv_ready, h + 1)
                sp.dma_start(inverse_dram.rearrange("m k n -> k m n"), inv[:, :, :]).then_inc(inv_stored, 16)
                sp.wait_ge(inv_stored, 16 * h + 16)
                for m, landed in enumerate((d_landed, u_landed)):
                    for d in range(2):
                        i0 = d * (INST // 2)
                        rows = inverse_dram[m ^ d, :, :].rearrange("(i b) (r c) -> (b r) i c", b=P // IB, c=IB)
                        sp.dma_start(packed[:, m * INST + i0:m * INST + i0 + INST // 2, :],
                                     rows[:, i0:i0 + INST // 2, :]).then_inc(landed, 16)
                for n in range(7, 10):
                    load(raw(GDN0 + n), 4 * h + (GDN0 + n))
            load_chunks(GDN0 + 4 * GH + 6, CHUNKS)
            for s in range(SEQS):
                for k in range(KT):
                    sp.wait_ge(y_ready, s * KT + k + 1)
                    sp.dma_start(yT[k, :, s * L:(s + 1) * L], seq(z_all[:, k, :], s)).then_inc(y_stored, 16)
            sp.wait_ge(y_stored, 16 * SEQS * KT)
            sp.wait_ge(d_landed, 32 * GH)
            sp.wait_ge(u_landed, 32 * GH)

        @block.gpsimd
        def _(pool):
            def split(c, ru, u, landed, free, n=D):
                pool.wait_ge(w_landed[ru], landed)
                if free is not None:
                    pool.wait_ge(proj_done, free)
                nc.gpsimd.tensor_tensor(w_hi[u][:, 0:n], w_raw[ru][:, 0:n], one[:, :].to_broadcast([P, n]),
                                        ALU.mult).then_inc(w_high, 1)
                pool.wait_ge(w_high, c + 1)
                nc.gpsimd.tensor_tensor(w_lo[u][:, 0:n], w_raw[ru][:, 0:n], w_hi[u][:, 0:n].bitcast(F32),
                                        ALU.subtract).then_inc(w_ready, 1)

            def split_one(c, free):
                split(c, raw(c), slot(c), 16 * (c // 2 + 1), free)

            def split_chunks(first, end):
                if (end - first) % 2:
                    split_one(first, 2 * first - 2)
                    first += 1
                with pool.Fori(0, (end - first) // 2) as i:
                    for u in range(2):
                        c = first + u
                        split(2 * i + c, raw(c), slot(c), 16 * i + 16 * (c // 2 + 1), 4 * i + (2 * c - 2))

            def low_x1(s):
                for k in range(KT):
                    pool.wait_ge(x1_high, s * KT + k + 1)
                    nc.gpsimd.tensor_tensor(seq(x_lo[:, k, :], s), seq(mix[:, k, :], s),
                                            seq(x_hi[:, k, :], s).bitcast(F32), ALU.subtract).then_inc(x1_ready, 1)

            nc.gpsimd.memset(one[:, :], 1.0).then_inc(one_set, 1)
            pool.wait_ge(one_set, 1)
            split(0, 0, 0, 16, None, KT * GATE_COLS)
            split_one(1, None)
            split_chunks(2, UP0)
            split_one(UP0, None)
            split_one(UP0 + 1, OUT_END - 1)
            low_x1(0)
            split_one(UP0 + 2, OUT_END)
            low_x1(1)
            split_chunks(UP0 + 3, CHUNKS)
            for s in range(SEQS):
                pool.wait_ge(rows2_ready, s + 1)
                for k in POOL_TILES:
                    zt = seq(z_all[:, k, :], s)
                    nc.gpsimd.tensor_tensor(zt, zt, sumsq2[:, s, :], ALU.mult).then_inc(pool_step, 1)
                    pool.wait_ge(pool_step, s * len(POOL_TILES) + POOL_TILES.index(k) + 1)
                    nc.gpsimd.tensor_tensor(zt, zt, sum2[:, s, :], ALU.subtract).then_inc(pool_scaled, 1)

        @block.tensor
        def _(pe):
            mm = nc.tensor.matmul

            def project(bank, u, s, xh=None, xl=None, wait_k=None, cols=P):
                xh = x_hi if xh is None else xh
                xl = x_lo if xl is None else xl
                n = 0
                for k in range(KT):
                    if wait_k is not None:
                        wait_k(k)
                    for w, x in ((w_hi, xh), (w_hi, xl), (w_lo, xh)):
                        last = mm(ps[bank][0:cols, :], w[u][:, k * cols:(k + 1) * cols], seq(x[:, k, :], s),
                                  start=n == 0, stop=n == 3 * KT - 1)
                        n += 1
                last.then_inc(proj_done, 1)

            class Filler:

                def __init__(self, chunks, free):
                    self.todo = [(j, c, u, s) for j, (c, u) in enumerate(chunks) for s in range(SEQS)]
                    self.free, self.n = free, 0

                def __call__(self, count):
                    for _ in range(count):
                        at, i = divmod(self.n, 3 * KT)
                        if at == len(self.todo):
                            return
                        j, c, u, s = self.todo[at]
                        if i == 0:
                            if s == 0:
                                pe.wait_ge(w_ready, c + 1)
                            self.free(j, s)
                        k, part = divmod(i, 3)
                        w, x = ((w_hi, x_hi), (w_hi, x_lo), (w_lo, x_hi))[part]
                        ins = mm(ps[s][:, :], w[u][:, k * P:(k + 1) * P], seq(x[:, k, :], s),
                                 start=i == 0, stop=i == 3 * KT - 1)
                        if i == 3 * KT - 1:
                            ins.then_inc(proj_done, 1)
                        self.n += 1

                def finish(self):
                    self(3 * KT * len(self.todo) - self.n)

            def nat_filler(pair, n, u0):
                return Filler([(3 * pair + (NAT0 + j), slot(u0 + j)) for j in range(n)],
                              lambda j, s: pe.wait_ge(nat_evac, 6 * pair + (2 * j + s + 1)))

            pe.wait_ge(w_ready, 1)
            for s in range(SEQS):
                project(s, 0, s, wait_k=lambda k, s=s: pe.wait_ge(x_ready, s * KT + k + 1),
                        cols=GATE_COLS)
            fill = nat_filler(0, 3, NAT0)
            fill(3 * KT)
            pe.wait_ge(cst_landed, 16)
            pe.wait_ge(nat_evac, 2)
            for t in range(NG):
                last = nc.tensor.transpose(ps[2][:, t * 64:(t + 1) * 64], gT[:, t * P:(t + 1) * P],
                                           ident[0:64, 0:64])
            last.then_inc(gate_tr, 1)
            fill(3 * KT)
            pe.wait_ge(bias_landed, 16 * (ROWS + 1))
            for hh in range(NA_HEADS):
                if hh == 4:
                    fill(3 * KT)
                    pe.wait_ge(gate_g, 1)
                    for d in range(2):
                        mm(ps[3][:, d * 4 * NG:(d + 1) * 4 * NG].rearrange("p (t h) -> p t h", h=4),
                           tri[d], gt_["g"][:, :, 4 * d:4 * d + 4], start=True, stop=True)
                    mm(ps[3][:, 8 * NG:16 * NG], mean_w[:, :], flat(gt_["g"][:, :, :]), start=True, stop=True
                       ).then_inc(gate_cum, 1)
                    fill(3 * KT)
                if hh >= 4:
                    pe.wait_ge(bm_ready, len(SHIFTS) * (hh - 3))
                mm(ps[4 + hh % 4][:, 0:BIAS_RUN], turned_round, bw[:, hh, :], start=True, stop=True).then_inc(bias_turned, 1)
            fill.finish()
            pe.wait_ge(gate_exp, 1)
            pe.wait_ge(bm_ready, len(SHIFTS) * NA_HEADS)

            def turn_values(pair, n):
                s, half = n // 2, n % 2
                pe.wait_ge(nat_evac, 6 * pair + (5 + s))
                if s == 0:
                    pe.wait_ge(o_evac, 2 * pair + 1)
                else:
                    pe.wait_ge(v_evac, 4 * pair + (n - 1))
                for b in (2 * half, 2 * half + 1):
                    for kt in range(2):
                        keys = v_nat[:, s, b, kt * P:(kt + 1) * P]
                        last = nc.tensor.transpose(ps[6 + half][:, ((b % 2) * 2 + kt) * P:((b % 2) * 2 + kt + 1) * P],
                                                   keys, ident)
                last.then_inc(vt_done, 1)

            def attend(pair, odd, last_pair):
                following = 1 if last_pair else 3
                fill = nat_filler(pair + 1, following, NAT0 + 3 * (odd + 1))
                per = following * SEQS * 3 * KT // (UNITS + 1)
                scores(pair, 0)
                fill(per)
                scores(pair, 1)
                turn_values(pair, 0)
                turn_values(pair, 1)
                fill(per)
                turn_values(pair, 2)
                turn_values(pair, 3)
                for n in range(2, UNITS + 3):
                    if n < UNITS:
                        scores(pair, n)
                    fill(per)
                    if n == UNITS:
                        fill.finish()
                    if n - 2 < UNITS:
                        turn(pair, n - 2)
                    if n >= 3:
                        values(pair, n - 3)

            def scores(pair, n):
                s, b = unit(n)
                if b == 0:
                    pe.wait_ge(nat_evac, 6 * pair + (7 + s))
                    pe.wait_ge(k_copied, 2 * pair + (s + 1))
                if n:
                    pe.wait_ge(s_biased, 8 * pair + n)
                for h in range(2):
                    keys = k_nat[64 * h:64 * h + 64, s, :].rearrange("p (r c) -> p r c", c=GRID_W)[
                        :, :, KC0[b]:KC0[b] + SPAN]
                    last = mm(ps[2 + h][:, 0:KEYS].rearrange("p (r c) -> p r c", c=SPAN),
                              q_nat[64 * h:64 * h + 64, s, b * P:(b + 1) * P], keys, start=True, stop=True)
                last.then_inc(qk_done, 1)

            def turn(pair, n):
                pe.wait_ge(p_ready, 8 * pair + (n + 1))
                if n >= 2:
                    pe.wait_ge(pt_evac, 8 * pair + (n - 1))
                for j in range(4):
                    last = nc.tensor.transpose(ps[4 + n % 2][:, j * P:(j + 1) * P],
                                               p_sb[n % 2][:, j * P:(j + 1) * P], ident)
                last.then_inc(pt_done, 1)

            def values(pair, n):
                s, b = unit(n)
                pe.wait_ge(pt_evac, 8 * pair + (n + 1))
                if n == 0:
                    pe.wait_ge(v_evac, 4 * pair + 4)
                for h in range(2):
                    for kt in range(2):
                        last = mm(ps[6 + s][64 * h:64 * h + 64, b * P:(b + 1) * P],
                                  v_tok[:, s, b, kt, 64 * h:64 * h + 64],
                                  pt_sb[n % 2][:, (2 * h + kt) * P:(2 * h + kt + 1) * P],
                                  start=kt == 0, stop=kt == 1)
                last.then_inc(pv_done, 1)

            with pe.Fori(0, PAIRS // 2 - 1) as i:
                for odd in range(2):
                    attend(2 * i + odd, odd, False)
            attend(PAIRS - 2, 0, False)
            attend(PAIRS - 1, 1, True)

            pe.wait_ge(o_evac, 2 * PAIRS + 1)

            def tile(ap, c):
                return ap[:, c * P:(c + 1) * P]

            def norm_sum(h, x, s):
                pe.wait_ge(sq_done, 4 * h + (2 * x + s + 1))
                mm(ps[2 + 2 * x + s][:, :], mean_w[:, :], q_d[:, 2 * x + s, :], start=True, stop=True).then_inc(nsum_done, 1)

            def delta_head(h, last_head):
                c = 4 * h + GDN0

                def cumulate(g):
                    s, d = g // 2, g % 2
                    if g >= 2:
                        pe.wait_ge(o_copied, 2 * h + (g - 1))
                    for cc in range(CH):
                        col = GLOG * 16 + d * 8 + s * CH + cc
                        ins = mm(tile(ps[4 + g], cc), hs[:, col:col + 1].to_broadcast([P, P]), tri[d],
                                 start=True, stop=True)
                    ins.then_inc(gc_done, 1)

                def cumulated(g):
                    pe.wait_ge(dt_ready, 4 * h + (g + 1))
                    pe.wait_ge(egr_ready, 4 * h + (g + 1))

                pe.wait_ge(hs_ready, h + 1)
                for g in range(GROUPS):
                    cumulate(g)
                pe.wait_ge(w_ready, c + 2)
                pe.wait_ge(conv_done, 6 * h + 1)
                project(0, slot(GDN0 + 1), 0)
                norm_sum(h, KX, 0)
                norm_sum(h, KX, 1)
                pe.wait_ge(conv_done, 6 * h + 2)
                project(1, slot(GDN0 + 1), 1)
                for s in range(SEQS):
                    pe.wait_ge(normed, 4 * h + (s + 1))
                    for cc in range(CH):
                        kc = tile(qkv[:, KX, s, :], cc)
                        ins = mm(tile(ps[2 + s], cc), kc, kc, start=True, stop=True)
                    ins.then_inc(kk_done, 1)
                for s in range(SEQS):
                    cumulated(2 + s)
                    for cc in range(CH):
                        ins = nc.tensor.transpose(tile(ps[6 + s], cc), tile(qkv[:, KX, s, :], cc), ident)
                    ins.then_inc(ktr_done, 1)
                pe.wait_ge(w_ready, c + 3)
                pe.wait_ge(conv_done, 6 * h + 3)
                project(0, slot(GDN0 + 2), 0)
                cumulated(0)
                norm_sum(h, QX, 0)
                pe.wait_ge(k_tok_ready, 2 * h + 1)
                for s in range(SEQS):
                    pe.wait_ge(masked, 2 * h + (s + 1))
                    for cc in range(CH):
                        n = s * CH + cc
                        ins = mm(ps[6][:, n * IB:(n + 1) * IB], tile(u_t[:, s, :], cc), fold, start=True, stop=True)
                ins.then_inc(folded, 1)
                pe.wait_ge(m_ready, 4 * h + 4)
                project(v_bank(1), slot(GDN0 + 2), 1)
                cumulated(1)
                norm_sum(h, QX, 1)
                pe.wait_ge(w_ready, c + 4)
                for s in range(SEQS):
                    if s:
                        pe.wait_ge(conv_done, 6 * h + 4)
                    project(z_bank(s), slot(GDN0 + 3), s)
                    if s == 0:
                        for sk in range(SEQS):
                            pe.wait_ge(normed, 4 * h + (2 + sk + 1))
                            for cc in range(CH):
                                ins = mm(tile(ps[4 + sk], cc), tile(qkv[:, KX, sk, :], cc), tile(qkv[:, QX, sk, :], cc),
                                         start=True, stop=True)
                            ins.then_inc(kq_done, 1)
                for s in range(SEQS):
                    pe.wait_ge(silu_done, 6 * h + (4 + s + 1))
                    if s == 0:
                        pe.wait_ge(k_tok_ready, 2 * h + 2)
                    else:
                        pe.wait_ge(fold_copied, h + 1)
                    for cc in range(CH):
                        ins = nc.tensor.transpose(tile(ps[7 - s], cc), tile(qkv[:, VX, s, :], cc), ident)
                    ins.then_inc(vtr_done, 1)
                fill = Filler([] if last_head else [(c + 4, slot(GDN0))],
                              lambda j, s: pe.wait_ge(z_silu, 2 * h + 2) if s else pe.wait_ge(conv_done, 6 * h + 5))
                fill(FIRST_FILL)
                for lv in range(NL):
                    for s in range(SEQS):
                        n = 2 * NL * h + (2 * lv + s + 1)
                        pe.wait_ge(c_ready, n)
                        pe.wait_ge(r_selected, n)
                        if lv == 0:
                            if s:
                                pe.wait_ge(conv_done, 6 * h + 6)
                            else:
                                pe.wait_ge(z_silu, 2 * h + 1)
                        for cc in range(CH):
                            ins = mm(tile(ps[2 + s], cc), tile(u_t[:, c_at(lv) + s, :], cc), tile(x_1[:, 2 + s, :], cc),
                                     start=True, stop=True)
                        ins.then_inc(x1_done, 1)
                    fill(LEVEL_FILL)
                    for s in range(SEQS):
                        n = 2 * NL * h + (2 * lv + s + 1)
                        pe.wait_ge(x1_evac, n)
                        pe.wait_ge(s_selected, n)
                        if lv == 0:
                            pe.wait_ge(att_ready, 4 * h + (2 * s + 2))
                            pe.wait_ge(vg_tok_ready, 2 * h + 2)
                        if lv < NL - 1:
                            for cc in range(CH):
                                mm(tile(ps[4 + s], cc), tile(m_t[:, 2 * s + 1, :], cc), tile(x_1[:, s, :], cc),
                                   start=True, stop=True)
                        for cc in range(CH):
                            ins = mm(tile(ps[6 + s], cc), tile(x_1[:, s, :], cc), tile(m_t[:, 2 * s + 1, :], cc),
                                     start=True, stop=True)
                        ins.then_inc(yy_done, 1)
                    fill(LEVEL_FILL)

                for k in range(CH):
                    def at_chunk(g):
                        return k if g % 2 == 0 else CH - 1 - k
                    if k:
                        for g in range(GROUPS):
                            pe.wait_ge(s_ready, 12 * h + (4 * (k - 1) + g + 1))
                            mm(ps[2 + g][:, 0:P], tile(qkv[:, KX, g // 2, :], at_chunk(g)), d_n[:, g, 0:P],
                               start=True, stop=True).then_inc(p1_done, 1)
                        fill(FILL)
                    for g in range(GROUPS):
                        if k:
                            pe.wait_ge(r_ready, 12 * h + (4 * (k - 1) + g + 1))
                            rhs = x_1[:, g, 0:P]
                        else:
                            pe.wait_ge(ud_ready, 4 * h + (g + 1))
                            rhs = tile(vg_tok[:, g // 2, :], at_chunk(g))
                        mm(ps[2 + g][:, P:2 * P], tile(u_t[:, g, :], at_chunk(g)), rhs,
                           start=True, stop=True).then_inc(p2_done, 1)
                    fill(FILL)
                    for g in range(GROUPS):
                        cc = at_chunk(g)
                        out = tile(ps[6 + g // 2], cc)
                        pe.wait_ge(vn_ready, 16 * h + (4 * k + g + 1))
                        if k < CH - 1:
                            mm(ps[2 + g][:, 2 * P:3 * P], tile(k_tok[:, g // 2, :], cc), x_1[:, g, 2 * P:3 * P],
                               start=True, stop=True).then_inc(su_done, 1)
                        if k:
                            mm(out, d_n[:, g, 0:P], tile(q_d[:, g, :], cc), start=False, stop=False)
                        elif g == 0:
                            pe.wait_ge(qd_ready, 4 * h + 4)
                        ins = mm(out, x_1[:, g, P:2 * P], tile(att[:, g, :], cc), start=k == 0 and g % 2 == 0,
                                 stop=k == CH - 1 and g % 2 == 1)
                        if k:
                            ins.then_inc(o_done, 1)
                    if k < CH - 1:
                        fill(FILL)
                fill.finish()
                for s in range(SEQS):
                    pe.wait_ge(osq_done, 2 * h + (s + 1))
                    mm(ps[2 + s][:, :], mean_w[:, :], q_d[:, s, :], start=True, stop=True).then_inc(osum_done, 1)

            with pe.Fori(0, GH - 1) as h:
                delta_head(h, False)
            delta_head(GH - 1, True)


            def output_product(bank, u, s, k):
                for n, (w, x) in enumerate(((w_hi, m_hi), (w_hi, m_lo), (w_lo, m_hi))):
                    ins = mm(ps[bank][:, :], w[u][:, k * P:(k + 1) * P], seq(x[k], s),
                             start=k == 0 and n == 0, stop=k == KT - 1 and n == 2)
                return ins

            def output(m, u, s, bank):
                if s == 0:
                    pe.wait_ge(w_ready, m + (OUT0 + 1))
                for k in range(KT):
                    ins = output_product(bank, u, s, k)
                ins.then_inc(proj_done, 1)

            pe.wait_ge(w_ready, OUT0 + 2)
            for k in range(KT):
                pe.wait_ge(mix_ready, k + 1)
                for m in range(2):
                    for s in range(SEQS):
                        ins = output_product(4 * m + s, slot(OUT0 + m), s, k)
                        if k == KT - 1:
                            ins.then_inc(proj_done, 1)
            for s in range(SEQS):
                pe.wait_ge(z_first, s + 1)
                mm(ps[2 + s][:, :], mean_w[:, :], seq(mix[:, 0, :], s), start=True, stop=True).then_inc(shift_summed, 1)
            with pe.Fori(1, KT // 2 - 1) as i:
                for u in range(2):
                    for s in range(SEQS):
                        pe.wait_ge(d_ready1, 4 * i + (2 * u + s - 3))
                        output(2 * i + u, slot(OUT0 + u), s, 4 * u + s)
            out6, out7 = (KT - 2, slot(OUT0 + KT - 2)), (KT - 1, slot(OUT0 + KT - 1))
            output(*out6, 0, 6)
            output(*out7, 0, 7)
            pe.wait_ge(d_ready1, 2 * (KT - 2))
            output(*out6, 1, 4)

            def norm_stats(s):
                pe.wait_ge(sq_added, 2 * (KT - 1) - 2 * (1 - s))
                mm(ps[6 - 2 * s][:, :], mean_w[:, :], sum1[:, s, :], start=True, stop=True)
                mm(ps[7 - 2 * s][:, :], mean_w[:, :], sumsq1[:, s, :], start=True, stop=True).then_inc(stats_done, 1)

            norm_stats(0)
            output(*out7, 1, 5)

            def first_up():
                for s in range(SEQS):
                    for x in range(2):
                        c = UP0 + x
                        if s == 0:
                            pe.wait_ge(w_ready, c + 1)

                        def wait_k(k):
                            if x == 0:
                                pe.wait_ge(x1_ready, s * KT + k + 1)
                                if s == 0 and k == 3:
                                    norm_stats(1)
                        project(2 * x + s, slot(c), s, wait_k=wait_k)

            def up(j):
                for x in range(2):
                    c = 2 * j + (UP0 + x)
                    pe.wait_ge(w_ready, c + 1)
                    for s in range(SEQS):
                        b = 2 * x + s
                        pe.wait_ge(up_conv, 4 * j + (b - 3))
                        project(b, slot(UP0 + 2 + x), s)

            first_up()
            with pe.Fori(1, FJ) as j:
                up(j)

            def down_products(m, s, t, u, start, stop):
                for n, (w, a) in enumerate(((w_hi, a_hi), (w_hi, a_lo), (w_lo, a_hi))):
                    ins = mm(ps[2 * m + s][:, :], w[u][:, t * 512 + m * P:t * 512 + (m + 1) * P],
                             seq(a[t], s), start=start and n == 0, stop=stop and n == 2)
                return ins

            def down(q, cc, c, u, first=False):
                pe.wait_ge(w_ready, c + 1)
                for t in range(2):
                    pe.wait_ge(a_ready, 2 * cc + (q * FJ + t + 1))
                    again = first and t == 0 and q
                    starts = first and t == 0 and q == 0
                    for m in (2, 3, 0, 1) if starts else range(4):
                        if starts and m < 2:
                            pe.wait_ge(up_conv, 4 * FJ - 2 + 2 * m)
                        if again and m == 3:
                            pe.wait_ge(acc_read, 8)
                            for s in range(SEQS):
                                mm(ps[6 + s][:, :], mean_w[:, :], seq(z_all[:, 0, :], s), start=True, stop=True
                                   ).then_inc(shift_summed2, 1)
                        for s in range(SEQS):
                            if again and m < 3:
                                pe.wait_ge(acc_read, 2 * m + s + 1)
                            elif again:
                                pe.wait_ge(shift_copied2, s + 1)
                            ins = down_products(m, s, t, u, first and t == 0, False)
                    ins.then_inc(proj_done, 1)

            def last_down(q, cc, c, u):
                if q == 0:
                    pe.wait_ge(w_ready, c + 1)
                    for t in range(2):
                        pe.wait_ge(a_ready, 2 * cc + t + 1)
                        for m in range(4):
                            for s in range(SEQS):
                                ins = down_products(m, s, t, u, False, t == 1)
                        ins.then_inc(proj_done, 1)
                    return
                pe.wait_ge(w_ready, c + 1)
                pe.wait_ge(a_ready, 2 * FJ)
                for s in range(SEQS):
                    for t in range(2):
                        for m in range(4):
                            ins = down_products(m, s, t, u, False, t == 1)
                            if t == 1:
                                ins.then_inc(proj_done, 1)

            for q in range(2):
                c0 = DOWN0 + q * DPASS
                down(q, 0, c0, slot(c0), first=True)
                with pe.Fori(0, (DPASS - 3) // 2) as i:
                    for u in range(2):
                        down(q, 2 * i + (1 + u), 2 * i + (c0 + 1 + u), slot(c0 + 1 + u))
                down(q, DPASS - 2, c0 + DPASS - 2, slot(c0 + DPASS - 2))
                last_down(q, DPASS - 1, c0 + DPASS - 1, slot(c0 + DPASS - 1))

            for s in range(SEQS):
                pe.wait_ge(summed2, 4 * (s + 1))
                pe.wait_ge(sq_added2, 9)
                mm(ps[s][:, :], mean_w[:, :], sum2[:, s, :], start=True, stop=True)
                mm(ps[2 + s][:, :], mean_w[:, :], sumsq2[:, s, :], start=True, stop=False)
                for m in range(4):
                    pe.wait_ge(sq_last_ready, 4 * s + m + 1)
                    last = mm(ps[2 + s][:, :], mean_w[:, :], sq_last[:, m, s, :], start=False, stop=m == 3)
                last.then_inc(stats_done2, 1)

        @block.scalar
        def _(act_e):
            A = nc.scalar.activation
            for k in range(1, KT, 2):
                act_e.dma_start(seq(mix[:, k, :], 0), xT[k, :, 0:L]).then_inc(x_landed[k], 16)

            def high_x(n):
                s, k = divmod(n, KT)
                act_e.wait_ge(x_landed[n], 16)
                nc.scalar.copy(seq(x_hi[:, k, :], s), seq(mix[:, k, :], s)).then_inc(x_high, 1)

            for n in range(SEQS * KT):
                high_x(n)

            def projected(pair, n):
                j, s = divmod(n, SEQS)
                act_e.wait_ge(proj_done, 6 * pair + (2 * (NAT0 + j) + s + 1))
                if j == 0:
                    nc.scalar.copy(k_next[:, s, :], ps[s][:, :]).then_inc(nat_evac, 1)
                elif j == 1:
                    for b, d in ((0, 3), (1, 1)):
                        src = bass.AP(ps[s].tensor, s * 512 + KC0[b],
                                      [[8 * 512, P], [KC0[b + d] - KC0[b], 2], [GRID_W, ROWS], [1, SPAN]])
                        ins = nc.scalar.copy(v_nat[:, s, b:b + d + 1:d, :].rearrange(
                            "p b (r c) -> p b r c", c=SPAN), src)
                    ins.then_inc(nat_evac, 1)
                else:
                    out = q_nat[:, s, :].rearrange("p (b r c) -> p r b c", b=BLOCKS, r=ROWS)
                    A(out, ps[s][:, :].rearrange("p (r b c) -> p r b c", r=ROWS, b=BLOCKS), ACT.Copy,
                      scale=HD ** -0.5).then_inc(nat_evac, 1)

            act_e.wait_ge(gate_landed, 16)
            for s in range(SEQS):
                act_e.wait_ge(proj_done, s + 1)
                A(seq(gT, s), ps[s][0:64, :], ACT.Identity, bias=gv[0:64, 0:1]).then_inc(nat_evac, 1)
            projected(0, 0)
            act_e.wait_ge(gate_tr, 1)
            nc.scalar.copy(flat(ga[:, :, :]), ps[2][:, :]).then_inc(gate_tok, 1)
            act_e.wait_ge(gate_tok, 1)
            step = Chain(act_e, astep)
            step(A(gt_["e1"][:, :, :], ga[:, :, 0:8], ACT.Exp, scale=-1.0))
            step(A(gt_["ab"][:, :, :], ga[:, :, 32:40], ACT.Abs))
            act_e.wait_ge(al_landed, 16)
            step(A(ea[:, :], al[:, :], ACT.Exp))
            step(A(gt_["e2"][:, :, :], gt_["ab"][:, :, :], ACT.Exp, scale=-1.0))
            act_e.wait_ge(eps_set, 4)
            A(gt_["lp"][:, :, :], gt_["e2"][:, :, :], ACT.Ln, bias=eps[:, 3:4]).then_inc(gate_soft, 1)
            projected(0, 1)
            projected(0, 2)
            act_e.wait_ge(gate_cum, 1)
            nc.scalar.copy(gcs[:, 0:8 * NG], ps[3][:, 0:8 * NG])
            step(A(gcs[:, 8 * NG:16 * NG], ps[3][:, 8 * NG:16 * NG], ACT.Copy, scale=float(D)))
            A(ecs[:, :], gcs[:, :], ACT.Exp).then_inc(gate_exp, 1)
            projected(0, 3)
            act_e.wait_ge(g_e, 1)
            A(gt_["kd"][:, :, :], gt_["dif"][:, :, :], ACT.Exp).then_inc(gate_exp, 1)
            projected(0, 4)
            projected(0, 5)

            def exps(pair, n):
                act_e.wait_ge(s_max, 8 * pair + (n + 1))
                if n >= 2:
                    act_e.wait_ge(pt_done, 8 * pair + (n - 1))
                for h in range(2):
                    ins = A(p_sb[n % 2][:, h * KEYS:(h + 1) * KEYS], s_sb[n % 2][:, h * KEYS:(h + 1) * KEYS], ACT.Exp,
                            bias=nmax[n % 2][:, h:h + 1], accum_out=psum_row[n % 2][:, h:h + 1])
                ins.then_inc(p_exp, 1)

            def turned(pair, n):
                act_e.wait_ge(pt_done, 8 * pair + (n + 1))
                if n >= 2:
                    act_e.wait_ge(pv_done, 8 * pair + (n - 1))
                nc.scalar.copy(pt_sb[n % 2][:, :], ps[4 + n % 2][:, :]).then_inc(pt_evac, 1)

            def attend(pair, last_pair):
                exps(pair, 0)
                exps(pair, 1)
                for n in range(4):
                    turned_values(pair, n)
                done_at = {1: 0, 2: 1, 4: 2, 5: 3, 7: 4, 8: 5}
                for n in range(1, UNITS + 2):
                    if n >= 2:
                        turned(pair, n - 2)
                    if 2 <= n < UNITS:
                        exps(pair, n)
                    if not last_pair and n in done_at:
                        if n == 1:
                            act_e.wait_ge(k_copied, 2 * pair + 2)
                        if n == 7:
                            act_e.wait_ge(qk_done, 8 * pair + 8)
                        projected(pair + 1, done_at[n])

            def turned_values(pair, n):
                act_e.wait_ge(vt_done, 4 * pair + (n + 1))
                s, half = n // 2, n % 2
                nc.scalar.copy(v_tok[:, s, 2 * half:2 * half + 2, :, :].rearrange("p b k n -> p (b k n)"),
                               ps[6 + half][:, :]).then_inc(v_evac, 1)

            with act_e.Fori(0, PAIRS // 2 - 1) as i:
                for odd in range(2):
                    attend(2 * i + odd, False)
            attend(PAIRS - 2, False)
            attend(PAIRS - 1, True)

            act_e.wait_ge(o_evac, 2 * PAIRS + 1)

            def centre(h, x, s):
                act_e.wait_ge(proj_done, 8 * h + (2 * (GDN0 + x) + s + 1))
                A(qkv[:, x, s, :], ps[v_bank(s) if x == VX else s][:, :], ACT.Identity,
                  scale=cw[:, x, TAPS // 2:TAPS // 2 + 1]).then_inc(center, 1)

            def high_mix(k):
                nc.scalar.copy(m_hi[k][:, :], mix[:, k, :]).then_inc(mix_high, 1)

            def delta_head(h, last_head):
                def silu(x, s):
                    act_e.wait_ge(conv_done, 6 * h + (2 * x + s + 1))
                    A(qkv[:, x, s, :], qkv[:, x, s, :], ACT.Silu).then_inc(silu_done, 1)
                    if x < 2:
                        act_e.wait_ge(silu_done, 6 * h + (2 * x + s + 1))
                        A(q_d[:, 2 * x + s, :], qkv[:, x, s, :], ACT.Square).then_inc(sq_done, 1)

                def inverse_roots(x):
                    for s in range(SEQS):
                        act_e.wait_ge(nsum_done, 4 * h + (2 * x + s + 1))
                        A(x_1[:, 2 * x + s, :], ps[2 + 2 * x + s][:, :], ACT.Ln, scale=float(D if x == KX else D * P),
                          bias=eps[:, x:x + 1]).then_inc(norm_ln, 1)
                    act_e.wait_ge(norm_ln, 4 * h + (2 * x + 2))
                    for s in range(SEQS):
                        A(x_1[:, 2 * x + s, :], x_1[:, 2 * x + s, :], ACT.Exp, scale=-0.5).then_inc(rs_ready, 1)

                def turned_v(s):
                    act_e.wait_ge(vtr_done, 2 * h + (s + 1))
                    nc.scalar.copy(vg_tok[:, s, :], ps[7 - s][:, :]).then_inc(vg_tok_ready, 1)

                def gate(s):
                    act_e.wait_ge(proj_done, 8 * h + (2 * (GDN0 + 3) + s + 1))
                    A(z_s[:, s, :], ps[z_bank(s)][:, :], ACT.Silu).then_inc(z_silu, 1)

                silu(KX, 0)
                silu(KX, 1)
                centre(h, QX, 0)
                nc.scalar.preload_act_table_set(LN_EXP)
                act_e.wait_ge(head_out, 2 * h + 1)
                inverse_roots(KX)
                for g in range(GROUPS):
                    act_e.wait_ge(dt_ready, 4 * h + (g + 1))
                    A(dt_[:, g, :], dt_[:, g, :], ACT.Exp).then_inc(dt_exp, 1)
                    A(egr[:, g, :], ps[4 + g][:, :], ACT.Exp).then_inc(egr_ready, 1)
                centre(h, QX, 1)
                silu(QX, 0)
                for s in range(SEQS):
                    act_e.wait_ge(ktr_done, 2 * h + (s + 1))
                    nc.scalar.copy(k_tok[:, s, :], ps[6 + s][:, :]).then_inc(k_tok_ready, 1)
                centre(h, VX, 0)
                act_e.wait_ge(folded, h + 1)
                nc.scalar.copy(packed[:, 0:INST // 2, :].rearrange("p i c -> p (i c)"), ps[6][:, 0:INST // 2 * IB]
                               ).then_inc(fold_copied, 1)
                silu(QX, 1)
                silu(VX, 0)
                centre(h, VX, 1)
                nc.scalar.preload_act_table_set(LN_EXP)
                inverse_roots(QX)
                gate(0)
                silu(VX, 1)
                gate(1)
                turned_v(0)
                turned_v(1)
                if last_head:
                    act_e.wait_ge(qd_ready, 4 * h + 4)
                    high_mix(0)
                for lv in range(NL):
                    for s in range(SEQS):
                        act_e.wait_ge(x1_done, 2 * NL * h + (2 * lv + s + 1))
                        nc.scalar.copy(x_1[:, s, :], ps[2 + s][:, :]).then_inc(x1_evac, 1)
                for k in range(CH):
                    for g in range(GROUPS):
                        s, d = g // 2, g % 2
                        cc = k if d == 0 else CH - 1 - k
                        col = d * 8 + s * CH + cc
                        act_e.wait_ge(p2_done, 16 * h + (4 * k + g + 1))
                        A(x_1[:, g, 2 * P:3 * P], ps[2 + g][:, P:2 * P], ACT.Identity,
                          scale=hs[:, KAPPA * 16 + col:KAPPA * 16 + col + 1])
                        A(x_1[:, g, P:2 * P], ps[2 + g][:, P:2 * P], ACT.Identity,
                          scale=hs[:, BETA * 16 + col:BETA * 16 + col + 1]).then_inc(vn_ready, 1)
                for s in range(SEQS):
                    act_e.wait_ge(o_done, 12 * h + (10 + 2 * s))
                    if s == 0:
                        act_e.wait_ge(ud_ready, 4 * h + 4)
                    A(q_d[:, s, :], ps[6 + s][:, :], ACT.Square).then_inc(osq_done, 1)
                    nc.scalar.copy(o_sb[:, s, :], ps[6 + s][:, :]).then_inc(o_copied, 1)
                if not last_head:
                    act_e.wait_ge(hs_ready, h + 2)
                    for s in range(SEQS):
                        centre(h + 1, KX, s)
                else:
                    act_e.wait_ge(o_done, 12 * h + 12)
                    high_mix(1)
                nc.scalar.preload_act_table_set(LN_EXP)
                for s in range(SEQS):
                    act_e.wait_ge(osum_done, 2 * h + (s + 1))
                    A(x_1[:, s, :], ps[2 + s][:, :], ACT.Ln, scale=D / P, bias=eps[:, 0:1]).then_inc(out_ln, 1)
                act_e.wait_ge(out_ln, 2 * h + 2)
                for s in range(SEQS):
                    A(x_1[:, s, :], x_1[:, s, :], ACT.Exp, scale=-0.5).then_inc(ors_ready, 1)

            act_e.sem_inc(o_copied, 2)
            act_e.wait_ge(hs_ready, 1)
            for s in range(SEQS):
                centre(0, KX, s)
            with act_e.Fori(0, GH - 1) as h:
                delta_head(h, False)
            delta_head(GH - 1, True)

            for k in range(2, KT):
                if k == KT - 3:
                    act_e.wait_ge(head_out, 2 * GH + 1)
                high_mix(k)

            for s in range(SEQS):
                act_e.wait_ge(shift_summed, s + 1)
                A(c1[:, s, :], ps[2 + s][:, :], ACT.Copy, scale=float(KT)).then_inc(shift_copied, 1)
            for s in range(SEQS):
                act_e.wait_ge(d_ready1, s + 1)
                A(sumsq1[:, s, :], seq(mix[:, 0, :], s), ACT.Square).then_inc(squared, 1)

            def square(m, s, n):
                act_e.wait_ge(d_ready1, n + 1)
                if not (isinstance(n, int) and n == 2):
                    act_e.wait_ge(sq_added, n - 2)
                A(sq1[:, :], seq(mix[:, bass.ds(m, 1), :].rearrange("p a n -> p (a n)"), s) if not isinstance(m, int)
                  else seq(mix[:, m, :], s), ACT.Square).then_inc(squared, 1)

            square(1, 0, 2)
            square(1, 1, 3)
            with act_e.Fori(2, KT - 2) as m:
                for s in range(SEQS):
                    square(m, s, 2 * m + s)
            def inverse_root(row, s, var_s, step_s, rs_s):
                act_e.wait_ge(var_s, s + 1)
                A(row, row, ACT.Ln, bias=eps[:, 2:3]).then_inc(step_s, 1)
                act_e.wait_ge(step_s, s + 1)
                A(row, row, ACT.Exp, scale=-0.5).then_inc(rs_s, 1)

            square(KT - 2, 0, 2 * (KT - 2))
            square(KT - 1, 0, 2 * (KT - 2) + 1)
            square(KT - 2, 1, 2 * (KT - 2) + 2)
            inverse_root(sumsq1[:, 0, :], 0, var_ready, ln_step, rs_rows)
            for s in range(SEQS):
                if s:
                    inverse_root(sumsq1[:, 1, :], 1, var_ready, ln_step, rs_rows)
                for k in range(KT):
                    if s == 0 and k == 2:
                        square(KT - 1, 1, 2 * (KT - 2) + 3)
                    n = s * KT + k
                    zt = seq(mix[:, k, :], s)
                    act_e.wait_ge(scaled, n + 1)
                    A(zt, zt, ACT.Identity, scale=ln_sb[:, 0, k:k + 1], bias=ln_sb[:, 1, k:k + 1]).then_inc(x1_scaled, 1)
                    act_e.wait_ge(x1_scaled, n + 1)
                    nc.scalar.copy(seq(x_hi[:, k, :], s), zt).then_inc(x1_high, 1)
            act_e.wait_ge(x1_ready, SEQS * KT)

            def up(j, first):
                def centre(x, s):
                    b = 2 * x + s
                    if first:
                        act_e.wait_ge(proj_done, 2 * UP0 + 2 * s + x + 1)
                    else:
                        act_e.wait_ge(proj_done, 4 * j + (2 * (UP0 + x) + s + 1))
                        act_e.wait_ge(up_act, 2 * j + (s - 1))
                    A(cv[:, b, :], ps[b][:, :], ACT.Identity,
                      scale=fw_j[:, x, 1:2], bias=fw_j[:, x, 3:4]).then_inc(up_center, 1)
                nc.scalar.copy(fw_j[:, :, :], fw[:, bass.ds(2 * j, 2), :]).then_inc(fw_copied, 1)
                act_e.wait_ge(fw_copied, j + 1)
                centre(0, 0)
                centre(0, 1)
                for s in range(SEQS):
                    act_e.wait_ge(up_conv, 4 * j + (s + 1))
                    A(cv[:, s, :], cv[:, s, :], ACT.Silu).then_inc(up_silu, 1)
                centre(1, 0)
                centre(1, 1)
                act_e.wait_ge(up_center, 4 * j + 4)

            act_e.wait_ge(par_landed, 64)
            def high(j, jj, u):
                if isinstance(j, int) and j < 2:
                    act_e.wait_ge(up_act, 2 * j + 2)
                else:
                    act_e.wait_ge(proj_done, j + (2 * DOWN0 - 1))
                nc.scalar.copy(a_hi[u][:, :], act[:, bass.ds(jj, 1), :].rearrange("p a n -> p (a n)")).then_inc(a_high, 1)

            up(0, True)
            with act_e.Fori(1, FJ - 1) as j:
                up(j, False)
            for u in range(2):
                high(u, u, u)
            up(FJ - 1, False)
            act_e.wait_ge(up_act, 2 * FJ)
            with act_e.Fori(1, FJ // 2) as i:
                for u in range(2):
                    high(2 * i + u, 2 * i + u, u)
            for u in range(2):
                high(FJ + u, u, u)
            for s in range(SEQS):
                act_e.wait_ge(shift_summed2, s + 1)
                A(c2[:, s, :], ps[6 + s][:, :], ACT.Copy, scale=float(KT)).then_inc(shift_copied2, 1)
            with act_e.Fori(0, 4) as m:
                for u in range(2):
                    high(2 * m + (FJ + 2 + u), 2 * m + (2 + u), u)
                for s in range(SEQS):
                    act_e.wait_ge(d_ready2, 2 * m + (s + 1))
                    act_e.wait_ge(sq_added2, 2 * m + (s + 1))
                    A(sq2[:, :], z_all[:, bass.ds(m, 1), s * L:(s + 1) * L].rearrange("p a n -> p (a n)"),
                      ACT.Square).then_inc(squared2, 1)
            with act_e.Fori(5, FJ // 2) as i:
                for u in range(2):
                    high(2 * i + (FJ + u), 2 * i + u, u)
            for s in range(SEQS):
                for m in range(4):
                    act_e.wait_ge(d_ready2, 8 + 4 * s + m + 1)
                    A(sq_last[:, m, s, :], seq(z_all[:, 4 + m, :], s), ACT.Square).then_inc(sq_last_ready, 1)
            for s in range(SEQS):
                inverse_root(sumsq2[:, s, :], s, var_ready2, ln_step2, rs_rows2)
            pooled = 0
            for s in range(SEQS):
                for k in range(KT):
                    zt = seq(z_all[:, k, :], s)
                    if k in POOL_TILES:
                        pooled += 1
                        act_e.wait_ge(pool_scaled, pooled)
                    else:
                        act_e.wait_ge(scaled2, s * KT + k + 1 - pooled)
                    A(zt, zt, ACT.Identity, scale=ln_sb[:, 2, k:k + 1], bias=ln_sb[:, 3, k:k + 1]).then_inc(y_ready, 1)

        @block.vector
        def _(dve):
            TT, TS, STT = nc.vector.tensor_tensor, nc.vector.tensor_scalar, nc.vector.scalar_tensor_tensor
            nc.vector.memset(eps[:, 0:1], RMS_EPS).then_inc(eps_set, 1)
            nc.vector.memset(eps[:, 1:2], P * RMS_EPS).then_inc(eps_set, 1)
            nc.vector.memset(eps[:, 2:3], LN_EPS).then_inc(eps_set, 1)
            nc.vector.memset(eps[:, 3:4], 1.0).then_inc(eps_set, 1)
            for counter in (o_evac, head_out):
                dve.sem_inc(counter, 1)
            step = Chain(dve, dstep)
            step(nc.vector.memset(mean_w[:, :], 1.0 / D))
            for n in range(SEQS * KT):
                s, k = divmod(n, KT)
                dve.wait_ge(x_high, n + 1)
                TT(seq(x_lo[:, k, :], s), seq(mix[:, k, :], s), seq(x_hi[:, k, :], s).bitcast(F32),
                   ALU.subtract).then_inc(x_ready, 1)
            dve.wait_ge(gate_soft, 1)
            step(nc.vector.tensor_scalar_add(gt_["beta"][:, :, :], gt_["e1"][:, :, :], 1.0))
            step(nc.vector.reciprocal(gt_["beta"][:, :, :], gt_["beta"][:, :, :]))
            step(STT(gt_["sp"][:, :, :], ga[:, :, 32:40], 0.0, gt_["lp"][:, :, :], ALU.max, ALU.add))
            STT(gt_["g"][:, :, :], gt_["sp"][:, :, :], -1.0, ea[:, :].unsqueeze(1).to_broadcast([P, NG, 8]),
                ALU.mult, ALU.mult).then_inc(gate_g, 1)
            dve.wait_ge(bias_landed, 16 * (ROWS + 1))
            for hh in range(NA_HEADS):
                dve.wait_ge(bias_turned, hh + 1)
                for t, sh in enumerate(SHIFTS):
                    win = bass.AP(ps[0].tensor, (4 + hh % 4) * 512 + sh - SHIFTS[-1], [[8 * 512, P], [DC, ROWS], [1, SPAN]])
                    TT(bm[:, t, hh, :].rearrange("p (r c) -> p r c", c=SPAN), win,
                       nmask[:, t, :].rearrange("p (r c) -> p r c", c=SPAN), ALU.add).then_inc(bm_ready, 1)

            def next_keys(pair, first=False):
                for s in range(SEQS):
                    dve.wait_ge(nat_evac, 6 * pair + (s + 3))
                    if not first:
                        dve.wait_ge(qk_done, 8 * pair)
                    nc.vector.tensor_copy(k_nat[:, s, :], k_next[:, s, :]).then_inc(k_copied, 1)

            next_keys(0, first=True)
            dve.wait_ge(gate_exp, 1)
            tot = gcs[:, 8 * NG:16 * NG].rearrange("p (t d h) -> p t d h", d=2, h=4)
            etot = ecs[:, 8 * NG:16 * NG].rearrange("p (t d h) -> p t d h", d=2, h=4)
            for d in range(2):
                gc = gcs[:, d * 4 * NG:(d + 1) * 4 * NG].rearrange("p (t h) -> p t h", h=4)
                ins = TT(gt_["dif"][:, :, 4 * d:4 * d + 4], tot[:, :, d, :], gc, ALU.subtract)
            ins.then_inc(g_e, 1)
            dve.wait_ge(gate_exp, 2)
            for d in range(2):
                hd = slice(4 * d, 4 * d + 4)
                gc = gcs[:, d * 4 * NG:(d + 1) * 4 * NG].rearrange("p (t h) -> p t h", h=4)
                eg = ecs[:, d * 4 * NG:(d + 1) * 4 * NG].rearrange("p (t h) -> p t h", h=4)

                def out(q):
                    return sc[:, :, q * 16 + d * 8:q * 16 + d * 8 + 8].rearrange("p h t -> p t h")
                nc.vector.tensor_copy(out(BETA), gt_["beta"][:, :, hd]).then_inc(sc_ready, 1)
                nc.vector.tensor_scalar_mul(out(NEG_EG), eg, -1.0).then_inc(sc_ready, 1)
                TT(out(KAPPA), gt_["kd"][:, :, hd], gt_["beta"][:, :, hd], ALU.mult).then_inc(sc_ready, 1)
                nc.vector.tensor_copy(out(CDECAY), etot[:, :, d, :]).then_inc(sc_ready, 1)
                nc.vector.tensor_scalar_mul(out(NEG_GC), gc, -1.0).then_inc(sc_ready, 1)
                nc.vector.tensor_copy(out(GLOG), gt_["g"][:, :, hd]).then_inc(sc_ready, 1)
            dve.wait_ge(sc_ready, 12)

            def biased(pair, n):
                s, b = unit(n)
                dve.wait_ge(qk_done, 8 * pair + (n + 1))
                if n >= 2:
                    dve.wait_ge(p_exp, 8 * pair + (n - 1))
                TT(s_sb[n % 2][:, :].rearrange("p (h n) -> p h n", h=2), banks[:, 2:4, 0:KEYS],
                   bm[:, SHIFTS.index(SHIFT[b]), bass.ds(2 * pair, 2), :], ALU.add).then_inc(s_biased, 1)
                dve.wait_ge(s_biased, 8 * pair + (n + 1))
                nc.vector.tensor_reduce(nmax[n % 2][:, :], s_sb[n % 2][:, :].rearrange("p (h n) -> p h n", h=2),
                                        AX.X, ALU.max, negate=True).then_inc(s_max, 1)

            def normalised(pair, n):
                dve.wait_ge(p_exp, 8 * pair + (n + 1))
                step(nc.vector.reciprocal(rrow[n % 2][:, :], psum_row[n % 2][:, :]))
                for h in range(2):
                    pr = p_sb[n % 2][:, h * KEYS:(h + 1) * KEYS]
                    ins = nc.vector.tensor_scalar_mul(pr, pr, rrow[n % 2][:, h:h + 1])
                ins.then_inc(p_ready, 1)

            def attended(pair, s):
                dve.wait_ge(pv_done, 8 * pair + 4 * (s + 1))
                nc.vector.tensor_copy(
                    mix[:, bass.ds(pair, 1), s * L:(s + 1) * L].rearrange("p a (r b c) -> p (a r) b c", r=ROWS, b=BLOCKS),
                    ps[6 + s][:, :].rearrange("p (b r c) -> p r b c", b=BLOCKS, r=ROWS)).then_inc(o_evac, 1)

            def attend(pair, last_pair):
                biased(pair, 0)
                biased(pair, 1)
                normalised(pair, 0)
                for n in range(2, UNITS):
                    biased(pair, n)
                    normalised(pair, n - 1)
                    if n == 7:
                        attended(pair, 0)
                if not last_pair:
                    next_keys(pair + 1)
                normalised(pair, UNITS - 1)
                attended(pair, 1)

            base = step.n
            dve.wait_ge(bm_ready, 3 * NA_HEADS)
            with dve.Fori(0, PAIRS // 2 - 1) as i:
                step.enter(i, 2 * UNITS, base)
                for odd in range(2):
                    attend(2 * i + odd, False)
            step.leave(PAIRS // 2 - 1)
            attend(PAIRS - 2, False)
            attend(PAIRS - 1, True)

            def tile(ap, c):
                return ap[:, c * P:(c + 1) * P]

            dve.wait_ge(par_landed, 64)
            dve.wait_ge(o_evac, 2 * PAIRS + 1)

            def head_constants(h):
                step(nc.vector.tensor_copy(hs[:, :], sc[:, bass.ds(h, 1), :].rearrange("p a n -> p (a n)")))
                nc.vector.tensor_copy(cw[:, :, :], cw_all[:, bass.ds(3 * h, 3), :]).then_inc(hs_ready, 1)
                dve.wait_ge(hs_ready, h + 1)

            def convolve(h, x, s):
                dve.wait_ge(center, 6 * h + (2 * x + s + 1))
                dst, src = qkv[:, x, s, :], ps[v_bank(s) if x == VX else s]
                for n, tap in enumerate((0, 1, 3, 4)):
                    o = tap - TAPS // 2
                    a, b = max(0, -o), L - max(0, o)
                    ins = STT(dst[:, a:b], src[:, a + o:b + o], cw[:, x, tap:tap + 1], dst[:, a:b],
                              ALU.mult, ALU.add)
                    if n < 3:
                        step(ins)
                ins.then_inc(conv_done, 1)

            def bcast(ap):
                return ap.unsqueeze(1).to_broadcast([P, CH, P])

            def chunks(ap):
                return ap.rearrange("p (c n) -> p c n", c=CH)

            def low_mix(k):
                dve.wait_ge(mix_high, k + 1)
                TT(m_lo[k][:, :], mix[:, k, :], m_hi[k][:, :].bitcast(F32), ALU.subtract).then_inc(mix_ready, 1)

            def delta_head(h, last_head):
                def normed_x(x):
                    for s in range(SEQS):
                        dve.wait_ge(rs_ready, 4 * h + (2 * x + s + 1))
                        TT(qkv[:, x, s, :], qkv[:, x, s, :], x_1[:, 2 * x + s, :], ALU.mult).then_inc(normed, 1)

                def log_decays(g):
                    s, d = g // 2, g % 2
                    dve.wait_ge(gc_done, 4 * h + (g + 1))
                    for cc in range(CH):
                        col = NEG_GC * 16 + d * 8 + s * CH + cc
                        ins = STT(tile(dt_[:, g, :], cc), tile(ps[4 + g], cc), hs[:, col:col + 1], negm[d],
                                  ALU.add, ALU.add)
                    ins.then_inc(dt_ready, 1)

                def lower(g):
                    s, d = g // 2, g % 2
                    dve.wait_ge(dt_exp, 4 * h + (g + 1))
                    dve.wait_ge(kk_done, 2 * h + (s + 1))
                    for cc in range(CH):
                        col = BETA * 16 + d * 8 + s * CH + cc
                        ins = STT(tile(m_t[:, g, :], cc), tile(ps[2 + s], cc), hs[:, col:col + 1],
                                  tile(dt_[:, g, :], cc), ALU.mult, ALU.mult)
                    ins.then_inc(m_ready, 1)

                def scores(g):
                    dve.wait_ge(kq_done, 2 * h + (g // 2 + 1))
                    TT(att[:, g, :], ps[4 + g // 2][:, :], dt_[:, g, :], ALU.mult).then_inc(att_ready, 1)

                def decayed_q(g):
                    dve.wait_ge(egr_ready, 4 * h + (g + 1))
                    TT(q_d[:, g, :], qkv[:, QX, g // 2, :], egr[:, g, :], ALU.mult).then_inc(qd_ready, 1)

                def eliminate():
                    half = slice(P // 2, P)
                    step(nc.vector.tensor_copy(blk[half, :].rearrange("p (r c) -> p r c", c=IB),
                                               packed[half, INST:2 * INST, :].rearrange("p c r -> p r c")))
                    lo = blk[:, :].rearrange("p (i j) -> p i j", i=IB)
                    y = inv[:, 0, :].rearrange("p (r c) -> p r c", c=IB)
                    n = 0
                    for j in range(IB - 1):
                        rows, cols = IB - 1 - j, j + 1
                        prod = outer[:, 0:rows * cols].rearrange("p (r c) -> p r c", c=cols)
                        below = y[:, j + 1:IB, 0:cols]
                        TT(prod, lo[:, j + 1:IB, j:j + 1].to_broadcast([P, rows, cols]),
                           y[:, j:j + 1, 0:cols].to_broadcast([P, rows, cols]), ALU.mult).then_inc(eliminated, 1)
                        dve.wait_ge(eliminated, ELIM_STEPS * h + (n + 1))
                        TT(below, below, prod, ALU.subtract).then_inc(eliminated, 1)
                        n += 2
                        dve.wait_ge(eliminated, ELIM_STEPS * h + n)
                    step(nc.vector.tensor_copy(inv[:, 1, :].rearrange("p (r c) -> p r c", c=IB),
                                               y.rearrange("p r c -> p c r")))

                def expand(small, out, done):
                    TT(out.rearrange("p (i b c) -> p i b c", i=CH, c=IB),
                       small.unsqueeze(2).to_broadcast([P, CH, P // IB, IB]),
                       same_block.rearrange("p (b c) -> p b c", c=IB).unsqueeze(1).to_broadcast([P, CH, P // IB, IB]),
                       ALU.mult).then_inc(done, 1)

                def both_directions(m):
                    f, b = (packed[:, m * INST + d * (INST // 2):m * INST + (d + 1) * (INST // 2), :] for d in range(2))
                    step(TT(f, f, b, ALU.add))
                    step(TT(f, f, fold.unsqueeze(1).to_broadcast([P, INST // 2, IB]), ALU.subtract))
                    step(TT(b, f, small_select.unsqueeze(1).to_broadcast([P, INST // 2, IB]), ALU.mult))

                def between(lv, s):
                    TT(chunks(u_t[:, c_at(lv) + s, :]), chunks(m_t[:, 2 * s, :]), bcast(lmask[lv]), ALU.mult
                       ).then_inc(c_ready, 1)

                def selected(lv, s):
                    TT(chunks(x_1[:, 2 + s, :]), chunks(d_n[:, s, :]), bcast(select[lv]), ALU.mult
                       ).then_inc(r_selected, 1)

                def selected_t(lv, s):
                    TT(chunks(m_t[:, 2 * s + 1, :]), chunks(d_n[:, 2 + s, :]), bcast(select[lv]), ALU.mult
                       ).then_inc(s_selected, 1)

                log_decays(0)
                log_decays(1)
                normed_x(KX)
                log_decays(2)
                log_decays(3)
                convolve(h, QX, 0)
                for g in range(GROUPS):
                    lower(g)
                for s in range(SEQS):
                    dve.wait_ge(m_ready, 4 * h + (2 * s + 2))
                    TT(m_t[:, 2 * s, :], m_t[:, 2 * s, :], m_t[:, 2 * s + 1, :], ALU.add).then_inc(joined_l, 1)
                    dve.wait_ge(joined_l, 2 * h + (s + 1))
                    TT(chunks(u_t[:, s, :]), chunks(m_t[:, 2 * s, :]), bcast(same_block), ALU.mult).then_inc(masked, 1)
                convolve(h, QX, 1)
                convolve(h, VX, 0)
                step(nc.vector.memset(inv[:, 0, :], 0.0))
                step(nc.vector.memset(inv[:, 0, 0:IB * IB:IB + 1], 1.0))
                dve.wait_ge(blocks_landed, 32 * h + 32)
                eliminate()
                dve.sem_inc(inv_ready, 1)
                normed_x(QX)
                dve.wait_ge(normed, 4 * h + 4)
                for g in range(GROUPS):
                    decayed_q(g)
                convolve(h, VX, 1)
                for s in range(SEQS):
                    between(0, s)
                for g in range(GROUPS):
                    scores(g)
                dve.wait_ge(qd_ready, 4 * h + 4)
                for m, landed in enumerate((d_landed, u_landed)):
                    dve.wait_ge(landed, 32 * h + 32)
                    both_directions(m)
                for m, out, done in ((0, lambda s: x_1[:, 2 + s, :], r_selected),
                                     (1, lambda s: m_t[:, 2 * s + 1, :], s_selected)):
                    for s in range(SEQS):
                        n = m * INST + INST // 2 + s * CH
                        expand(packed[:, n:n + CH, :], out(s), done)
                for m in range(2):
                    for s in range(SEQS):
                        n = m * INST + s * CH
                        expand(packed[:, n:n + CH, :], d_n[:, 2 * m + s, :], expanded)
                dve.wait_ge(expanded, 4 * h + 4)
                for lv in range(NL):
                    if lv < NL - 1:
                        for s in range(SEQS):
                            if lv:
                                dve.wait_ge(x1_done, 2 * NL * h + (2 * (lv - 1) + s + 1))
                            between(lv + 1, s)
                    for s in range(SEQS):
                        dve.wait_ge(yy_done, 2 * NL * h + (2 * lv + s + 1))
                        w, v = d_n[:, s, :], d_n[:, 2 + s, :]
                        if lv < NL - 1:
                            TT(w, w, ps[4 + s][:, :], ALU.subtract).then_inc(w_updated, 1)
                        TT(v, v, ps[6 + s][:, :], ALU.subtract).then_inc(v_updated, 1)
                        if lv < NL - 1:
                            dve.wait_ge(w_updated, 2 * (NL - 1) * h + (2 * lv + s + 1))
                            selected(lv + 1, s)
                            dve.wait_ge(v_updated, 2 * NL * h + (2 * lv + s + 1))
                            selected_t(lv + 1, s)
                        else:
                            dve.wait_ge(v_updated, 2 * NL * h + (2 * lv + s + 1))
                            if s == 0:
                                dve.wait_ge(x1_done, 2 * NL * h + 2 * NL)
                            for d in range(2):
                                TT(chunks(u_t[:, 2 * s + d, :]), chunks(v), bcast(tri[d]), ALU.mult).then_inc(ud_ready, 1)
                if last_head:
                    low_mix(0)
                for k in range(CH):
                    if k:
                        for g in range(GROUPS):
                            s, d = g // 2, g % 2
                            cc = k if d == 0 else CH - 1 - k
                            col = NEG_EG * 16 + d * 8 + s * CH + cc
                            dve.wait_ge(p1_done, 12 * h + (4 * (k - 1) + g + 1))
                            STT(x_1[:, g, 0:P], ps[2 + g][:, 0:P], hs[:, col:col + 1], tile(vg_tok[:, s, :], cc),
                                ALU.mult, ALU.add).then_inc(r_ready, 1)
                    if k < CH - 1:
                        for g in range(GROUPS):
                            s, d = g // 2, g % 2
                            cc = k if d == 0 else CH - 1 - k
                            col = CDECAY * 16 + d * 8 + s * CH + cc
                            dve.wait_ge(su_done, 12 * h + (4 * k + g + 1))
                            if k == 0:
                                nc.vector.tensor_copy(d_n[:, g, 0:P], ps[2 + g][:, 2 * P:3 * P]).then_inc(s_ready, 1)
                            else:
                                dve.wait_ge(o_done, 12 * h + (4 * (k - 1) + g + 1))
                                STT(d_n[:, g, 0:P], d_n[:, g, 0:P], hs[:, col:col + 1], ps[2 + g][:, 2 * P:3 * P],
                                    ALU.mult, ALU.add).then_inc(s_ready, 1)
                if not last_head:
                    dve.wait_ge(vn_ready, 16 * h + 16)
                    head_constants(h + 1)
                    for s in range(SEQS):
                        convolve(h + 1, KX, s)
                else:
                    low_mix(1)
                for s in range(SEQS):
                    dve.wait_ge(ors_ready, 2 * h + (s + 1))
                    step(TT(o_sb[:, s, :], o_sb[:, s, :], x_1[:, s, :], ALU.mult))
                    dve.wait_ge(z_silu, 2 * h + (s + 1))
                    STT(mix[:, bass.ds(h + PAIRS, 1), s * L:(s + 1) * L].rearrange("p a n -> p (a n)"), o_sb[:, s, :],
                        nw[:, 0:1], z_s[:, s, :], ALU.mult, ALU.mult).then_inc(head_out, 1)
                dve.wait_ge(head_out, 2 * h + 3)

            head_constants(0)
            for s in range(SEQS):
                convolve(0, KX, s)
            base = step.base + step.n
            with dve.Fori(0, GH - 1) as h:
                step.enter(h, GDN_STEPS, base)
                delta_head(h, False)
            step.leave(GH - 1)
            delta_head(GH - 1, True)

            for k in range(2, KT):
                low_mix(k)
            dve.wait_ge(mix_ready, KT)

            def tile_of(t, m, s):
                return t[:, bass.ds(m, 1), s * L:(s + 1) * L].rearrange("p a n -> p (a n)")

            def unshifted(m, s):
                step(TT(tile_of(mix, m, s), tile_of(x_hi, m, s).bitcast(F32), tile_of(x_lo, m, s).bitcast(F32), ALU.add))

            def ahead(m, s):
                unshifted(m, s)
                step(STT(tile_of(mix, m, s), tile_of(mix, m, s), ALPHA, c1[:, s, :], ALU.mult, ALU.subtract))

            def residual(m, s, n, bank, done):
                dve.wait_ge(proj_done, done)
                dst = tile_of(mix, m, s)
                TT(dst, dst, ps[bank][:, :], ALU.add).then_inc(d_ready1, 1)
                dve.wait_ge(d_ready1, n + 1)
                step(TT(sum1[:, s, :], sum1[:, s, :], dst, ALU.add))

            def add_square(s, n):
                dve.wait_ge(squared, n + 1)
                TT(sumsq1[:, s, :], sumsq1[:, s, :], sq1[:, :], ALU.add).then_inc(sq_added, 1)
                dve.wait_ge(sq_added, n - 1)

            for s in range(SEQS):
                unshifted(0, s)
            for s in range(SEQS):
                dve.wait_ge(proj_done, 2 * OUT0 + s + 1)
                dst = seq(mix[:, 0, :], s)
                STT(dst, dst, ALPHA, ps[s][:, :], ALU.mult, ALU.add).then_inc(z_first, 1)
            dve.wait_ge(z_first, SEQS)
            for s in range(SEQS):
                dve.wait_ge(shift_copied, s + 1)
                dst = seq(mix[:, 0, :], s)
                TT(dst, dst, c1[:, s, :], ALU.subtract).then_inc(d_ready1, 1)
                dve.wait_ge(d_ready1, s + 1)
                step(nc.vector.tensor_copy(sum1[:, s, :], dst))
            for s in range(SEQS):
                ahead(1, s)
            base = step.base + step.n

            def output_chunk(m, bank):
                for s in range(SEQS):
                    residual(m, s, 2 * m + s, bank + s, 2 * m + (2 * OUT0 + s + 1))
                    ahead(m + 1, s)
                    add_square(s, 2 * m + s)
            output_chunk(1, 4)
            base = step.base + step.n
            with dve.Fori(1, KT // 2 - 1) as i:
                step.enter(i - 1, 12, base)
                for u in range(2):
                    output_chunk(2 * i + u, 4 * u)
            step.leave(KT // 2 - 2)
            for s in range(SEQS):
                ahead(KT - 1, s)

            def last_tiles(m, s):
                n = 2 * (KT - 2) + 2 * s + m - (KT - 2)
                residual(m, s, n, 6 - 2 * s + m - (KT - 2), 2 * OUT0 + n + 1)
                add_square(s, n)

            def variance(mean, square, sums, sumsq, var_s):
                step(nc.vector.tensor_copy(sums, mean))
                step(TT(sums, sums, mean, ALU.mult))
                TT(sumsq, square, sums, ALU.subtract).then_inc(var_s, 1)

            def scaled_mean(s, mean, sums, sumsq, rs_s):
                dve.wait_ge(rs_s, s + 1)
                step(TT(sums, mean, sumsq, ALU.mult))

            def scale_tile(zt, s, sums, sumsq, done):
                step(TT(zt, zt, sumsq, ALU.mult))
                TT(zt, zt, sums, ALU.subtract).then_inc(done, 1)

            last_tiles(KT - 2, 0)
            last_tiles(KT - 1, 0)
            last_tiles(KT - 2, 1)
            for s in range(SEQS):
                bank = 6 - 2 * s
                dve.wait_ge(stats_done, s + 1)
                variance(ps[bank][:, :], ps[bank + 1][:, :], sum1[:, s, :], sumsq1[:, s, :], var_ready)
                scaled_mean(s, ps[bank][:, :], sum1[:, s, :], sumsq1[:, s, :], rs_rows)
                for k in range(KT):
                    if s == 0 and k == 2:
                        last_tiles(KT - 1, 1)
                    scale_tile(seq(mix[:, k, :], s), s, sum1[:, s, :], sumsq1[:, s, :], scaled)
            dve.wait_ge(x1_ready, SEQS * KT)

            def up(j):
                def convolve(x, s):
                    b = 2 * x + s
                    dve.wait_ge(up_center, 4 * j + (b + 1))
                    for o, tap in ((-1, 0), (1, 2)):
                        a, e = max(0, -o), L - max(0, o)
                        ins = STT(cv[:, b, a:e], ps[b][:, a + o:e + o],
                                  fw[:, bass.ds(2 * j + x, 1), tap:tap + 1].rearrange("p a b -> p (a b)"),
                                  cv[:, b, a:e], ALU.mult, ALU.add)
                        if tap == 0:
                            step(ins)
                    ins.then_inc(up_conv, 1)

                def product(s):
                    dve.wait_ge(up_silu, 2 * j + (s + 1))
                    dve.wait_ge(up_conv, 4 * j + (3 + s))
                    TT(act[:, bass.ds(j, 1), s * L:(s + 1) * L].rearrange("p a n -> p (a n)"), cv[:, s, :], cv[:, 2 + s, :],
                       ALU.mult).then_inc(up_act, 1)

                convolve(0, 0)
                convolve(0, 1)
                convolve(1, 0)
                product(0)
                convolve(1, 1)
                product(1)

            base = step.base + step.n
            with dve.Fori(0, FJ - 1) as j:
                step.enter(j, 4, base)
                up(j)
            step.leave(FJ - 1)

            def low(j, jj, u):
                dve.wait_ge(a_high, j + 1)
                TT(a_lo[u][:, :], act[:, bass.ds(jj, 1), :].rearrange("p a n -> p (a n)") if not isinstance(jj, int)
                   else act[:, jj, :], a_hi[u][:, :].bitcast(F32), ALU.subtract).then_inc(a_ready, 1)

            for u in range(2):
                low(u, u, u)
            up(FJ - 1)
            dve.wait_ge(up_act, 2 * FJ)

            def joined(m, s):
                step(TT(tile_of(z_all, m, s), tile_of(x_hi, m, s).bitcast(F32), tile_of(x_lo, m, s).bitcast(F32), ALU.add))

            base = step.base + step.n
            with dve.Fori(1, 5) as i:
                step.enter(i - 1, SEQS, base)
                for u in range(2):
                    low(2 * i + u, 2 * i + u, u)
                for s in range(SEQS):
                    joined(i - 1, s)
            step.leave(4)
            with dve.Fori(5, FJ // 2) as i:
                for u in range(2):
                    low(2 * i + u, 2 * i + u, u)
            low(FJ, 0, 0)
            for m in range(4):
                if m == 2:
                    low(FJ + 1, 1, 1)
                for s in range(SEQS):
                    zt = seq(z_all[:, m, :], s)
                    if m == 0 and s == 0:
                        dve.wait_ge(proj_done, 2 * DOWN0 + FJ)
                    STT(zt, zt, ALPHA, ps[2 * m + s][:, :], ALU.mult, ALU.add).then_inc(acc_read, 1)
            step(nc.vector.memset(sum2[:, :, :], 0.0))
            nc.vector.memset(sumsq2[:, :, :], 0.0).then_inc(sq_added2, 1)
            dve.wait_ge(acc_read, 8)
            dve.wait_ge(shift_copied2, 2)

            def add2(m, s, n):
                dve.wait_ge(d_ready2, n + 1)
                return TT(sum2[:, s, :], sum2[:, s, :], tile_of(z_all, m, s), ALU.add)

            base = step.base + step.n
            with dve.Fori(0, 4) as m:
                step.enter(m, 3 * SEQS, base)
                for u in range(2):
                    low(2 * m + (FJ + 2 + u), 2 * m + (2 + u), u)
                for s in range(SEQS):
                    zt = tile_of(z_all, m, s)
                    TT(zt, zt, c2[:, s, :], ALU.subtract).then_inc(d_ready2, 1)
                    step(add2(m, s, 2 * m + s))
                    joined(m + 4, s)
                    zt = tile_of(z_all, m + 4, s)
                    step(STT(zt, zt, ALPHA, c2[:, s, :], ALU.mult, ALU.subtract))
                    dve.wait_ge(squared2, 2 * m + (s + 1))
                    TT(sumsq2[:, s, :], sumsq2[:, s, :], sq2[:, :], ALU.add).then_inc(sq_added2, 1)
            step.leave(4)
            with dve.Fori(5, FJ // 2) as i:
                for u in range(2):
                    low(2 * i + (FJ + u), 2 * i + u, u)
            for s in range(SEQS):
                for m in range(4):
                    zt = seq(z_all[:, 4 + m, :], s)
                    dve.wait_ge(proj_done, 2 * DOWN0 + 2 * FJ - 2 + 4 * s + m + 1)
                    TT(zt, zt, ps[2 * m + s][:, :], ALU.add).then_inc(d_ready2, 1)
                    n = 8 + 4 * s + m
                    add2(4 + m, s, n).then_inc(summed2, 1)
                    dve.wait_ge(summed2, 4 * s + m + 1)
            for s in range(SEQS):
                dve.wait_ge(stats_done2, s + 1)
                variance(ps[s][:, :], ps[2 + s][:, :], sum2[:, s, :], sumsq2[:, s, :], var_ready2)
                if s == 0:
                    scaled_mean(0, ps[0][:, :], sum2[:, 0, :], sumsq2[:, 0, :], rs_rows2)
                    dve.sem_inc(rows2_ready, 1)
            for s in range(SEQS):
                if s:
                    scaled_mean(1, ps[1][:, :], sum2[:, 1, :], sumsq2[:, 1, :], rs_rows2)
                    dve.sem_inc(rows2_ready, 1)
                for k in range(KT):
                    if k not in POOL_TILES:
                        scale_tile(seq(z_all[:, k, :], s), s, sum2[:, s, :], sumsq2[:, s, :], scaled2)


def build(nc, arrays):
    args = {name: nc.dram_tensor(name, a.shape, F32, kind="ExternalInput").ap() for name, a in arrays.items()}
    yT = nc.dram_tensor("yT", (KT, P, T), F32, kind="ExternalOutput").ap()
    block_dram = nc.dram_tensor("block_dram", (P // 2, IB * IB), F32, kind="Internal").ap()
    inverse_dram = nc.dram_tensor("inverse_dram", (2, P, IB * IB), F32, kind="Internal").ap()
    encoder_layer(nc, yT=yT, block_dram=block_dram, inverse_dram=inverse_dram, **args)


def shape_constants():
    i = np.arange(P)
    parts = [np.eye(P), i[:, None] <= i[None, :], i[:, None] >= i[None, :]]
    parts += [np.where(i[:, None] <= i[None, :], 0.0, NEG), np.where(i[:, None] >= i[None, :], 0.0, NEG)]
    for v in LEVELS:
        half = i >> v
        parts.append((half[:, None] ^ half[None, :]) == 1)
    for v in LEVELS:
        half = i >> v
        parts.append((half[:, None] == half[None, :])
                     & np.where(half[:, None] % 2 == 0, i[:, None] >= i[None, :], i[:, None] <= i[None, :]))
    parts.append(np.eye(P)[::-1])
    parts.append(i[:, None] // IB == i[None, :] // IB)
    parts.append(i[:, None] % IB == np.arange(IB)[None, :])
    row, col = i[:, None] % IB, np.arange(IB)[None, :]
    parts.append(np.where(i[:, None] // IB % 2 == 0, row >= col, row <= col))
    consts = np.concatenate([p.astype(np.float32) for p in parts], axis=1)
    mask = np.zeros((P, len(SHIFTS), KEYS), np.float32)
    for t, sh in enumerate(SHIFTS):
        b = SHIFT.index(sh)
        qc = b * QB + np.arange(QB)
        start = np.clip(qc - WIN_C // 2, 0, GRID_W - WIN_C)
        kc = KC0[b] + np.arange(SPAN)
        seen = (kc[None, :] >= start[:, None]) & (kc[None, :] < start[:, None] + WIN_C)
        mask[:, t, :] = np.tile(np.where(seen, 0.0, NEG), (ROWS, ROWS))
    return consts, mask


def kernel(**inputs):
    import concourse.bacc as bacc
    from concourse.bass_utils import run_bass_kernel_spmd

    a = {n: np.asarray(v) for n, v in inputs.items()}
    x = np.concatenate([a["x_prompt"][0], a["x_sample"][0]], axis=0)
    w_in = a["w_in"][0]
    cuts = np.cumsum([0, 512, 512, 512, 512, 512, 512, 512, 16])

    def chunk(w):
        return w.reshape(KT, P, -1).transpose(1, 0, 2).reshape(P, -1)

    def part(i, n):
        return chunk(w_in[:, cuts[i] + n * P:cuts[i] + (n + 1) * P])

    w_gate = np.zeros((D, GATE_COLS), np.float32)
    w_gate[:, 0:8] = w_in[:, cuts[7]:cuts[7] + 8]
    w_gate[:, 32:40] = w_in[:, cuts[7] + 8:cuts[7] + 16]
    gate_vec = np.zeros((P, 1), np.float32)
    gate_vec[32:40, 0] = a["gdn_dt_bias"][0].reshape(8)
    w_nat = np.stack([part(i, n) for n in range(PAIRS) for i in (1, 2, 0)])
    w_gdn = np.stack([part(i, h) for h in range(GH) for i in (4, 3, 5, 6)])
    w_out = np.stack([chunk(a["w_out"][0][:, m * P:(m + 1) * P]) for m in range(KT)])
    up = a["ffn_w_up"][0]
    w_up = np.stack([chunk(up[:, x0 + j * P:x0 + (j + 1) * P]) for j in range(FJ) for x0 in (0, FF)])
    w_down = a["ffn_w_down"][0].reshape(DPASS, 2, P, 2, 512).transpose(3, 0, 2, 1, 4).reshape(2 * DPASS, P, D)
    w_all = np.concatenate([w_nat, w_gdn, w_out, w_up, w_down], axis=0)
    rpb = np.zeros(NA_HEADS * DR * DC + 2 * PAD, np.float32)
    rpb[PAD:-PAD] = a["na_rpb"][0].reshape(-1)
    gconv = a["gdn_conv_w"][0].reshape(TAPS, 3, GH, P)[:, [1, 0, 2]].transpose(3, 2, 1, 0).reshape(P, 3 * GH, TAPS)
    fconv = np.concatenate([a["ffn_conv_w"][0], a["ffn_conv_b"]], axis=0)
    fconv = fconv.reshape(4, 2, FJ, P).transpose(3, 2, 1, 0).reshape(P, 2 * FJ, 4)
    ln = np.stack([a[n][0].reshape(KT, P) for n in ("ln1_g", "ln1_b", "ln2_g", "ln2_b")]).transpose(2, 0, 1)
    consts, nat_mask = shape_constants()
    arrays = {
        "xT": x.T.reshape(KT, P, T), "w_gate": chunk(w_gate), "w_all": w_all, "rpb": rpb, "gdn_conv": gconv, "gate_vec": gate_vec,
        "a_log": a["gdn_a_log"][0].reshape(1, 8), "norm_w": a["gdn_norm_w"].reshape(P, 1), "ln_par": ln,
        "ffn_conv": fconv, "consts": consts, "nat_mask": nat_mask,
    }
    arrays = {n: np.ascontiguousarray(v) for n, v in arrays.items()}
    nc = bacc.Bacc("TRN2", target_bir_lowering=False, num_devices=1)
    build(nc, arrays)
    r = run_bass_kernel_spmd(nc, [arrays], core_ids=[0])
    y = r.results[0]["yT"].reshape(D, SEQS, L)
    return (np.ascontiguousarray(y[:, 0].T)[None], np.ascontiguousarray(y[:, 1].T)[None])
```
